# Optimizing a Trainium2 kernel written in Bass

```python
import math
import jax, jax.numpy as jnp
from jax import lax
import numpy as np

D_MODEL = 2048
BATCH = 1
SEQ = 256
DEPTH = 1

CHUNK = 64
Q_BLOCK = 128
EPS = 1e-6
SB_HEADS = 8
SB_HEAD_DIM = 128
SB_WIDTH = SB_HEADS * SB_HEAD_DIM
MLA_HEADS = 8
MLA_NOPE_DIM = 128
MLA_ROPE_DIM = 64
MLA_QK_DIM = MLA_NOPE_DIM + MLA_ROPE_DIM
MLA_V_DIM = 128
MLA_WIDTH = MLA_HEADS * MLA_V_DIM
Q_LORA_RANK = 512
KV_LORA_RANK = 256
ROPE_THETA = 10000.0
D_MIX = SB_WIDTH + MLA_WIDTH
IN_SPLITS = (SB_WIDTH, SB_WIDTH, SB_WIDTH, SB_WIDTH,
             Q_LORA_RANK, KV_LORA_RANK, MLA_ROPE_DIM, MLA_WIDTH)
D_IN = sum(IN_SPLITS)


def rms_norm(x, w):
    xf = x.astype(jnp.float32)
    y = xf * lax.rsqrt(jnp.mean(xf * xf, axis=-1, keepdims=True) + EPS)
    return (y * w.astype(jnp.float32)).astype(x.dtype)

def rope_tables(positions):
    inv_freq = ROPE_THETA ** (-jnp.arange(0, MLA_ROPE_DIM, 2, dtype=jnp.float32) / MLA_ROPE_DIM)
    ang = positions.astype(jnp.float32)[..., None] * inv_freq
    return jnp.cos(ang), jnp.sin(ang)

def apply_rope(x, cos, sin):
    x1, x2 = jnp.split(x.astype(jnp.float32), 2, axis=-1)
    out = jnp.concatenate([x1 * cos - x2 * sin, x2 * cos + x1 * sin], axis=-1)
    return out.astype(x.dtype)

def to_heads(t, n_heads):
    b, s, _ = t.shape
    return t.reshape(b, s, n_heads, -1).transpose(0, 2, 1, 3)

def from_heads(t):
    b, h, s, d = t.shape
    return t.transpose(0, 2, 1, 3).reshape(b, s, h * d)

def stick_breaking_attention(q, k, v):
    seq, d = q.shape[2], q.shape[3]
    scale = 1.0 / math.sqrt(d)
    outs = []
    for b0 in range(0, seq, Q_BLOCK):
        kl = b0 + Q_BLOCK
        z = jnp.einsum('bhqd,bhkd->bhqk', q[:, :, b0:kl], k[:, :, :kl]).astype(jnp.float32) * scale
        t_idx = b0 + jnp.arange(Q_BLOCK)[:, None]
        s_idx = jnp.arange(kl)[None, :]
        before = s_idx < t_idx
        log_keep = jnp.where(before, jax.nn.log_sigmoid(-z), 0.0)
        later = lax.cumsum(log_keep, axis=3, reverse=True) - log_keep
        a = jnp.where(before, jnp.exp(jax.nn.log_sigmoid(z) + later), 0.0)
        outs.append(jnp.einsum('bhqk,bhkd->bhqd', a.astype(v.dtype), v[:, :, :kl]))
    return jnp.concatenate(outs, axis=2)

def chunk_causal_softmax_attention(q, k, v):
    seq, d = q.shape[2], q.shape[3]
    scale = 1.0 / math.sqrt(d)
    outs = []
    for b0 in range(0, seq, Q_BLOCK):
        kl = b0 + Q_BLOCK
        s_ = jnp.einsum('bhqd,bhkd->bhqk', q[:, :, b0:kl], k[:, :, :kl]).astype(jnp.float32) * scale
        t_chunk = (b0 + jnp.arange(Q_BLOCK))[:, None] // CHUNK
        s_chunk = jnp.arange(kl)[None, :] // CHUNK
        s_ = jnp.where(s_chunk <= t_chunk, s_, -jnp.inf)
        p = jax.nn.softmax(s_, axis=-1)
        outs.append(jnp.einsum('bhqk,bhkd->bhqd', p.astype(v.dtype), v[:, :, :kl]))
    return jnp.concatenate(outs, axis=2)

def hybrid_layer(x, cos, sin, pre_norm_w, w_in, q_norm_w, w_q_up, kv_norm_w, w_kv_up, w_out, post_norm_w):
    b, s, _ = x.shape
    h = rms_norm(x, pre_norm_w)
    proj = h @ w_in
    split_pts = tuple(int(i) for i in np.cumsum(IN_SPLITS)[:-1])
    sb_q, sb_k, sb_v, sb_gate, c_q, c_kv, k_rope, mla_gate = jnp.split(proj, split_pts, axis=-1)

    o_a = from_heads(stick_breaking_attention(to_heads(sb_q, SB_HEADS),
                                              to_heads(sb_k, SB_HEADS),
                                              to_heads(sb_v, SB_HEADS)))

    q_full = (rms_norm(c_q, q_norm_w) @ w_q_up).reshape(b, s, MLA_HEADS, MLA_QK_DIM)
    q_nope, q_rot = jnp.split(q_full, [MLA_NOPE_DIM], axis=-1)
    q_rot = apply_rope(q_rot, cos[:, :, None, :], sin[:, :, None, :])
    kv = (rms_norm(c_kv, kv_norm_w) @ w_kv_up).reshape(b, s, MLA_HEADS, MLA_NOPE_DIM + MLA_V_DIM)
    k_nope, v_mla = jnp.split(kv, [MLA_NOPE_DIM], axis=-1)
    k_rot = apply_rope(k_rope, cos, sin)
    k_rot = jnp.broadcast_to(k_rot[:, :, None, :], (b, s, MLA_HEADS, MLA_ROPE_DIM))
    q_mla = jnp.concatenate([q_nope, q_rot], axis=-1).transpose(0, 2, 1, 3)
    k_mla = jnp.concatenate([k_nope, k_rot], axis=-1).transpose(0, 2, 1, 3)
    o_b = from_heads(chunk_causal_softmax_attention(q_mla, k_mla, v_mla.transpose(0, 2, 1, 3)))

    mixed = jnp.concatenate([o_a * jax.nn.silu(sb_gate), o_b * jax.nn.silu(mla_gate)], axis=-1)
    y = mixed @ w_out
    return x + rms_norm(y, post_norm_w)

def first_inputs(seed: int = 0) -> dict:
    key = jax.random.key(seed)
    ks = jax.random.split(key, 12)
    f32 = jnp.float32
    x = jax.random.normal(ks[0], (BATCH, SEQ, D_MODEL), f32)
    positions = jnp.broadcast_to(jnp.arange(SEQ, dtype=jnp.int32)[None, :], (BATCH, SEQ))
    pre_norm_w = 1.0 + 0.05 * jax.random.normal(ks[1], (DEPTH, D_MODEL), f32)
    w_in = jax.random.normal(ks[2], (DEPTH, D_MODEL, D_IN), f32) * D_MODEL ** -0.5
    q_norm_w = 1.0 + 0.05 * jax.random.normal(ks[3], (DEPTH, Q_LORA_RANK), f32)
    w_q_up = jax.random.normal(ks[4], (DEPTH, Q_LORA_RANK, MLA_HEADS * MLA_QK_DIM), f32) * Q_LORA_RANK ** -0.5
    kv_norm_w = 1.0 + 0.05 * jax.random.normal(ks[5], (DEPTH, KV_LORA_RANK), f32)
    w_kv_up = jax.random.normal(ks[6], (DEPTH, KV_LORA_RANK, MLA_HEADS * (MLA_NOPE_DIM + MLA_V_DIM)), f32) * KV_LORA_RANK ** -0.5
    w_out = jax.random.normal(ks[7], (DEPTH, D_MIX, D_MODEL), f32) * D_MIX ** -0.5
    post_norm_w = 1.0 + 0.05 * jax.random.normal(ks[8], (DEPTH, D_MODEL), f32)
    return {'x': x, 'positions': positions, 'pre_norm_w': pre_norm_w, 'w_in': w_in,
            'q_norm_w': q_norm_w, 'w_q_up': w_q_up, 'kv_norm_w': kv_norm_w, 'w_kv_up': w_kv_up,
            'w_out': w_out, 'post_norm_w': post_norm_w}

def first_block(x, positions, pre_norm_w, w_in, q_norm_w, w_q_up, kv_norm_w, w_kv_up, w_out, post_norm_w):
    cos, sin = rope_tables(positions)
    for i in range(DEPTH):
        x = hybrid_layer(x, cos, sin, pre_norm_w[i], w_in[i], q_norm_w[i], w_q_up[i],
                         kv_norm_w[i], w_kv_up[i], w_out[i], post_norm_w[i])
    return x


N_META = 16
HEAD_DIM = 128
D_ATTN = D_MODEL // 2
ATTN_HEADS = D_ATTN // HEAD_DIM
POOL_WINDOWS = (2, 4, 8, 16)
N_POOL_GROUPS = len(POOL_WINDOWS)
D_POOL = D_MODEL // 2
POOL_GROUP_DIM = D_POOL // N_POOL_GROUPS
D_FF = 11 * D_MODEL // 4
CONV_WIDTH = 3

SPLIT_SIZES = (D_ATTN, D_ATTN, D_ATTN, ATTN_HEADS, D_POOL, D_MODEL, D_MODEL)
SPLIT_IDX = tuple(int(i) for i in np.cumsum(SPLIT_SIZES)[:-1])
D_IN_2 = sum(SPLIT_SIZES)
F_OFF = 3 * D_ATTN


def rmsnorm(x, g):
    xf = x.astype(jnp.float32)
    y = xf * lax.rsqrt(jnp.mean(xf * xf, axis=-1, keepdims=True) + EPS)
    return (y * g.astype(jnp.float32)).astype(x.dtype)

def forgetting_attention(q, k, v, logf):
    B, L, H, Dh = q.shape
    n_blocks = -(-L // Q_BLOCK)
    Lp = n_blocks * Q_BLOCK
    pad = ((0, 0), (0, Lp - L), (0, 0), (0, 0))
    q = jnp.pad(q, pad)
    k = jnp.pad(k, pad)
    v = jnp.pad(v, pad)
    logf = jnp.pad(logf, ((0, 0), (0, Lp - L), (0, 0)))
    c = jnp.cumsum(logf, axis=1)
    c = jnp.transpose(c, (0, 2, 1))
    scale = HEAD_DIM ** -0.5
    pos = jnp.arange(Lp)
    outs = []
    for i in range(n_blocks):
        q0, q1 = i * Q_BLOCK, (i + 1) * Q_BLOCK
        qb = q[:, q0:q1]
        kb = k[:, :q1]
        vb = v[:, :q1]
        s = jnp.einsum('bqhd,bkhd->bhqk', qb, kb).astype(jnp.float32) * scale
        bias = c[:, :, q0:q1, None] - c[:, :, None, :q1]
        mask = pos[q0:q1, None] >= pos[None, :q1]
        s = jnp.where(mask[None, None], s + bias, -jnp.inf)
        p = jax.nn.softmax(s, axis=-1).astype(vb.dtype)
        outs.append(jnp.einsum('bhqk,bkhd->bqhd', p, vb))
    o = jnp.concatenate(outs, axis=1)[:, :L]
    return o.reshape(B, L, H * Dh)

def multiscale_pool(u, pool_w, pool_scale):
    B, L, _ = u.shape
    uf = u.astype(jnp.float32).reshape(B, L, N_POOL_GROUPS, POOL_GROUP_DIM)
    csum = jnp.cumsum(uf, axis=1)
    pos = jnp.arange(L)
    outs = []
    for g, w in enumerate(POOL_WINDOWS):
        cg = csum[:, :, g]
        prev = jnp.pad(cg[:, :L - w], ((0, 0), (w, 0), (0, 0)))
        cnt = jnp.minimum(pos + 1, w).astype(jnp.float32)[None, :, None]
        outs.append((cg - prev) / cnt - uf[:, :, g])
    d = jnp.stack(outs, axis=2).astype(u.dtype)
    y = jnp.einsum('blgc,gcd->blgd', d, pool_w).reshape(B, L, D_POOL)
    return y * pool_scale

def mixer_block(h, w_in, b_in, w_attn_o, pool_w, pool_scale, w_pool_o, w_out):
    B, L, _ = h.shape
    z = h @ w_in + b_in
    q, k, v, f_logit, u, g_attn, g_pool = jnp.split(z, SPLIT_IDX, axis=-1)
    q = q.reshape(B, L, ATTN_HEADS, HEAD_DIM)
    k = k.reshape(B, L, ATTN_HEADS, HEAD_DIM)
    v = v.reshape(B, L, ATTN_HEADS, HEAD_DIM)
    logf = jax.nn.log_sigmoid(f_logit.astype(jnp.float32))
    attn = forgetting_attention(q, k, v, logf)
    pool = multiscale_pool(u, pool_w, pool_scale)
    m = jax.nn.sigmoid(g_attn) * (attn @ w_attn_o) + jax.nn.sigmoid(g_pool) * (pool @ w_pool_o)
    return m @ w_out

def causal_dwconv(a, conv_w, conv_b):
    L = a.shape[1]
    ap = jnp.pad(a, ((0, 0), (CONV_WIDTH - 1, 0), (0, 0)))
    out = conv_b
    for j in range(CONV_WIDTH):
        out = out + ap[:, j:j + L] * conv_w[j]
    return out

def conv_ffn(h, w_up, conv_w, conv_b, w_down):
    a = causal_dwconv(h @ w_up, conv_w, conv_b)
    gate, val = jnp.split(a, 2, axis=-1)
    return (jax.nn.gelu(gate, approximate=True) * val) @ w_down

def second_inputs(seed: int = 0) -> dict:
    key = jax.random.key(seed)
    ks = jax.random.split(key, 18)
    f32 = jnp.float32
    nrm = lambda k, shape, s: jax.random.normal(k, shape, f32) * s
    gain = lambda k, n: jnp.ones((DEPTH, n), f32) + nrm(k, (DEPTH, n), 0.02)
    b_in = nrm(ks[4], (DEPTH, D_IN_2), 0.02)
    f_bias = jax.random.uniform(ks[5], (DEPTH, ATTN_HEADS), f32, 1.0, 5.0)
    b_in = b_in.at[:, F_OFF:F_OFF + ATTN_HEADS].add(f_bias)
    return {
        'x': nrm(ks[0], (BATCH, SEQ, D_MODEL), 1.0),
        'meta_tokens': nrm(ks[1], (N_META, D_MODEL), 1.0),
        'mix_pre_g': gain(ks[2], D_MODEL),
        'w_in': nrm(ks[3], (DEPTH, D_MODEL, D_IN_2), D_MODEL ** -0.5),
        'b_in': b_in,
        'w_attn_o': nrm(ks[6], (DEPTH, D_ATTN, D_MODEL), D_ATTN ** -0.5),
        'pool_w': nrm(ks[7], (DEPTH, N_POOL_GROUPS, POOL_GROUP_DIM, POOL_GROUP_DIM), POOL_GROUP_DIM ** -0.5),
        'pool_scale': jnp.ones((DEPTH, D_POOL), f32) + nrm(ks[8], (DEPTH, D_POOL), 0.1),
        'w_pool_o': nrm(ks[9], (DEPTH, D_POOL, D_MODEL), D_POOL ** -0.5),
        'w_out': nrm(ks[10], (DEPTH, D_MODEL, D_MODEL), D_MODEL ** -0.5),
        'mix_post_g': gain(ks[11], D_MODEL),
        'ffn_pre_g': gain(ks[12], D_MODEL),
        'w_ffn_up': nrm(ks[13], (DEPTH, D_MODEL, 2 * D_FF), D_MODEL ** -0.5),
        'ffn_conv_w': nrm(ks[14], (DEPTH, CONV_WIDTH, 2 * D_FF), CONV_WIDTH ** -0.5),
        'ffn_conv_b': nrm(ks[15], (DEPTH, 2 * D_FF), 0.02),
        'w_ffn_down': nrm(ks[16], (DEPTH, D_FF, D_MODEL), D_FF ** -0.5),
        'ffn_post_g': gain(ks[17], D_MODEL),
    }

def second_block(x, meta_tokens, mix_pre_g, w_in, b_in, w_attn_o, pool_w, pool_scale, w_pool_o,
              w_out, mix_post_g, ffn_pre_g, w_ffn_up, ffn_conv_w, ffn_conv_b, w_ffn_down,
              ffn_post_g):
    B = x.shape[0]
    meta = jnp.broadcast_to(meta_tokens.astype(x.dtype)[None], (B, N_META, D_MODEL))
    r = jnp.concatenate([meta, x], axis=1)
    for l in range(DEPTH):
        h = rmsnorm(r, mix_pre_g[l])
        mix = mixer_block(h, w_in[l], b_in[l], w_attn_o[l], pool_w[l], pool_scale[l],
                          w_pool_o[l], w_out[l])
        r = r + rmsnorm(mix, mix_post_g[l])
        h = rmsnorm(r, ffn_pre_g[l])
        ff = conv_ffn(h, w_ffn_up[l], ffn_conv_w[l], ffn_conv_b[l], w_ffn_down[l])
        r = r + rmsnorm(ff, ffn_post_g[l])
    return r[:, N_META:]


def setup_inputs(seed=0):
    out = dict(first_inputs(seed))
    for name, value in second_inputs(seed + 1).items():
        if name != "x":
            out[name + "_2"] = value
    return out


def reference(
    x, positions, pre_norm_w, w_in, q_norm_w, w_q_up, kv_norm_w, w_kv_up, w_out, post_norm_w,
    meta_tokens_2, mix_pre_g_2, w_in_2, b_in_2, w_attn_o_2, pool_w_2, pool_scale_2, w_pool_o_2,
    w_out_2, mix_post_g_2, ffn_pre_g_2, w_ffn_up_2, ffn_conv_w_2, ffn_conv_b_2, w_ffn_down_2,
    ffn_post_g_2,
):
    x = first_block(
        x, positions, pre_norm_w, w_in, q_norm_w, w_q_up, kv_norm_w, w_kv_up, w_out,
        post_norm_w,
    )
    return second_block(
        x, meta_tokens_2, mix_pre_g_2, w_in_2, b_in_2, w_attn_o_2, pool_w_2, pool_scale_2,
        w_pool_o_2, w_out_2, mix_post_g_2, ffn_pre_g_2, w_ffn_up_2, ffn_conv_w_2, ffn_conv_b_2,
        w_ffn_down_2, ffn_post_g_2,
    )


_drawn_inputs = setup_inputs


def setup_inputs(seed=0):
    import zlib

    import numpy as np

    out = dict(_drawn_inputs(seed))
    spreads = {}
    factors = {'q_norm_w': 6.258,
     'kv_norm_w': 3.954,
     'mix_pre_g_2': 3.861,
     'mix_post_g_2': 4.403,
     'ffn_pre_g_2': 3.787,
     'ffn_conv_b_2': 4.082,
     'ffn_post_g_2': 5.618}
    for name, (base, spread) in spreads.items():
        noise = np.random.default_rng([zlib.crc32(name.encode()), seed]).standard_normal(out[name].shape)
        drawn = base * np.exp(spread * noise) if base else spread * noise
        out[name] = __import__('jax').numpy.asarray(drawn.astype(out[name].dtype))
    for name, factor in factors.items():
        out[name] = (out[name] * factor).astype(out[name].dtype)
    return out
```

```python
from contextlib import ExitStack

import numpy as np
import concourse.bass as bass
from concourse import mybir

F32 = mybir.dt.float32
F32R = mybir.dt.float32r
I32 = mybir.dt.int32
ALU = mybir.AluOpType
ACT = mybir.ActivationFunctionType
AX = mybir.AxisListType

P = 128
D = 2048
SEQ = 256
META = 16
L2 = SEQ + META
HALO = 2
T0 = META - HALO
NQ = L2 - T0
KD = D // P
EPS = 1e-6
HEADS = 8
QL = 512 // P
KVL = 256 // P
ROPE = 64
MLA_QK = 192
D_FF = 5632
KF = D_FF // P
QB = NQ // 3
KL = [T0 + QB * (i + 1) for i in range(3)]
POOL_W = (2, 4, 8, 16)
BIG = 2.0 ** 100
GROUP = 1024
RAW = 8
SPL = 4

C_ID, C_ONE, C_NTRI, C_NONE, C_ROT = 0, 128, 256, 384, 512
C_CAUSAL = 640
C_FREQ = C_CAUSAL + QB
C_EYE8 = C_FREQ + 1
C_ROWSEL = C_EYE8 + 8
C_COLMASK = C_ROWSEL + 128
NCONST = C_COLMASK + 64

V_PRE, V_QN, V_KVN, V_POST, V_MPRE, V_MPOST, V_FPRE, V_PSC = 0, 16, 20, 22, 38, 54, 70, 86
NV1 = 94
V_BQKV, V_BU, V_BGA, V_BGP = 94, 118, 126, 142
NV2 = 64
NV = NV1 + NV2


VEC1 = (("pre_norm_w", 16), ("q_norm_w", 4), ("kv_norm_w", 2), ("post_norm_w", 16), ("mix_pre_g_2", 16),
        ("mix_post_g_2", 16), ("ffn_pre_g_2", 16), ("pool_scale_2", 8))
NSMALL = 1 + len(VEC1) + 4 + 4 + 1
MLA_BLOCKS = ((0, 0, P), (0, P, 2 * P), (1, 0, P), (1, P, 2 * P))
FG_BLOCKS = ((4, 0, 0), (4, KL[0], KL[0]), (5, 0, KL[0] + KL[1]))
INV_2PI = float(1 / (2 * np.pi))
MAGIC = 1.5 * 2 ** 23
PI_HI, PI_LO = 6.28125, float(2 * np.pi - 6.28125)


def constants():
    c = np.zeros((P, NCONST), np.float32)
    i = np.arange(P)
    c[:, C_ID:C_ID + P] = np.eye(P)
    c[:, C_ONE:C_ONE + P] = 1
    c[:, C_NTRI:C_NTRI + P] = -(i[:, None] >= i[None, :]).astype(np.float32)
    c[:, C_NONE:C_NONE + P] = -1
    for b in range(2):
        for j in range(32):
            c[64 * b + 32 + j, C_ROT + 64 * b + j] = -1
            c[64 * b + j, C_ROT + 64 * b + 32 + j] = 1
    q = np.arange(QB)
    c[:QB, C_CAUSAL:C_CAUSAL + QB] = np.where(q[None, :] > q[:, None], -BIG, 0)
    freq = (np.float32(10000.0) ** (-np.arange(0, ROPE, 2, dtype=np.float32) / np.float32(ROPE))).astype(np.float32)
    c[:, C_FREQ] = freq[i % 32]
    c[:8, C_EYE8:C_EYE8 + 8] = np.eye(8)
    c[32:40, C_EYE8:C_EYE8 + 8] = np.eye(8)
    c[0, C_ROWSEL:C_ROWSEL + 64] = 1
    c[0, C_COLMASK:C_COLMASK + 64] = -BIG
    return c


class Phase:

    def __init__(self, name, iters, sizes):
        self.name, self.iters, self.sizes, self.n = name, iters, sizes, len(sizes)


PHASES = [
    Phase("B1", 1, [(1024, 1)] * 8),
    Phase("B2", 1, [(768, 1)] * 8),
    Phase("A", HEADS, [(1024, 2)] * 8),
    Phase("C", HEADS // 2, [(1024, 1)] * 4 + [(768, 4)] * 2 + [(512, 1)] * 2),
    Phase("D", 4, [(1024, 1)] * 8),
    Phase("F0", 1, [(1024, 3)] * 8),
    Phase("E", 1, [(1024, 1)] * 2),
    Phase("F", HEADS - 1, [(1024, 3)] * 8),
    Phase("Ga", 1, [(1024, 1)] * 8),
    Phase("K", 1, [(512, 1)] * 4),
    Phase("Gb", 1, [(1024, 1)] * 4),
    Phase("G1", 1, [(1024, 1)] * 12),
    Phase("G", 3, [(1024, 1)] * 24),
    Phase("H", 4, [(1024, 1)] * 8),
    Phase("I0", 2, [(1024, 2)] * 8),
    Phase("I", 10, [(1024, 2)] * 16),
    Phase("J", 11, [(1024, 1)] * 8),
]


ROW_MAJOR = [(kk, half) for kk in range(4) for half in range(2)]
HALF_MAJOR = [(kk, half) for half in range(2) for kk in range(4)]


def plan():
    first, filled = 0, [0] * RAW
    for ph in PHASES:
        ph.first = first
        assert ph.iters == 1 or ph.n % RAW == 0
        per, ph.full = [0] * RAW, []
        for j, (_, dmas) in enumerate(ph.sizes):
            s = (first + j) % RAW
            per[s] += 16 * dmas
            ph.full.append([filled[s] + per[s], s])
        for f in ph.full:
            f.append(per[f[1]])
        filled = [a + b * ph.iters for a, b in zip(filled, per)]
        first += ph.iters * ph.n
    return {ph.name: ph for ph in PHASES}


class Steps:

    def __init__(self, eng, sem):
        self.eng, self.sem, self.base, self.n, self.it, self.stride = eng, sem, 0, 0, None, 0

    def mark(self, ins):
        self.n += 1
        ins.then_inc(self.sem, 1)

    def sync(self):
        if self.it is None:
            if self.base + self.n > 0:
                self.eng.wait_ge(self.sem, self.base + self.n)
        else:
            self.eng.wait_ge(self.sem, self.it * self.stride + (self.base + self.n))

    def loop(self, it, stride):
        self.base, self.n, self.it, self.stride = self.base + self.n, 0, it, stride

    def done(self, iters):
        assert self.n == self.stride, f"stride is {self.n}, not {self.stride}"
        self.base, self.n, self.it = self.base + iters * self.stride, 0, None


def build(nc, a, out):
    ph = plan()
    off = [(nc.sbuf_base + 63) // 64 * 64]
    end = nc.sbuf_usable_end

    def region(nbytes):
        o = off[0]
        off[0] += (nbytes + 31) // 32 * 32
        assert off[0] <= end, (off[0], end)
        return o

    def at(o, name, shape, dt=F32):
        return nc.alloc_sbuf_tensor_at(name, shape, dt, offset=o)

    raw = at(region(RAW * GROUP * 4), "raw", [P, RAW, GROUP])
    w_hi = at(region(SPL * GROUP * 4), "w_hi", [P, SPL, GROUP], F32R)
    w_lo = at(region(SPL * GROUP * 4), "w_lo", [P, SPL, GROUP], F32R)
    X_REG = region(KD * L2 * 4)
    xT = at(X_REG, "xT", [P, KD, L2])
    H_REG = region(2 * KD * L2 * 4)
    h_hi = at(H_REG, "h_hi", [P, KD, L2], F32R)
    h_lo = at(H_REG + KD * L2 * 4, "h_lo", [P, KD, L2], F32R)
    Y_REG = region(KD * L2 * 4)
    yT = at(Y_REG, "yT", [P, KD, L2])
    MB = KD * NQ * 4
    M_REG = region(2 * MB)
    mix_hi = at(M_REG, "mix_hi", [P, KD, NQ], F32R)
    mix_lo = at(M_REG + MB, "mix_lo", [P, KD, NQ], F32R)
    AB = HEADS * NQ * 4
    AP_REG = region(4 * AB)
    att_hi = at(AP_REG, "att_hi", [P, HEADS, NQ], F32R)
    att_lo = at(AP_REG + AB, "att_lo", [P, HEADS, NQ], F32R)
    POOL_REG = AP_REG + 2 * AB
    pool_hi = at(POOL_REG, "pool_hi", [P, HEADS, NQ], F32R)
    pool_lo = at(POOL_REG + AB, "pool_lo", [P, HEADS, NQ], F32R)
    cst = at(region(NCONST * 4), "cst", [P, NCONST])
    vec = at(region(NV * 4), "vec", [P, NV])
    cvw = at(region(4 * 88 * 4), "cvw", [P, 4, 88])
    rstd = at(region(L2 * 4), "rstd", [P, L2])
    root = at(region(L2 * 4), "root", [P, L2])
    stat = at(region(24 * 4), "stat", [P, 24])
    nmx, den, rden = stat[:, 0:4], stat[:, 4:8], stat[:, 8:12]
    b_f = at(region(32), "b_f", [8, 1])
    bqs = at(region(32), "bqs", [P, HEADS])

    x_in = at(M_REG, "x_in", [P, 2, D])
    meta_in = at(M_REG + 2 * D * 4, "meta_in", [META, D])
    vrow = at(M_REG + 3 * D * 4, "vrow", [P, 6, P])
    pos_i = at(M_REG + 3 * D * 4 + 6 * P * 4, "pos_i", [P, SEQ], I32)
    pos_f = at(M_REG + 3 * D * 4 + 6 * P * 4 + SEQ * 4, "pos_f", [P, SEQ])

    junk = at(X_REG, "junk", [P, 4, 1024])
    r_q = at(region(SEQ * 4), "r_q", [P, SEQ])
    r_kv = at(region(SEQ * 4), "r_kv", [P, SEQ])
    r_tok = at(Y_REG, "r_tok", [P, 2, D])
    gpost = at(H_REG, "gpost", [P, D])
    o_tok = at(H_REG + D * 4, "o_tok", [P, 2, D])

    def area(o, limit, *parts):
        r, o0 = [], o
        for name, shape, dt in parts:
            r.append(at(o, name, shape, dt))
            o += (int(np.prod(shape[1:])) * 4 + 31) // 32 * 32
        assert o - o0 <= limit, (parts[0][0], o - o0, limit)
        return r

    cosT, sinT, krot, qkvg, egate, sgate, mo, lnz, spz, aw, vtok, _ = area(
        POOL_REG, 2 * AB, ("cosT", [P, SEQ], F32), ("sinT", [P, SEQ], F32), ("krot", [P, SEQ], F32),
        ("qkvg", [P, 4, SEQ], F32), ("egate", [P, SEQ], F32), ("sgate", [P, SEQ], F32), ("mo", [P, SEQ], F32),
        ("lnz", [P, 384], F32), ("spz", [P, 384], F32), ("aw", [P, 384], F32), ("vtok", [P, 2, P], F32),
        ("pad", [P, 128], F32))
    SPZ = POOL_REG + 10 * SEQ * 4
    cp = at(SPZ, "cp", [P, 2, 384])
    cpt = at(SPZ + 3072, "cpt", [P, 2, 384])
    ysq, yacc = area(H_REG, 2 * KD * L2 * 4, ("ysq", [P, 4, NQ], F32), ("yacc", [P, 4, NQ], F32))
    lat, kr, tb = area(Y_REG, KD * L2 * 4, ("lat", [P, 6, SEQ], F32), ("kr", [P, SEQ], F32), ("tb", [P, 4, SEQ], F32))
    latsq, = area(M_REG, 2 * MB, ("latsq", [P, 6, SEQ], F32))
    cg, cqn, ckv, cqr, ct1, cqrr, csg, cmo, cvt = area(
        Y_REG, KD * L2 * 4, ("cg", [P, 2, SEQ], F32), ("cqn", [P, 2, SEQ], F32), ("ckv", [P, 2, 2, SEQ], F32),
        ("cqr", [P, SEQ], F32), ("ct1", [P, SEQ], F32), ("cqrr", [P, SEQ], F32), ("csg", [P, 2, SEQ], F32),
        ("cmo", [P, 2, SEQ], F32), ("cvt", [P, 4, P], F32))
    uT, augR, augL, fz, fq, fk, fv, ones8, tf = area(
        M_REG, 2 * MB, ("uT", [P, HEADS, 16 + L2], F32), ("augR", [40, HEADS, L2], F32), ("augL", [40, NQ], F32),
        ("fz", [8, 3, L2], F32), ("fq", [P, NQ], F32), ("fk", [P, L2], F32), ("fv", [P, L2], F32),
        ("ones8", [40, L2], F32), ("tf", [P, 4, L2], F32))
    d_hi, d_lo = area(M_REG + HEADS * (16 + L2) * 4, 8704 + 1056 + 3264 + 1056 + 3 * 1088,
                      ("d_hi", [P, HEADS, NQ], F32R), ("d_lo", [P, HEADS, NQ], F32R))
    fpt, fvt, fp = area(POOL_REG, 2 * AB, ("fpt", [P, 6, QB], F32), ("fvt", [P, 3, P], F32), ("fp", [QB, sum(KL)], F32))
    gsa, gsp, gta, gtp = area(Y_REG, KD * L2 * 4, *[(n, [P, 2, NQ], F32) for n in ("gsa", "gsp", "gta", "gtp")])
    wsum, = area(Y_REG, 4 * 2 * NQ * 4, ("wsum", [P, 2, 2, L2], F32))
    pdiff, = area(Y_REG + 4 * 2 * NQ * 4, KD * L2 * 4 - 4 * 2 * NQ * 4, ("pdiff", [P, 4, 2, NQ], F32))
    actT, ab, cv, ge, a_hi, a_lo = area(
        M_REG, 2 * MB + 4 * AB, ("actT", [P, KF, SEQ], F32), ("ab", [P, 4, NQ], F32), ("cv", [P, 4, SEQ], F32),
        ("ge", [P, 2, SEQ], F32), ("a_hi", [P, 4, SEQ], F32R), ("a_lo", [P, 4, SEQ], F32R))

    pt = nc.alloc_psum_tensor("pt", [P, 8, 512], F32)
    ident, ones = cst[:, C_ID:C_ID + P], cst[:, C_ONE:C_ONE + P]
    ntri, nones, rot = cst[:, C_NTRI:C_NTRI + P], cst[:, C_NONE:C_NONE + P], cst[:, C_ROT:C_ROT + P]
    L1T, QT, KT2 = slice(META, L2), slice(T0, L2), slice(0, L2)

    def number(p, it, j):
        return p.first + it * p.n + j

    with ExitStack() as ctx:
        def sem(name):
            return ctx.enter_context(nc.semaphore(name))

        def sems(prefix, names):
            return [sem(prefix + n) for n in names.split()]

        raw_in = [sem(f"raw_in{i}") for i in range(RAW)]
        hi_done, lo_done, used = sems("w_", "hi_done lo_done used")
        act_st, dve_st, pool_st = sems("steps_", "act dve pool")
        sp_turn = sem("sp_turn")
        small_in, x_land, meta_land, pos_land, gpost_land, out_land = sems("in_", "small x meta pos gpost out")
        vec_t, vec_ev, x_t, x_ev_d, x_ev_a = sems("start_", "vec_t vec_ev x_t x_ev_d x_ev_a")
        x_new, h_hi_s, h_rdy, sq_rdy, sq_acc, sq_sum, root_s = sems("norm_", "x_new h_hi h_rdy sq acc sum root")
        lat_ev, lat_sq, lat_hi_s, lat_rdy, lat_sum, lat_root, tab_r, tab_f, kr_c, kr_done = sems(
            "lat_", "ev sq hi rdy sum root tab_r tab_f kr_c kr_done")
        A_ev, A_eg, A_rec, A_sg, A_z, A_ln, A_sp, A_spm, A_ex, A_e, A_w, A_vt, A_pv, A_mo, A_mh = sems(
            "sb_", "ev eg rec sg z ln sp spm ex e w vt pv mo mh")
        mix_rdy = sem("mix_rdy")
        C_ev, C_eg, C_rec, C_sg, C_rot, C_t1, C_rope, C_s, C_vt, C_mx, C_p, C_pn, C_pt, C_pe, C_pv, C_mo, C_mh = sems(
            "mla_", "ev eg rec sg rot t1 rope s vt mx p pn pt pe pv mo mh")
        y_ev, y_acc, y_cp, y_t = sems("y_", "ev acc cp t")
        F_ev, F_b, F_s, F_vt, F_mx, F_p, F_pn, F_pt, F_pa, F_pd, F_pv, F_ah, F_ar = sems(
            "fg_", "ev b s vt mx p pn pt pa pd pv ah ar")
        E_x, E_e, E_sp, E_aug, E_pad = sems("forget_", "x e sp aug pad")
        p_t, p_h, p_d, p_kh, p_r = sems("pool_", "t h d kh r")
        g_ev, g_sg, g_t, g_m, g_mh, g_mr = sems("mixer_", "ev sg t m mh mr")
        i_ev, i_cb, i_cv, i_ge, i_act, i_rt, i_re, i_rd = sems("up_", "ev cb cv ge act rt re rd")
        j_hi, j_a, j_y, j_sq, j_b, j_rt, j_r, j_t, j_od, j_op = sems("down_", "hi a y sq b root r t od op")

        block = ctx.enter_context(nc.Block())

        @block.sync
        def _(sp):
            w_in1 = a["w_in"][0].rearrange("(k p) n -> p k n", p=P)
            w_in2 = a["w_in_2"][0].rearrange("(k p) n -> p k n", p=P)
            w_up = a["w_ffn_up_2"][0].rearrange("(k p) (f n) -> p k f n", p=P, f=2)

            def load(p, it, j, *pieces):
                g = number(p, it, j)
                if p.first + j >= RAW:
                    sp.wait_ge(lo_done, g - RAW + 1)
                    sp.sem_inc(sp_turn, 1)
                s = (p.first + j) % RAW
                assert len(pieces) == p.sizes[j][1]
                for dst, src in pieces:
                    sp.dma_start(dst(raw[:, s, :]), src).then_inc(raw_in[s], 16)

            def kn(k, n=None):
                return lambda r: (r if n is None else r[:, 0:k * n]).rearrange("p (k n) -> p k n", k=k)

            def row(kk, f, parts=None):
                return lambda r: r.rearrange("p (k f n) -> p k f n", k=2, f=f)[:, kk, 0:parts or f, :]

            sp.dma_start(x_in[:], a["x"][0].rearrange("(t p) n -> p t n", p=P)).then_inc(x_land, 16)
            for j in range(8):
                load(ph["B1"], 0, j, (kn(2), w_in1[:, 2 * j:2 * j + 2, 4096:4608]))
            for j in range(8):
                load(ph["B2"], 0, j, (kn(2, 384), w_in1[:, 2 * j:2 * j + 2, 4608:4992]))
            heads1 = w_in1[:, :, 0:4096].rearrange("p k (f n) -> p k f n", f=4)
            with sp.Fori(0, HEADS) as h:
                for j in range(8):
                    load(ph["A"], h, j, *[(row(kk, 4), heads1[:, 2 * j + kk, :, bass.ds(h * P, P)]) for kk in range(2)])
            wq = a["w_q_up"][0].rearrange("(k p) n -> p k n", p=P)
            wkv = a["w_kv_up"][0].rearrange("(k p) n -> p k n", p=P)
            with sp.Fori(0, HEADS // 2) as c:
                for j in range(4):
                    load(ph["C"], c, j, (kn(4), w_in1[:, 4 * j:4 * j + 4, bass.ds(c * 256 + 4928, 256)]))
                for j in range(2):
                    load(ph["C"], c, 4 + j, *[
                        (lambda r, kk=kk, o=o, n=n: r[:, kk * 384 + o:kk * 384 + o + 2 * n].rearrange("p (h n) -> p h n", h=2),
                         wq[:, 2 * j + kk, bass.ds(c * 384, 384)].rearrange("p (h n) -> p h n", h=2)[:, :, (0, P)[o > 0]:(P, MLA_QK)[o > 0]])
                        for kk in range(2) for o, n in ((0, P), (2 * P, ROPE))])
                for j in range(2):
                    load(ph["C"], c, 6 + j, (kn(1, 512), wkv[:, j:j + 1, bass.ds(c * 512, 512)]))
            wo1 = a["w_out"][0].rearrange("(k p) n -> p k n", p=P)
            with sp.Fori(0, 4) as c:
                for j in range(8):
                    load(ph["D"], c, j, (kn(2), wo1[:, 2 * j:2 * j + 2, bass.ds(c * 512, 512)]))
            heads2 = w_in2[:, :, 0:3072].rearrange("p k (f n) -> p k f n", f=3)

            def qkvu(p, it, h):
                for j in range(8):
                    load(p, it, j,
                         *[(row(kk, 4, 3), heads2[:, 2 * j + kk, :, bass.ds(h * P, P)]) for kk in range(2)],
                         (lambda r: r.rearrange("p (k f n) -> p k f n", k=2, f=4)[:, :, 3, :],
                          w_in2[:, 2 * j:2 * j + 2, bass.ds(h * P + 3080, P)]))

            qkvu(ph["F0"], 0, 0)
            for j in range(2):
                load(ph["E"], 0, j, (kn(8), w_in2[:, 8 * j:8 * j + 8, 3072:3200]))
            with sp.Fori(0, HEADS - 1) as it:
                qkvu(ph["F"], it, it + 1)
            wao = a["w_attn_o_2"][0].rearrange("(k p) n -> p k n", p=P)
            wpo = a["w_pool_o_2"][0].rearrange("(k p) n -> p k n", p=P)

            def gates(p, it, j0, c):
                for j in range(8):
                    load(p, it, j0 + j, (kn(4), w_in2[:, 4 * (j % 4):4 * (j % 4) + 4,
                                                      bass.ds(c * 256 + (4104 if j < 4 else 6152), 256)]))

            def ups(p, it, j0, c):
                for j in range(4):
                    src = wao if j < 2 else wpo
                    load(p, it, j0 + j, (kn(4), src[:, 4 * (j % 2):4 * (j % 2) + 4, bass.ds(c * 256, 256)]))

            gates(ph["Ga"], 0, 0, 0)
            for g in range(4):
                load(ph["K"], 0, g, (kn(2, 256), a["pool_w_2"][0, g].rearrange("(k p) n -> p k n", p=P)))
            ups(ph["Gb"], 0, 0, 0)
            gates(ph["G1"], 0, 0, 1)
            ups(ph["G1"], 0, 8, 1)
            with sp.Fori(0, 3) as b:
                for e in range(2):
                    gates(ph["G"], b, 12 * e, b * 2 + (2 + e))
                    ups(ph["G"], b, 12 * e + 8, b * 2 + (2 + e))
            wo2 = a["w_out_2"][0].rearrange("(k p) n -> p k n", p=P)
            with sp.Fori(0, 4) as c:
                for j in range(8):
                    load(ph["H"], c, j, (kn(2), wo2[:, 2 * j:2 * j + 2, bass.ds(c * 512, 512)]))

            def ffn_up(p, it, j0, i):
                for j in range(8):
                    load(p, it, j0 + j, *[(row(kk, 2), w_up[:, 2 * j + kk, :, bass.ds(i * 256, 256)]) for kk in range(2)])

            with sp.Fori(0, 2) as it:
                ffn_up(ph["I0"], it, 0, it)
            with sp.Fori(0, 10) as b:
                for e in range(2):
                    ffn_up(ph["I"], b, 8 * e, b * 2 + (2 + e))
            wd = a["w_ffn_down_2"][0]

            def down(it, order):
                for j, (kk, half) in enumerate(order):
                    load(ph["J"], it, j, (lambda r: r, wd[bass.ds(it * 512 + kk * P, P), half * 1024:half * 1024 + 1024]))

            with sp.Fori(0, 10) as it:
                down(it, ROW_MAJOR)
            down(10, HALF_MAJOR)
            sp.wait_ge(used, ph["J"].first)
            sp.dma_start(gpost[:], a["ffn_post_g_2"][0].partition_broadcast(P)).then_inc(gpost_land, 16)
            outv = out[0].rearrange("(t p) n -> p t n", p=P)
            for t in range(2):
                for half, rdy in ((1, j_od), (0, j_op)):
                    sp.wait_ge(rdy, t + 1)
                    cs = slice(half * 1024, half * 1024 + 1024)
                    sp.dma_start(outv[:, t, cs], o_tok[:, t, cs]).then_inc(out_land, 16)
            sp.wait_ge(out_land, 64)

        @block.tensor
        def _(pe):
            def ma(out_, l, r, start, stop=False):
                return nc.tensor.matmul(out_, l, r, start=start, stop=stop, skip_group_check=True)

            tr = nc.tensor.transpose

            def group(p, it, j, k0, nk, tiles, acts, k_all, bank_free=None):
                pe.wait_ge(lo_done, number(p, it, j) + 1)
                s = (p.first + j) % SPL
                width = p.sizes[j][0] // nk

                def products(kk, tile):
                    dst, cols, tok, opens = tile
                    k = k0 + kk
                    wh, wl = (cols(w[:, s, kk * width:kk * width + width]) for w in (w_hi, w_lo))
                    ma(dst, wh, acts[0][:, k, tok], opens and k == 0)
                    ma(dst, wh, acts[1][:, k, tok], False)
                    return ma(dst, wl, acts[0][:, k, tok], False, k == k_all - 1)

                if bank_free:
                    for n, tile in enumerate(tiles):
                        bank_free(n)
                        for kk in range(nk):
                            last = products(kk, tile)
                else:
                    for kk in range(nk):
                        for tile in tiles:
                            last = products(kk, tile)
                last.then_inc(used, 1)

            def cut(c):
                return lambda w: w[:, c:c + P]

            def ramp(p, norm, tiles, tok, width):
                for j in range(8):
                    pe.wait_ge(h_rdy, KD * norm + 2 * j + 2)
                    group(p, 0, j, 2 * j, 2, tiles, H, KD)
                pe.wait_ge(sq_acc, norm + 1)
                ma(pt[:, 7, 0:width], ones, yT[:, 0, tok], True, True).then_inc(sq_sum, 1)

            H, MIX, ATT, POOL = (h_hi, h_lo), (mix_hi, mix_lo), (att_hi, att_lo), (pool_hi, pool_lo)
            full = slice(0, SEQ)

            pe.wait_ge(small_in, 16 * NSMALL)
            tr(pt[:, 6, 0:NV1], vrow[0:NV1, 0, :], cst[0:NV1, C_ID:C_ID + NV1])
            tr(pt[:, 6, NV1:NV], vrow[0:NV2, 1, :], cst[0:NV2, C_ID:C_ID + NV2])
            for i in range(4):
                last = tr(pt[:, 7, 88 * i:88 * i + 88], vrow[0:88, 2 + i, :], cst[0:88, C_ID:C_ID + 88])
            last.then_inc(vec_t, 1)
            pe.wait_ge(x_land, 16)
            for b in range(8):
                if b == 6:
                    pe.wait_ge(x_ev_d, 1)
                if b == 7:
                    pe.wait_ge(x_ev_a, 1)
                for i in range(4):
                    k, t = 2 * b + i // 2, i % 2
                    last = tr(pt[:, b % 6, i * P:i * P + P], x_in[:, t, k * P:k * P + P], ident)
                last.then_inc(x_t, 1)
            pe.wait_ge(meta_land, 16)
            pe.wait_ge(x_ev_d, 2)
            for k in range(KD):
                last = tr(pt[:, 2, k * META:k * META + META], meta_in[:, k * P:k * P + P], cst[0:META, C_ID:C_ID + META])
            last.then_inc(x_t, 1)

            pe.wait_ge(x_ev_d, 5)
            pe.wait_ge(x_ev_a, 4)
            pe.wait_ge(vec_ev, 2)
            ramp(ph["B1"], 0, [(pt[:, n, 0:SEQ], cut(n * P), L1T, True) for n in range(4)], L1T, SEQ)
            for j in range(8):
                group(ph["B2"], 0, j, 2 * j, 2, [(pt[:, 4 + n, 0:SEQ], cut(n * P), L1T, True) for n in range(3)], H, KD)

            def sb_values(h):
                pe.wait_ge(A_w, h + 1)
                pe.wait_ge(A_vt, h + 1)
                ma(pt[:, 6, 0:256], vtok[:, 0, :], aw[:, 0:256], True)
                ma(pt[:, 6, 128:256], vtok[:, 1, :], aw[:, 256:384], False, True).then_inc(A_pv, 1)

            def sb_scores(h):
                pe.wait_ge(A_ev, h * 2 + 2)
                for t in range(2):
                    tr(pt[:, 5, t * P:t * P + P], qkvg[:, 2, t * P:t * P + P], ident)
                ma(pt[:, 4, 0:256], qkvg[:, 1, 0:P], qkvg[:, 0, 0:256], True)
                ma(pt[:, 4, 256:384], qkvg[:, 1, P:2 * P], qkvg[:, 0, P:2 * P], False, True).then_inc(A_z, 1)

            def sb_later(h):
                pe.wait_ge(A_spm, h + 1)
                ma(pt[:, 4, 0:256], ntri, spz[:, 0:256], False)
                ma(pt[:, 4, 128:256], nones, spz[:, 256:384], False)
                ma(pt[:, 4, 256:384], ntri, spz[:, 256:384], False, True).then_inc(A_ex, 1)

            def sb_unit(h, post, values):
                def bank_free(n):
                    if post and n == 0:
                        pe.wait_ge(A_ev, h * 2 - 1)
                    elif post and n == 1:
                        pe.wait_ge(A_ev, h * 2)
                    elif n == 0:
                        pe.wait_ge(lat_ev, 1)

                if values:
                    sb_values(h - 2)
                for j in range(8):
                    group(ph["A"], h, j, 2 * j, 2, [(pt[:, n, 0:SEQ], cut(n * P), L1T, True) for n in range(4)], H, KD,
                          bank_free if j == 0 else None)
                    if post and j == 1:
                        sb_scores(h - 1)
                    if post and j == 4:
                        sb_later(h - 1)
                    if not post and j == 3:
                        pe.wait_ge(lat_sq, 2)
                        pe.wait_ge(lat_ev, 3)
                        pe.wait_ge(root_s, 1)
                        for i in range(QL):
                            ma(pt[:, 7, 0:256], ones, latsq[:, i, :], i == 0)
                        for i in range(KVL):
                            ma(pt[:, 7, 256:512], ones, latsq[:, QL + i, :], False, i == KVL - 1)
                        ma(pt[:, 6, 256:512], rot, kr[:], True, True).then_inc(lat_sum, 1)

            sb_unit(0, False, False)
            pe.wait_ge(kr_done, 1)
            sb_unit(1, True, False)
            with pe.Fori(0, HEADS - 2) as n:
                sb_unit(n + 2, True, True)

            def mla_rope(c):
                pe.wait_ge(C_ev, c * 5 + 3)
                ma(pt[:, 2, 256:512], rot, cqr[:], True, True).then_inc(C_rot, 1)

            def mla_scores(c):
                pe.wait_ge(C_ev, c * 5 + 5)
                pe.wait_ge(C_rope, c + 1)
                if isinstance(c, int) and c == 0:
                    pe.wait_ge(A_mo, HEADS)
                else:
                    pe.wait_ge(C_mo, c)
                for x in range(2):
                    for t in range(2):
                        tr(pt[:, 6, (2 * x + t) * P:(2 * x + t + 1) * P], ckv[:, x, 1, t * P:t * P + P], ident)
                for x in range(2):
                    r = slice(64 * x, 64 * x + 64)
                    for t, o0 in ((0, 0), (1, P)):
                        n = P * (t + 1)
                        s_ = pt[:, 4 + x, o0:o0 + n]
                        ma(s_, cqn[:, x, t * P:t * P + P], ckv[:, x, 0, 0:n], t == 0)
                        ma(s_, cqrr[r, t * P:t * P + P], krot[r, 0:n], False)
                        last = ma(s_[:, n - 64:n], cst[0:1, C_ROWSEL:C_ROWSEL + P], cst[0:1, C_COLMASK:C_COLMASK + 64],
                                  False, True)
                last.then_inc(C_s, 1)

            def mla_turn(c):
                pe.wait_ge(C_pn, c + 1)
                for x in range(2):
                    for i in range(3):
                        last = tr(pt[:, 4 + x, i * P:i * P + P], cp[:, x, i * P:i * P + P], ident)
                last.then_inc(C_pt, 1)

            def mla_values(c):
                pe.wait_ge(C_pe, c + 1)
                pe.wait_ge(C_vt, c + 1)
                for x in range(2):
                    ma(pt[:, 6, 256 * x:256 * x + 256], cvt[:, 2 * x, :], cpt[:, x, 0:256], x == 0)
                    last = ma(pt[:, 6, 256 * x + 128:256 * x + 256], cvt[:, 2 * x + 1, :], cpt[:, x, 256:384], False, True)
                last.then_inc(C_pv, 1)

            def mla_gemm(c, j):
                p = ph["C"]
                first = isinstance(c, int) and c == 0
                if j < 4:
                    if j == 0:
                        pe.wait_ge(A_ev, 2 * HEADS) if first else pe.wait_ge(C_ev, c * 5 - 4)
                    group(p, c, j, 4 * j, 4, [(pt[:, 0, 0:256], cut(0), L1T, True), (pt[:, 0, 256:512], cut(P), L1T, False)], H, KD)
                elif j < 6:
                    if j == 4:
                        if first:
                            pe.wait_ge(lat_rdy, 6)
                        else:
                            pe.wait_ge(C_ev, c * 5 - 2)
                            pe.wait_ge(C_rope, c)
                    group(p, c, j, 2 * (j - 4), 2,
                          [(pt[:, 1, 0:256], cut(0), full, True), (pt[:, 1, 256:512], cut(P), full, False),
                           (pt[:, 2, 0:256], cut(2 * P), full, True)],
                          ATT, QL)
                else:
                    if j == 6:
                        if first:
                            pe.wait_ge(lat_root, 1)
                        else:
                            pe.wait_ge(C_ev, c * 5)
                    group(p, c, j, j - 6, 1,
                          [(pt[:, 3, 0:256], cut(0), full, True), (pt[:, 3, 256:512], cut(P), full, False),
                           (pt[:, 7, 0:256], cut(2 * P), full, True), (pt[:, 7, 256:512], cut(3 * P), full, False)],
                          (att_hi[:, QL:QL + KVL, :], att_lo[:, QL:QL + KVL, :]), KVL)

            def mla_unit(c):
                for j in range(8):
                    mla_gemm(c, j)
                    if j == 0:
                        mla_rope(c - 1)
                    if j == 2:
                        mla_scores(c - 1)
                    if j == 5:
                        mla_turn(c - 1)

            sb_values(HEADS - 2)
            for j in range(8):
                mla_gemm(0, j)
                if j == 1:
                    sb_scores(HEADS - 1)
                if j == 4:
                    sb_later(HEADS - 1)
            sb_values(HEADS - 1)
            mla_unit(1)
            with pe.Fori(0, 2) as n:
                mla_values(n)
                mla_unit(n + 2)

            def out_chunk(p, c, j, tok):
                b = 4 * (c % 2)
                w = tok.stop - tok.start
                group(p, c, j, 2 * j, 2, [(pt[:, b + n, 0:w], cut(n * P), tok, True) for n in range(4)], MIX, KD)

            def y_square_sum(norm, tok):
                w = tok.stop - tok.start
                pe.wait_ge(y_ev, 4 * norm)
                pe.wait_ge(y_acc, 2 * norm)
                for i in range(4):
                    ma(pt[:, 0, 0:w], ones, yacc[:, i, 0:w], i == 0)
                for i in range(4):
                    last = ma(pt[:, 0, 0:w], ones, ysq[:, i, 0:w], False, i == 3)
                last.then_inc(sq_sum, 1)

            mla_values(2)
            mla_rope(3)
            pe.wait_ge(C_ev, 20)
            pe.wait_ge(C_rope, 4)
            for j in range(8):
                if j == 6:
                    mla_values(3)
                    pe.wait_ge(mix_rdy, 11)
                if j == 7:
                    pe.wait_ge(mix_rdy, 12)
                out_chunk(ph["D"], 0, j, full)
                if j == 1:
                    mla_scores(3)
                if j == 4:
                    mla_turn(3)
            for c in range(1, 4):
                if c >= 2:
                    pe.wait_ge(y_ev, c - 1)
                for j in range(8):
                    out_chunk(ph["D"], c, j, full)
            y_square_sum(1, full)

            FT = [(pt[:, 0, 0:NQ], cut(0), QT, True)] + [(pt[:, n, 0:L2], cut(n * P), KT2, True) for n in (1, 2, 3)]
            PTS = [(0, 0, KL[0]), (KL[0], 0, P), (KL[0] + P, 0, KL[1] - P),
                   (KL[0] + KL[1], 1, P), (KL[0] + KL[1] + P, 1, P), (KL[0] + KL[1] + 2 * P, 1, KL[2] - 2 * P)]

            def fg_scores(h):
                pe.wait_ge(F_b, h * 4 + 4)
                tr(pt[:, 6, 0:P], fv[:, 0:P], ident)
                tr(pt[:, 6, P:2 * P], fv[:, P:2 * P], ident)
                tr(pt[0:L2 - 2 * P, 6, 2 * P:3 * P], fv[:, 2 * P:L2], ident)
                for i, (b, o0) in enumerate(((4, 0), (4, KL[0]), (5, 0))):
                    s_ = pt[0:QB, b, o0:o0 + KL[i]]
                    qs = slice(QB * i, QB * i + QB)
                    ma(s_, fq[:, qs], fk[:, 0:KL[i]], i != 1)
                    ma(s_, augL[:, qs], augR[:, h, 0:KL[i]], False)
                    last = ma(s_[:, KL[i] - QB:KL[i]], cst[0:QB, C_ID:C_ID + QB], cst[0:QB, C_CAUSAL:C_CAUSAL + QB],
                              False, True)
                last.then_inc(F_s, 1)

            def fg_turn(h):
                pe.wait_ge(F_pn, h + 1)
                for i, (c0, b, n) in enumerate(PTS):
                    last = tr(pt[0:n, 4 + b, (i % 3) * QB:(i % 3) * QB + QB], fp[:, c0:c0 + n], cst[0:QB, C_ID:C_ID + QB])
                last.then_inc(F_pt, 1)

            def fg_values(h):
                pe.wait_ge(F_pa, h + 1)
                pe.wait_ge(F_pd, h + 1)
                pe.wait_ge(F_vt, h + 1)
                for i, v, blk in ((0, 0, 0), (1, 0, 1), (2, 1, 1), (3, 0, 2), (4, 1, 2), (5, 2, 2)):
                    n = PTS[i][2]
                    last = ma(pt[:, 7, blk * QB:blk * QB + QB], fvt[0:n, v, :], fpt[0:n, i, :], i == 0, i in (0, 2, 5))
                last.then_inc(F_pv, 1)

            ramp(ph["F0"], 1, FT, KT2, L2)
            for j in range(2):
                group(ph["E"], 0, j, 8 * j, 8, [(pt[:, 4, 0:L2], cut(0), KT2, True)], H, KD)

            def fg_unit(h, it, values):
                if values:
                    fg_values(h - 2)
                for j in range(8):
                    group(ph["F"], it, j, 2 * j, 2, FT, H, KD,
                          (lambda n: pe.wait_ge(F_ev, h * 4 + (n - 3))) if j == 0 else None)
                    if j == 2:
                        if not values:
                            pe.wait_ge(E_aug, 1)
                        fg_scores(h - 1)
                    if j == 5:
                        fg_turn(h - 1)

            fg_unit(1, 0, False)
            with pe.Fori(0, HEADS - 2) as n:
                fg_unit(n + 2, n + 1, True)

            def gate_group(p, it, j0, j):
                b = 0 if j < 4 else 2
                group(p, it, j0 + j, 4 * (j % 4), 4, [(pt[:, b + n, 0:NQ], cut(n * P), QT, True) for n in range(2)], H, KD)

            def up_group(p, it, j0, j):
                b, acts = (4, ATT) if j < 2 else (6, POOL)
                group(p, it, j0 + j, 4 * (j % 2), 4, [(pt[:, b + n, 0:NQ], cut(n * P), slice(0, NQ), True) for n in range(2)],
                      acts, HEADS)

            fg_values(HEADS - 2)
            pe.wait_ge(F_ev, HEADS * 4)
            for j in range(8):
                gate_group(ph["Ga"], 0, 0, j)
                if j == 2:
                    fg_scores(HEADS - 1)
                if j == 5:
                    fg_turn(HEADS - 1)
            fg_values(HEADS - 1)
            for g in range(4):
                if g == 1:
                    pe.wait_ge(F_ar, HEADS)
                if g >= 2:
                    pe.wait_ge(p_r, g - 1)
                pe.wait_ge(p_d, g + 1)
                b = 4 + 2 * (g % 2)
                group(ph["K"], 0, g, 0, 2, [(pt[:, b + n, 0:NQ], cut(n * P), slice(0, NQ), True) for n in range(2)],
                      (d_hi[:, 2 * g:2 * g + 2, :], d_lo[:, 2 * g:2 * g + 2, :]), 2)
            for j in range(4):
                if j % 2 == 0:
                    pe.wait_ge(p_r, 3 + j // 2)
                up_group(ph["Gb"], 0, 0, j)

            def pair(p, it, j0, c):
                for j in range(8):
                    if j % 4 == 0:
                        pe.wait_ge(g_ev, c * 2 - 1 + j // 4)
                    gate_group(p, it, j0, j)
                for j in range(4):
                    if j % 2 == 0:
                        pe.wait_ge(g_t, c * 2 - 1 + j // 2)
                    up_group(p, it, j0 + 8, j)

            pair(ph["G1"], 0, 0, 1)
            with pe.Fori(0, 3) as n:
                for e in range(2):
                    pair(ph["G"], n, 12 * e, n * 2 + (2 + e))

            MT = slice(0, NQ)
            for c in range(4):
                if c == 0:
                    pe.wait_ge(g_ev, 16)
                if c == 1:
                    pe.wait_ge(g_t, 16)
                if c >= 2:
                    pe.wait_ge(y_ev, 4 + c - 1)
                for j in range(8):
                    if c == 0 and j >= 6:
                        pe.wait_ge(g_mr, j + 1)
                    out_chunk(ph["H"], c, j, MT)
            y_square_sum(2, MT)

            def up_tiles(e):
                return [(pt[:, 4 * e + n, 0:NQ], cut(n * P), QT, True) for n in range(4)]

            def residual_turn(j):
                if j == 3:
                    pe.wait_ge(root_s, 5)
                if j >= 4:
                    pe.wait_ge((i_re, i_rd)[j % 2], j // 2 - 1)
                for i in range(4):
                    k, t = 2 * j + i // 2, i % 2
                    last = tr(pt[:, 4 + j % 4, (2 * t + i // 2) * P:(2 * t + i // 2 + 1) * P],
                              xT[:, k, META + t * P:META + t * P + P], ident)
                last.then_inc(i_rt, 1)

            ramp(ph["I0"], 2, up_tiles(0), QT, NQ)
            for j in range(8):
                residual_turn(j)
            pe.wait_ge(i_re, 4)
            pe.wait_ge(i_rd, 4)
            for j in range(8):
                group(ph["I0"], 1, j, 2 * j, 2, up_tiles(1), H, KD)
            with pe.Fori(0, 10) as n:
                for e in range(2):
                    pe.wait_ge(i_ev, n * 2 + (1 + e))
                    for j in range(8):
                        group(ph["I"], n, 8 * e + j, 2 * j, 2, up_tiles(e), H, KD)

            def down(it, order, opens, closes):
                for j, (kk, half) in enumerate(order):
                    pe.wait_ge(lo_done, number(ph["J"], it, j) + 1)
                    if half == 0:
                        pe.wait_ge(j_a, it * 4 + (kk + 1))
                    s = (ph["J"].first + j) % SPL
                    for t in range(2):
                        if opens and j == 0:
                            pe.wait_ge(i_ev, 21 + t)
                        for c in range(2):
                            bank = pt[:, 4 * t + 2 * half + c, :]
                            ts, cs = slice(t * P, t * P + P), slice(c * 512, c * 512 + 512)
                            ma(bank, a_hi[:, kk, ts], w_hi[:, s, cs], opens and kk == 0)
                            ma(bank, a_hi[:, kk, ts], w_lo[:, s, cs], False)
                            last = ma(bank, a_lo[:, kk, ts], w_hi[:, s, cs], False, closes and kk == 3)
                    last.then_inc(used, 1)

            down(0, ROW_MAJOR, True, False)
            with pe.Fori(0, 9) as n:
                down(n + 1, ROW_MAJOR, False, False)
            down(10, HALF_MAJOR, False, True)


        @block.scalar
        def _(act):
            A = nc.scalar.activation
            st = Steps(act, act_st)

            def hi(p, it, j):
                base, s, step = p.full[j]
                g = number(p, it, j)
                act.wait_ge(raw_in[s], base if p.iters == 1 else it * step + base)
                if p.first + j >= SPL:
                    act.wait_ge(used, g - SPL + 1)
                n = p.sizes[j][0]
                A(w_hi[:, (p.first + j) % SPL, 0:n], raw[:, s, 0:n], ACT.Copy).then_inc(hi_done, 1)

            def small(dst, src):
                act.dma_start(dst, src).then_inc(small_in, 16)

            small(cst[:], a["consts"])
            r = 0
            for name, n in VEC1:
                small(vrow[r:r + n, 0, :], a[name][0].rearrange("(r c) -> r c", c=P))
                r += n
            bi = a["b_in_2"][0]
            r = 0
            for lo, n in ((0, 24), (3080, 8), (4104, 16), (6152, 16)):
                small(vrow[r:r + n, 1, :], bi[lo:lo + n * P].rearrange("(r c) -> r c", c=P))
                r += n
            for i in range(3):
                small(vrow[0:88, 2 + i, :], a["ffn_conv_w_2"][0, i].rearrange("(r c) -> r c", c=P))
            small(vrow[0:88, 5, :], a["ffn_conv_b_2"][0].rearrange("(r c) -> r c", c=P))
            small(b_f[:], bi[3072:3080].rearrange("(r c) -> r c", c=1))
            act.dma_start(meta_in[:], a["meta_tokens_2"]).then_inc(meta_land, 16)
            act.dma_start(pos_i[:], a["positions"][0].partition_broadcast(P)).then_inc(pos_land, 16)

            def prep(norm, k, tok, g):
                if norm == 0:
                    act.wait_ge(x_ev_d, k // 4 + 1) if (k // 2) % 2 == 0 else act.wait_ge(x_ev_a, k // 4 + 1)
                else:
                    act.wait_ge(x_new, KD * (norm - 1) + k + 1)
                A(h_hi[:, k, tok], xT[:, k, tok], ACT.Copy, scale=vec[:, g + k:g + k + 1]).then_inc(h_hi_s, 1)
                A(yT[:, k, tok], xT[:, k, tok], ACT.Square).then_inc(sq_rdy, 1)

            def ramp(p, norm, tok, g, split):
                for j in range(8):
                    if j >= split:
                        hi(p, 0, j)
                    prep(norm, 2 * j, tok, g)
                    prep(norm, 2 * j + 1, tok, g)

            def sqrt_mean(dst, src, n):
                return A(dst, src, ACT.Sqrt, scale=1.0 / n, bias=EPS_AP)

            EPS_AP = stat[:, 20:21]
            act.wait_ge(vec_ev, 4)
            for b in (1, 3, 5, 7):
                act.wait_ge(x_t, b + 1)
                A(xT[:, 2 * b:2 * b + 2, META:L2], pt[:, b % 6, :].rearrange("p (k t) -> p k t", k=2), ACT.Copy).then_inc(x_ev_a, 1)
            ramp(ph["B1"], 0, L1T, V_PRE, 0)
            for j in range(8):
                hi(ph["B2"], 0, j)
                if j == 2:
                    act.wait_ge(sq_sum, 1)
                    sqrt_mean(root[:, L1T], pt[:, 7, 0:SEQ], D).then_inc(root_s, 1)
                if j == 3:
                    act.wait_ge(lat_ev, 1)
                    A(latsq[:, 0:QL, :], lat[:, 0:QL, :], ACT.Square).then_inc(lat_sq, 1)
                if j == 6:
                    act.wait_ge(tab_r, 1)
                    A(sinT[:], tb[:, 1, :], ACT.Sin).then_inc(tab_f, 1)
                    A(cosT[:], tb[:, 3, :], ACT.Sin).then_inc(tab_f, 1)
            for j in range(8):
                hi(ph["A"], 0, j)
                if j == 3:
                    act.wait_ge(lat_ev, 2)
                    A(latsq[:, QL:, :], lat[:, QL:, :], ACT.Square).then_inc(lat_sq, 1)
                    for i in range(QL + KVL):
                        A(att_hi[:, i, 0:SEQ], lat[:, i, :], ACT.Copy, scale=vec[:, V_QN + i:V_QN + i + 1]).then_inc(lat_hi_s, 1)
                if j == 6:
                    act.wait_ge(lat_sum, 1)
                    sqrt_mean(tb[:, 0, :], pt[:, 7, 0:SEQ], QL * P)
                    sqrt_mean(tb[:, 1, :], pt[:, 7, SEQ:2 * SEQ], KVL * P).then_inc(lat_root, 1)

            def sb_mix(h):
                act.wait_ge(A_mo, h + 1)
                A(mix_hi[:, bass.ds(h, 1), 0:SEQ], mo[:].unsqueeze(1), ACT.Copy).then_inc(A_mh, 1)

            def sb_gate(h):
                act.wait_ge(A_ev, h * 2 + 2)
                A(egate[:], qkvg[:, 3, :], ACT.Exp, scale=-1.0).then_inc(A_eg, 1)

            def sb_softplus(h):
                act.wait_ge(A_z, h + 1)
                st.mark(A(lnz[:], pt[:, 4, 0:384], ACT.Abs))
                st.sync()
                st.mark(A(lnz[:], lnz[:], ACT.Exp, scale=-1.0))
                st.sync()
                A(lnz[:], lnz[:], ACT.Ln, bias=ONE_AP).then_inc(A_ln, 1)
                A(vtok[:], pt[:, 5, 0:256].rearrange("p (t d) -> p t d", t=2), ACT.Copy).then_inc(A_vt, 1)

            def sb_exp(h):
                act.wait_ge(A_ex, h + 1)
                A(aw[:], pt[:, 4, 0:384], ACT.Exp).then_inc(A_e, 1)

            ONE_AP = cst[:, C_ONE:C_ONE + 1]

            def sb_unit(h, mix):
                for j in range(8):
                    hi(ph["A"], h, j)
                    if j == 2:
                        if mix:
                            sb_mix(h - 2)
                        sb_gate(h - 1)
                    if j == 4:
                        sb_softplus(h - 1)
                    if j == 7:
                        sb_exp(h - 1)

            sb_unit(1, False)
            with act.Fori(0, HEADS - 2) as n:
                st.loop(n, 2)
                sb_unit(n + 2, True)
            st.done(HEADS - 2)

            def mla_mix(c):
                act.wait_ge(C_mo, c + 1)
                A(mix_hi[:, bass.ds(c * 2 + HEADS, 2), 0:SEQ], cmo[:], ACT.Copy).then_inc(C_mh, 1)

            def mla_gate(c):
                act.wait_ge(C_ev, c * 5 + 1)
                A(csg[:], cg[:], ACT.Exp, scale=-1.0).then_inc(C_eg, 1)

            def mla_exp(c):
                act.wait_ge(C_s, c + 1)
                A(cvt[:], pt[:, 6, :].rearrange("p (i d) -> p i d", i=4), ACT.Copy).then_inc(C_vt, 1)
                for i, (x, o0, n) in enumerate(MLA_BLOCKS):
                    if i % 2 == 0:
                        act.wait_ge(C_mx, c * 4 + (i + 2))
                    A(cp[:, x, o0:o0 + n], pt[:, 4 + x, o0:o0 + n], ACT.Exp, bias=nmx[:, i:i + 1],
                      accum_out=den[:, i:i + 1]).then_inc(C_p, 1)

            def mla_turned(c):
                act.wait_ge(C_pt, c + 1)
                A(cpt[:], pt[:, 4:6, 0:384], ACT.Copy).then_inc(C_pe, 1)

            for j in range(8):
                hi(ph["C"], 0, j)
                if j == 2:
                    sb_mix(HEADS - 2)
                    sb_gate(HEADS - 1)
                if j == 4:
                    sb_softplus(HEADS - 1)
                if j == 7:
                    sb_exp(HEADS - 1)

            def mla_unit(c, mix):
                for j in range(8):
                    hi(ph["C"], c, j)
                    if j == 2:
                        if mix:
                            mla_mix(c - 2)
                        else:
                            sb_mix(HEADS - 1)
                        mla_gate(c - 1)
                    if j == 5:
                        mla_exp(c - 1)
                    if j == 7:
                        mla_turned(c - 1)

            mla_unit(1, False)
            with act.Fori(0, 2) as n:
                mla_unit(n + 2, True)

            def y_chunk(p, norm, c, tok):
                w = tok.stop - tok.start
                b = 4 * (c % 2)
                act.wait_ge(used, number(p, c, 7) + 1)
                if c >= 2:
                    act.wait_ge(y_acc, 2 * (norm - 1) + c - 1)
                i = A((ysq if c else yacc)[:, :, 0:w], pt[:, b:b + 4, 0:w], ACT.Square)
                if c == 3:
                    i.then_inc(y_ev, 1)
                i = A(yT[:, 4 * c:4 * c + 4, tok], pt[:, b:b + 4, 0:w], ACT.Copy)
                i.then_inc(y_cp if c == 3 else y_ev, 1)

            for j in range(8):
                hi(ph["D"], 0, j)
                if j == 2:
                    mla_mix(2)
                    mla_gate(3)
                if j == 4:
                    mla_exp(3)
                if j == 7:
                    mla_turned(3)
                    mla_mix(3)
            for c in range(1, 4):
                for j in range(8):
                    hi(ph["D"], c, j)
                    if j == 2:
                        y_chunk(ph["D"], 1, c - 1, L1T)
            y_chunk(ph["D"], 1, 3, L1T)
            for j in range(SPL):
                hi(ph["F0"], 0, j)
            act.wait_ge(sq_sum, 2)
            sqrt_mean(root[:, L1T], pt[:, 0, 0:SEQ], D).then_inc(root_s, 1)

            ramp(ph["F0"], 1, KT2, V_MPRE, SPL)
            hi(ph["E"], 0, 0)
            hi(ph["E"], 0, 1)

            def fg_att(h):
                act.wait_ge(F_pv, h + 1)
                A(att_hi[:, bass.ds(h, 1), :], pt[:, 7:8, 0:NQ], ACT.Copy).then_inc(F_ah, 1)

            def fg_bias(h):
                for i, dst in enumerate((fq[:], fk[:], fv[:], None)):
                    act.wait_ge(F_ev, h * 4 + (i + 1))
                    n = NQ if i == 0 else L2
                    b = bqs[:, bass.ds(h, 1)] if i == 0 else vec[:, bass.ds(h + (V_BQKV + 8 * i), 1)]
                    if i == 3:
                        A(uT[:, bass.ds(h, 1), 16:16 + L2], tf[:, 3:4, :], ACT.Identity, bias=b).then_inc(F_b, 1)
                    else:
                        A(dst, tf[:, i, 0:n], ACT.Identity, bias=b, scale=P ** -0.5 if i == 0 else 1.0).then_inc(F_b, 1)

            def fg_exp(h):
                act.wait_ge(F_s, h + 1)
                A(fvt[:, 0:2, :], pt[:, 6, 0:256].rearrange("p (t d) -> p t d", t=2), ACT.Copy)
                A(fvt[0:L2 - 2 * P, 2, :], pt[0:L2 - 2 * P, 6, 256:384], ACT.Copy).then_inc(F_vt, 1)
                for i, (b, o0, c0) in enumerate(FG_BLOCKS):
                    if i != 1:
                        act.wait_ge(F_mx, h * 3 + (2, 0, 3)[i])
                    A(fp[:, c0:c0 + KL[i]], pt[0:QB, b, o0:o0 + KL[i]], ACT.Exp, bias=nmx[0:QB, i:i + 1],
                      accum_out=den[0:QB, i:i + 1]).then_inc(F_p, 1)

            def fg_turned(h):
                act.wait_ge(F_pt, h + 1)
                A(fpt[:, 3:5, :], pt[:, 5, 0:2 * QB].rearrange("p (i q) -> p i q", i=2), ACT.Copy)
                A(fpt[0:KL[2] - 2 * P, 5, :], pt[0:KL[2] - 2 * P, 5, 2 * QB:3 * QB], ACT.Copy).then_inc(F_pa, 1)

            def fg_post(h, j, att):
                if j == 2 and att:
                    fg_att(h - 1)
                    fg_bias(h)
                if j == 5:
                    fg_exp(h)
                if j == 7:
                    fg_turned(h)

            act.wait_ge(sq_sum, 3)
            sqrt_mean(root[:], pt[:, 7, 0:L2], D).then_inc(root_s, 1)
            for j in range(8):
                hi(ph["F"], 0, j)
                if j == 0:
                    fg_bias(0)
                if j == 1:
                    act.wait_ge(E_x, 1)
                    st.mark(A(fz[:, 1, :], fz[:, 0, :], ACT.Abs))
                    st.sync()
                    st.mark(A(fz[:, 1, :], fz[:, 1, :], ACT.Exp, scale=-1.0))
                    st.sync()
                    A(fz[:, 1, :], fz[:, 1, :], ACT.Ln, bias=cst[0:8, C_ONE:C_ONE + 1]).then_inc(E_e, 1)
                fg_post(0, j, False)
            with act.Fori(0, HEADS - 2) as n:
                for j in range(8):
                    hi(ph["F"], n + 1, j)
                    fg_post(n + 1, j, True)

            def sigmoid(c, which):
                act.wait_ge(g_ev, c * 2 + (which + 1))
                for n in range(2):
                    i = A((gsa, gsp)[which][:, n, :], (gta, gtp)[which][:, n, :], ACT.Sigmoid,
                          bias=vec[:, bass.ds(c * 2 + ((V_BGA, V_BGP)[which] + n), 1)])
                i.then_inc(g_sg, 1)

            def mixed(c):
                act.wait_ge(g_m, c + 1)
                A(mix_hi[:, bass.ds(c * 2, 2), :], gta[:], ACT.Copy).then_inc(g_mh, 1)

            def pool_hi_part(g):
                act.wait_ge(F_s, HEADS)
                act.wait_ge(p_t, g + 1)
                A(d_hi[:, 2 * g:2 * g + 2, :], pdiff[:, g], ACT.Copy).then_inc(p_h, 1)

            for j in range(8):
                hi(ph["Ga"], 0, j)
                fg_post(HEADS - 1, j, True)
                if j >= 5:
                    pool_hi_part(j - 5)
            pool_hi_part(3)
            sigmoid(0, 0)
            for g in range(4):
                hi(ph["K"], 0, g)
            fg_att(HEADS - 1)
            sigmoid(0, 1)
            for g in range(4):
                act.wait_ge(used, number(ph["K"], 0, g) + 1)
                for n in range(2):
                    i = A(pool_hi[:, 2 * g + n, :], pt[:, 4 + 2 * (g % 2) + n, 0:NQ], ACT.Copy,
                          scale=vec[:, V_PSC + 2 * g + n:V_PSC + 2 * g + n + 1])
                i.then_inc(p_kh, 1)
                hi(ph["Gb"], 0, g)

            def pair(p, it, j0, c):
                for j in range(12):
                    hi(p, it, j0 + j)
                    if j == 3:
                        mixed(c - 1)
                    if j == 7:
                        sigmoid(c, 0)
                    if j == 11:
                        sigmoid(c, 1)

            pair(ph["G1"], 0, 0, 1)
            with act.Fori(0, 3) as n:
                for e in range(2):
                    pair(ph["G"], n, 12 * e, n * 2 + (2 + e))
            for c in range(4):
                for j in range(8):
                    hi(ph["H"], c, j)
                    if j == 3 and c == 0:
                        mixed(7)
                    if j == 2 and c:
                        y_chunk(ph["H"], 2, c - 1, QT)
            y_chunk(ph["H"], 2, 3, QT)
            for j in range(SPL):
                hi(ph["I0"], 0, j)
            act.wait_ge(sq_sum, 4)
            sqrt_mean(root[:, QT], pt[:, 0, 0:NQ], D).then_inc(root_s, 1)

            ramp(ph["I0"], 2, QT, V_FPRE, SPL)
            hi(ph["I0"], 1, 0)
            act.wait_ge(sq_sum, 5)
            sqrt_mean(root[:, QT], pt[:, 7, 0:NQ], D).then_inc(root_s, 1)
            for j in range(0, 8, 2):
                act.wait_ge(i_rt, j + 1)
                A(r_tok[:, :, 256 * j:256 * j + 256], pt[:, 4 + j % 4, :].rearrange("p (t c) -> p t c", t=2),
                  ACT.Copy).then_inc(i_re, 1)
                if j < 6:
                    hi(ph["I0"], 1, j // 2 + 1)

            def conv_tap2(i):
                act.wait_ge(i_ev, i + 1)
                if not (isinstance(i, int) and i == 0):
                    act.wait_ge(i_act, i)
                for n in range(4):
                    t = i * 2 + ((n // 2) * KF + n % 2)
                    ins = A(cv[:, n, :], ab[:, n, HALO:NQ], ACT.Identity, bias=cvw[:, 3, bass.ds(t, 1)],
                            scale=cvw[:, 2, bass.ds(t, 1)])
                ins.then_inc(i_cb, 1)

            def gelu(i):
                act.wait_ge(i_cv, i + 1)
                A(ge[:], cv[:, 0:2, :], ACT.Gelu_apprx_tanh).then_inc(i_ge, 1)

            for j in range(8):
                if j >= 4:
                    hi(ph["I0"], 1, j)
                if j == 4:
                    conv_tap2(0)
                if j == 6:
                    gelu(0)
            with act.Fori(0, 10) as n:
                for e in range(2):
                    for j in range(8):
                        hi(ph["I"], n, 8 * e + j)
                        if j == 2:
                            conv_tap2(n * 2 + (1 + e))
                        if j == 5:
                            gelu(n * 2 + (1 + e))

            def a_hi_part(it, kk):
                A(a_hi[:, kk, :], actT[:, bass.ds(it * 4 + kk, 1), :].rearrange("p o t -> p (o t)"), ACT.Copy).then_inc(j_hi, 1)

            def down(it, post):
                for j in range(8):
                    if j % 2 == 0:
                        a_hi_part(it, j // 2)
                    hi(ph["J"], it, j)
                    if post and j == 2:
                        conv_tap2(21)
                    if post and j == 5:
                        gelu(21)

            act.wait_ge(i_act, 20)
            down(0, True)
            with act.Fori(0, 9) as n:
                down(n + 1, False)
            act.wait_ge(i_act, 22)
            for j in range(8):
                hi(ph["J"], 10, j)
                if j < 4:
                    a_hi_part(10, j)

            def out_square(t, half):
                A(junk[:, 2 * t + half, :].rearrange("p (c n) -> p c n", c=2), pt[:, 4 * t + 2 * half:4 * t + 2 * half + 2, :], ACT.Square,
                  accum_out=stat[:, 12 + 2 * t + half:13 + 2 * t + half]).then_inc(j_sq, 1)

            act.wait_ge(used, ph["J"].first + 84)
            for t in range(2):
                out_square(t, 0)
            st.mark(A(stat[:, 16:17], stat[:, 20:21], ACT.Sqrt))
            act.wait_ge(used, ph["J"].first + 88)
            out_square(0, 1)
            act.wait_ge(j_y, 1)
            out_square(1, 1)
            st.sync()
            for t in range(2):
                act.wait_ge(j_sq, 3 + t)
                act.wait_ge(j_b, 2)
                A(stat[:, 16 + t:17 + t], stat[:, 13 + 2 * t:14 + 2 * t], ACT.Sqrt, scale=1.0 / D,
                  bias=stat[:, 18 + t:19 + t]).then_inc(j_rt, 1)
            for t in range(2):
                act.wait_ge(j_r, t + 1)
                A(o_tok[:, t, 0:1024], o_tok[:, t, 0:1024], ACT.Copy, scale=stat[:, 22 + t:23 + t]).then_inc(j_t, 1)

        @block.vector
        def _(dve):
            V = nc.vector
            st = Steps(dve, dve_st)

            def lo(p, it, j):
                s, t, n = (p.first + j) % RAW, (p.first + j) % SPL, p.sizes[j][0]
                dve.wait_ge(hi_done, number(p, it, j) + 1)
                V.tensor_tensor(w_lo[:, t, 0:n], raw[:, s, 0:n], w_hi[:, t, 0:n].bitcast(F32), ALU.subtract).then_inc(lo_done, 1)

            def stt(out_, in0, sc, in1, op0, op1):
                return V.scalar_tensor_tensor(out=out_, in0=in0, scalar=sc, in1=in1, op0=op0, op1=op1)

            def tt(out_, x, y, op):
                return V.tensor_tensor(out_, x, y, op)

            def bc(ap, n):
                return ap.unsqueeze(1).to_broadcast([P, n, ap.shape[-1]])

            def prep_lo(k, tok, g, norm):
                dve.wait_ge(h_hi_s, KD * norm + k + 1)
                stt(h_lo[:, k, tok], xT[:, k, tok], vec[:, g + k:g + k + 1], h_hi[:, k, tok].bitcast(F32),
                    ALU.mult, ALU.subtract).then_inc(h_rdy, 1)

            st.mark(V.memset(stat[:, 20:21], EPS))
            dve.wait_ge(vec_t, 1)
            V.tensor_copy(vec[:], pt[:, 6, 0:NV]).then_inc(vec_ev, 1)
            V.tensor_copy(cvw[:].rearrange("p i n -> p (i n)"), pt[:, 7, 0:352]).then_inc(vec_ev, 1)
            dve.wait_ge(vec_ev, 2)
            V.tensor_scalar(bqs[:], vec[:, V_BQKV:V_BQKV + HEADS], P ** -0.5, None, ALU.mult).then_inc(vec_ev, 1)
            V.memset(stat[:, 21:22], 0.0).then_inc(vec_ev, 1)
            for b in (0, 2, 4, 6):
                dve.wait_ge(x_t, b + 1)
                V.tensor_copy(xT[:, 2 * b:2 * b + 2, META:L2], pt[:, b % 6, :].rearrange("p (k t) -> p k t", k=2)).then_inc(x_ev_d, 1)
            dve.wait_ge(x_t, 9)
            V.tensor_copy(xT[:, :, 0:META], pt[:, 2, 0:256].rearrange("p (k t) -> p k t", k=KD)).then_inc(x_ev_d, 1)
            for j in range(8):
                lo(ph["B1"], 0, j)
                prep_lo(2 * j, L1T, V_PRE, 0)
                prep_lo(2 * j + 1, L1T, V_PRE, 0)
            for j in range(8):
                lo(ph["B2"], 0, j)
                if j == 2:
                    dve.wait_ge(root_s, 1)
                    st.mark(V.reciprocal(rstd[:, L1T], root[:, L1T]))
                    st.sync()
                    tt(lat[:, 0:QL, :], pt[:, 0:QL, 0:SEQ], bc(rstd[:, L1T], QL), ALU.mult).then_inc(lat_ev, 1)
                if j == 3:
                    dve.wait_ge(pos_land, 16)
                    st.mark(V.tensor_copy(pos_f[:], pos_i[:]))
                    st.sync()
                    st.mark(V.tensor_scalar(tb[:, 0, :], pos_f[:], cst[:, C_FREQ:C_FREQ + 1], None, ALU.mult))
                    st.sync()
                    for r, turn in ((1, 0.0), (3, 0.25)):
                        st.mark(V.tensor_scalar(tb[:, 2, :], tb[:, 0, :], INV_2PI, turn, ALU.mult, ALU.add))
                        st.sync()
                        st.mark(V.tensor_scalar(tb[:, 2, :], tb[:, 2, :], MAGIC, MAGIC, ALU.add, ALU.subtract))
                        st.sync()
                        st.mark(stt(tb[:, r, :], tb[:, 2, :], -PI_HI, tb[:, 0, :], ALU.mult, ALU.add))
                        st.sync()
                        st.mark(stt(tb[:, r, :], tb[:, 2, :], -PI_LO, tb[:, r, :], ALU.mult, ALU.add))
                        st.sync()
                        if turn:
                            st.mark(V.tensor_scalar(tb[:, r, :], tb[:, r, :], float(np.pi / 2), None, ALU.add))
                            st.sync()
                        i = V.tensor_scalar(tb[:, r, :], tb[:, r, :], 3.1415925, -3.1415925, ALU.min, ALU.max)
                        if turn:
                            i.then_inc(tab_r, 1)
                        else:
                            st.mark(i)
            for j in range(8):
                lo(ph["A"], 0, j)
                if j == 2:
                    dve.wait_ge(used, ph["A"].first)
                    tt(lat[:, QL:, :], pt[:, 4:6, 0:SEQ], bc(rstd[:, L1T], KVL), ALU.mult).then_inc(lat_ev, 1)
                    dve.wait_ge(tab_f, 2)
                    tt(kr[0:64, :], pt[0:64, 6, 0:SEQ], rstd[0:64, L1T], ALU.mult)
                    tt(kr[64:128, :], pt[0:64, 6, 0:SEQ], rstd[0:64, L1T], ALU.mult).then_inc(lat_ev, 1)
                if j == 3:
                    for i in range(QL + KVL):
                        dve.wait_ge(lat_hi_s, i + 1)
                        stt(att_lo[:, i, 0:SEQ], lat[:, i, :], vec[:, V_QN + i:V_QN + i + 1],
                            att_hi[:, i, 0:SEQ].bitcast(F32), ALU.mult, ALU.subtract).then_inc(lat_rdy, 1)
                if j == 6:
                    dve.wait_ge(lat_sum, 1)
                    tt(tb[:, 2, :], kr[:], cosT[:], ALU.mult)
                    tt(tb[:, 3, :], pt[:, 6, 256:512], sinT[:], ALU.mult).then_inc(kr_done, 1)
                    dve.wait_ge(kr_done, 1)
                    tt(krot[:], tb[:, 2, :], tb[:, 3, :], ALU.add).then_inc(kr_c, 1)
                    dve.wait_ge(lat_root, 1)
                    st.mark(V.reciprocal(r_q[:], tb[:, 0, :]))
                    st.mark(V.reciprocal(r_kv[:], tb[:, 1, :]))
                    st.sync()
                    st.mark(V.tensor_scalar(r_q[:], r_q[:], MLA_QK ** -0.5, None, ALU.mult))
                    st.sync()

            def sb_result(h):
                dve.wait_ge(A_pv, h + 1)
                dve.wait_ge(A_sg, h + 1)
                tt(mo[:], pt[:, 6, 0:256], sgate[:], ALU.mult).then_inc(A_mo, 1)

            def sb_mix(h):
                dve.wait_ge(A_mh, h + 1)
                tt(mix_lo[:, bass.ds(h, 1), 0:SEQ], mo[:].unsqueeze(1), mix_hi[:, bass.ds(h, 1), 0:SEQ].bitcast(F32),
                   ALU.subtract).then_inc(mix_rdy, 1)

            def sb_in(h):
                dve.wait_ge(used, number(ph["A"], h, 7) + 1)
                if not (isinstance(h, int) and h == 0):
                    dve.wait_ge(A_sg, h)
                stt(qkvg[:, 0, :], pt[:, 0, 0:SEQ], P ** -0.5, rstd[:, L1T], ALU.mult, ALU.mult).then_inc(A_ev, 1)
                tt(qkvg[:, 1:4, :], pt[:, 1:4, 0:SEQ], bc(rstd[:, L1T], 3), ALU.mult).then_inc(A_ev, 1)

            def sb_post(h, j, mix):
                if j == 2:
                    sb_in(h)
                    if mix:
                        sb_result(h - 1)
                        sb_mix(h - 1)
                if j == 3:
                    dve.wait_ge(A_eg, h + 1)
                    st.mark(V.tensor_scalar(egate[:], egate[:], 1.0, None, ALU.add))
                    st.sync()
                    V.reciprocal(egate[:], egate[:]).then_inc(A_rec, 1)
                if j == 4:
                    dve.wait_ge(A_ln, h + 1)
                    stt(spz[:], pt[:, 4, 0:384], 0.0, lnz[:], ALU.max, ALU.add).then_inc(A_sp, 1)

            for j in range(8):
                lo(ph["A"], 1, j)
                sb_post(0, j, False)
            with dve.Fori(0, HEADS - 2) as n:
                st.loop(n, 1)
                for j in range(8):
                    lo(ph["A"], n + 2, j)
                    sb_post(n + 1, j, True)
            st.done(HEADS - 2)
            for j in range(8):
                lo(ph["C"], 0, j)
                sb_post(HEADS - 1, j, True)

            def mla_result(c):
                dve.wait_ge(C_pv, c + 1)
                dve.wait_ge(C_sg, c + 1)
                tt(cmo[:], pt[:, 6, :].rearrange("p (x t) -> p x t", x=2), csg[:], ALU.mult).then_inc(C_mo, 1)

            def mla_mix(c):
                dve.wait_ge(C_mh, c + 1)
                tt(mix_lo[:, bass.ds(c * 2 + HEADS, 2), 0:SEQ], cmo[:], mix_hi[:, bass.ds(c * 2 + HEADS, 2), 0:SEQ].bitcast(F32),
                   ALU.subtract).then_inc(mix_rdy, 1)

            def mla_in(c):
                dve.wait_ge(used, number(ph["C"], c, 7) + 1)
                if not (isinstance(c, int) and c == 0):
                    dve.wait_ge(C_sg, c)

                def two(b):
                    return pt[:, b, :].rearrange("p (x t) -> p x t", x=2)
                tt(cg[:], two(0), bc(rstd[:, L1T], 2), ALU.mult).then_inc(C_ev, 1)
                tt(cqn[:], two(1), bc(r_q[:], 2), ALU.mult).then_inc(C_ev, 1)
                tt(cqr[:], pt[:, 2, 0:SEQ], r_q[:], ALU.mult).then_inc(C_ev, 1)
                tt(ckv[:, 0, :, :], two(3), bc(r_kv[:], 2), ALU.mult).then_inc(C_ev, 1)
                tt(ckv[:, 1, :, :], two(7), bc(r_kv[:], 2), ALU.mult).then_inc(C_ev, 1)

            def mla_post(c, j, first, early=0):
                if j == 2:
                    mla_in(c)
                    if first:
                        sb_result(HEADS - 1)
                        sb_mix(HEADS - 1)
                    else:
                        mla_result(c - 1)
                        mla_mix(c - 1)
                    dve.wait_ge(C_rot, c + 1)
                    st.mark(tt(cqrr[:], pt[:, 2, 256:512], sinT[:], ALU.mult))
                    dve.wait_ge(C_t1, c + 1)
                    st.sync()
                    tt(cqrr[:], cqrr[:], ct1[:], ALU.add).then_inc(C_rope, 1)
                if j == 3:
                    dve.wait_ge(C_eg, c + 1)
                    st.mark(V.tensor_scalar(csg[:], csg[:], 1.0, None, ALU.add))
                    st.sync()
                    V.reciprocal(csg[:], csg[:]).then_inc(C_rec, 1)
                if j == 5 - early:
                    dve.wait_ge(C_s, c + 1)
                    for i, (x, o0, n) in enumerate(MLA_BLOCKS):
                        V.tensor_reduce(nmx[:, i:i + 1], pt[:, 4 + x, o0:o0 + n], AX.X, ALU.max, negate=True).then_inc(C_mx, 1)
                if j == 6 - early:
                    dve.wait_ge(C_p, c * 4 + 4)
                    st.mark(V.reciprocal(rden, den))
                    st.sync()
                    for i, (x, o0, n) in enumerate(MLA_BLOCKS):
                        ins = V.tensor_scalar(cp[:, x, o0:o0 + n], cp[:, x, o0:o0 + n], rden[:, i:i + 1], None, ALU.mult)
                    ins.then_inc(C_pn, 1)

            for j in range(8):
                lo(ph["C"], 1, j)
                mla_post(0, j, True)
            with dve.Fori(0, 2) as n:
                st.loop(n, 3)
                for j in range(8):
                    lo(ph["C"], n + 2, j)
                    mla_post(n + 1, j, False)
            st.done(2)
            for j in range(8):
                lo(ph["D"], 0, j)
                mla_post(3, j, False, 1)
            mla_result(3)
            mla_mix(3)
            for c in range(1, 4):
                for j in range(8):
                    lo(ph["D"], c, j)

            def residual(norm, p, tok, g, gn):
                for j in range(SPL):
                    lo(p, 0, j)
                dve.wait_ge(root_s, 2 * norm)
                st.mark(V.reciprocal(rstd[:, tok], root[:, tok]))
                dve.wait_ge(y_cp, norm)
                st.sync()

                def scaled(k):
                    stt(yT[:, k, tok], yT[:, k, tok], vec[:, g + k:g + k + 1], rstd[:, tok], ALU.mult, ALU.mult).then_inc(y_t, 1)

                scaled(0)
                scaled(1)
                for k in range(KD):
                    if k % 2 == 0 and k // 2 >= SPL:
                        lo(p, 0, k // 2)
                    if k + 2 < KD:
                        scaled(k + 2)
                    prep_lo(k, KT2 if norm == 1 else tok, gn, norm)

            residual(1, ph["F0"], L1T, V_POST, V_MPRE)
            lo(ph["E"], 0, 0)
            lo(ph["E"], 0, 1)

            def fg_in(h):
                if not (isinstance(h, int) and h == 0):
                    dve.wait_ge(F_b, h * 4)
                tt(tf[:, 0, 0:NQ], pt[:, 0, 0:NQ], rstd[:, QT], ALU.mult).then_inc(F_ev, 1)
                for i in (1, 2, 3):
                    tt(tf[:, i, :], pt[:, i, 0:L2], rstd[:], ALU.mult).then_inc(F_ev, 1)

            def fg_post(h, j):
                if j == 2 and not (isinstance(h, int) and h == 0):
                    fg_in(h)
                    dve.wait_ge(F_ah, h)
                    tt(att_lo[:, bass.ds(h - 1, 1), :], pt[:, 7:8, 0:NQ], att_hi[:, bass.ds(h - 1, 1), :].bitcast(F32),
                       ALU.subtract).then_inc(F_ar, 1)
                if j == 5:
                    dve.wait_ge(F_s, h + 1)
                    for i, (b, o0, c0) in enumerate(FG_BLOCKS):
                        V.tensor_reduce(nmx[0:QB, i:i + 1], pt[0:QB, b, o0:o0 + KL[i]], AX.X, ALU.max, negate=True).then_inc(F_mx, 1)
                if j == 6:
                    dve.wait_ge(F_p, h * 3 + 3)
                    st.mark(V.reciprocal(rden[0:QB, 0:3], den[0:QB, 0:3]))
                    st.sync()
                    for i, (b, o0, c0) in enumerate(FG_BLOCKS):
                        ins = V.tensor_scalar(fp[:, c0:c0 + KL[i]], fp[:, c0:c0 + KL[i]], rden[0:QB, i:i + 1], None, ALU.mult)
                    ins.then_inc(F_pn, 1)
                if j == 7:
                    dve.wait_ge(F_pt, h + 1)
                    V.tensor_copy(fpt[0:KL[0], 0, :], pt[0:KL[0], 4, 0:QB])
                    V.tensor_copy(fpt[:, 1, :], pt[:, 4, QB:2 * QB])
                    V.tensor_copy(fpt[0:KL[1] - P, 2, :], pt[0:KL[1] - P, 4, 2 * QB:3 * QB]).then_inc(F_pd, 1)

            dve.wait_ge(root_s, 3)
            st.mark(V.reciprocal(rstd[:], root[:]))
            dve.wait_ge(used, ph["E"].first)
            st.sync()
            fg_in(0)
            for j in range(8):
                lo(ph["F"], 0, j)
                if j == 1:
                    dve.wait_ge(used, ph["F"].first)
                    st.mark(tt(fz[:, 0, :], pt[0:8, 4, 0:L2], rstd[0:8, :], ALU.mult))
                    st.sync()
                    V.tensor_scalar(fz[:, 0, :], fz[:, 0, :], b_f[:, 0:1], -1.0, ALU.add, ALU.mult).then_inc(E_x, 1)
                if j == 2:
                    dve.wait_ge(E_e, 1)
                    st.mark(stt(fz[:, 2, :], fz[:, 0, :], 0.0, fz[:, 1, :], ALU.max, ALU.add))
                    dve.wait_ge(E_pad, 1)
                    st.sync()
                    st.mark(V.tensor_tensor_scan(fz[:, 1, :], ones8[0:8, :], fz[:, 2, :], 0.0, ALU.mult, ALU.add))
                    st.sync()
                    V.tensor_scalar(augL[32:40, :], fz[:, 1, QT], -1.0, None, ALU.mult)
                    for h in range(HEADS):
                        ins = V.tensor_scalar(augR[0:8, h, :], fz[:, 1, :], cst[0:8, C_EYE8 + h:C_EYE8 + h + 1], None, ALU.mult)
                    ins.then_inc(E_aug, 1)
                fg_post(0, j)
            with dve.Fori(0, HEADS - 2) as n:
                st.loop(n, 1)
                for j in range(8):
                    lo(ph["F"], n + 1, j)
                    if j == 2:
                        dve.wait_ge(used, number(ph["F"], n, 7) + 1)
                    fg_post(n + 1, j)
            st.done(HEADS - 2)

            def pool_diff(g):
                dve.wait_ge(F_s, HEADS)
                dve.wait_ge(p_h, g + 1)
                tt(d_lo[:, 2 * g:2 * g + 2, :], pdiff[:, g], d_hi[:, 2 * g:2 * g + 2, :].bitcast(F32), ALU.subtract).then_inc(p_d, 1)

            def gate_in(p, it, j, which):
                dve.wait_ge(used, number(p, it, j) + 1)
                tt((gta, gtp)[which][:], pt[:, 2 * which:2 * which + 2, 0:NQ], bc(rstd[:, QT], 2), ALU.mult).then_inc(g_ev, 1)

            def up_in(c, last_group):
                dve.wait_ge(used, last_group + 1)
                for i, (t_, s_) in enumerate(((gta, gsa), (gtp, gsp))):
                    dve.wait_ge(g_sg, c * 2 + (i + 1))
                    tt(t_[:], pt[:, 4 + 2 * i:6 + 2 * i, 0:NQ], s_[:], ALU.mult).then_inc(g_t, 1)

            def mixed(c):
                dve.wait_ge(g_mh, c + 1)
                tt(mix_lo[:, bass.ds(c * 2, 2), :], gta[:], mix_hi[:, bass.ds(c * 2, 2), :].bitcast(F32), ALU.subtract).then_inc(g_mr, 1)

            for j in range(8):
                lo(ph["Ga"], 0, j)
                if j == 2:
                    dve.wait_ge(used, number(ph["F"], HEADS - 2, 7) + 1)
                fg_post(HEADS - 1, j)
                if j >= 5:
                    pool_diff(j - 5)
            pool_diff(3)
            gate_in(ph["Ga"], 0, 3, 0)
            for g in range(4):
                lo(ph["K"], 0, g)
            dve.wait_ge(F_ah, HEADS)
            tt(att_lo[:, HEADS - 1, :], pt[:, 7, 0:NQ], att_hi[:, HEADS - 1, :].bitcast(F32), ALU.subtract).then_inc(F_ar, 1)
            gate_in(ph["Ga"], 0, 7, 1)
            for g in range(4):
                dve.wait_ge(p_kh, g + 1)
                for n in range(2):
                    i = stt(pool_lo[:, 2 * g + n, :], pt[:, 4 + 2 * (g % 2) + n, 0:NQ],
                            vec[:, V_PSC + 2 * g + n:V_PSC + 2 * g + n + 1], pool_hi[:, 2 * g + n, :].bitcast(F32),
                            ALU.mult, ALU.subtract)
                i.then_inc(p_r, 1)
                lo(ph["Gb"], 0, g)

            def pair(p, it, j0, c, before):
                for j in range(12):
                    lo(p, it, j0 + j)
                    if j == 2:
                        up_in(c - 1, before)
                    if j == 3:
                        mixed(c - 1)
                    if j == 6:
                        dve.wait_ge(g_mr, c)
                        gate_in(p, it, j0 + 3, 0)
                    if j == 10:
                        gate_in(p, it, j0 + 7, 1)

            pair(ph["G1"], 0, 0, 1, number(ph["Gb"], 0, 3))
            with dve.Fori(0, 3) as n:
                for e in range(2):
                    pair(ph["G"], n, 12 * e, n * 2 + (2 + e), number(ph["G"], n, 12 * e - 1))
            for c in range(4):
                for j in range(8):
                    lo(ph["H"], c, j)
                    if c == 0 and j == 2:
                        up_in(7, ph["H"].first - 1)
                    if c == 0 and j == 3:
                        mixed(7)
            residual(2, ph["I0"], QT, V_MPOST, V_FPRE)

            def up_out(i, last_group, e):
                dve.wait_ge(used, last_group + 1)
                if not (isinstance(i, int) and i == 0):
                    dve.wait_ge(i_cv, i)
                tt(ab[:], pt[:, 4 * e:4 * e + 4, 0:NQ], bc(rstd[:, QT], 4), ALU.mult).then_inc(i_ev, 1)

            def conv(i):
                dve.wait_ge(i_cb, i + 1)
                for tap in (1, 0):
                    for n in range(4):
                        t = i * 2 + ((n // 2) * KF + n % 2)
                        ins = stt(cv[:, n, :], ab[:, n, tap:tap + SEQ], cvw[:, tap, bass.ds(t, 1)], cv[:, n, :], ALU.mult, ALU.add)
                    if tap:
                        st.mark(ins)
                        st.sync()
                ins.then_inc(i_cv, 1)

            lo(ph["I0"], 1, 0)
            dve.wait_ge(root_s, 5)
            st.mark(V.reciprocal(rstd[:, QT], root[:, QT]))
            for j in range(1, 8, 2):
                dve.wait_ge(i_rt, j + 1)
                V.tensor_copy(r_tok[:, :, 256 * j:256 * j + 256],
                              pt[:, 4 + j % 4, :].rearrange("p (t c) -> p t c", t=2)).then_inc(i_rd, 1)
                if j < 7:
                    lo(ph["I0"], 1, j // 2 + 1)
            st.sync()
            up_out(0, number(ph["I0"], 0, 7), 0)
            for j in range(4, 8):
                lo(ph["I0"], 1, j)
                if j == 4:
                    conv(0)
            with dve.Fori(0, 10) as n:
                st.loop(n, 2)
                for e in range(2):
                    for j in range(8):
                        lo(ph["I"], n, 8 * e + j)
                        if j == 2:
                            up_out(n * 2 + (1 + e), number(ph["I"], n, 8 * e - 1), 1 - e)
                        if j == 3:
                            conv(n * 2 + (1 + e))
            st.done(10)

            def a_lo_part(it, kk):
                dve.wait_ge(j_hi, it * 4 + (kk + 1))
                tt(a_lo[:, kk, :], actT[:, bass.ds(it * 4 + kk, 1), :].rearrange("p o t -> p (o t)"),
                   a_hi[:, kk, :].bitcast(F32), ALU.subtract).then_inc(j_a, 1)

            def down(it, post):
                for j in range(8):
                    if j % 2 == 0:
                        a_lo_part(it, j // 2)
                    lo(ph["J"], it, j)
                    if post and j == 2:
                        up_out(21, ph["J"].first - 1, 1)
                    if post and j == 3:
                        conv(21)

            down(0, True)
            with dve.Fori(0, 9) as n:
                down(n + 1, False)
            for j in range(8):
                lo(ph["J"], 10, j)
                if j < 4:
                    a_lo_part(10, j)

            def weighted(t, half):
                cs = slice(half * 1024, half * 1024 + 1024)
                return tt(o_tok[:, t, cs], pt[:, 4 * t + 2 * half:4 * t + 2 * half + 2, :].rearrange("p b n -> p (b n)"), gpost[:, cs],
                          ALU.mult)

            dve.wait_ge(gpost_land, 16)
            for t in range(2):
                dve.wait_ge(j_sq, t + 1)
                V.tensor_scalar(stat[:, 18 + t:19 + t], stat[:, 12 + 2 * t:13 + 2 * t], 1.0 / D, EPS, ALU.mult, ALU.add).then_inc(j_b, 1)
                st.mark(weighted(t, 0))
            dve.wait_ge(used, ph["J"].first + 88)
            weighted(1, 1).then_inc(j_y, 1)
            dve.wait_ge(j_sq, 3)
            st.mark(weighted(0, 1))
            st.sync()
            dve.wait_ge(j_y, 1)
            for t in range(2):
                cs = slice(1024, 2048)
                dve.wait_ge(j_rt, t + 1)
                V.reciprocal(stat[:, 22 + t:23 + t], stat[:, 16 + t:17 + t]).then_inc(j_r, 1)
                dve.wait_ge(j_r, t + 1)
                stt(o_tok[:, t, cs], o_tok[:, t, cs], stat[:, 22 + t:23 + t], r_tok[:, t, cs], ALU.mult, ALU.add).then_inc(j_od, 1)

        @block.gpsimd
        def _(pool):
            G = nc.gpsimd

            st = Steps(pool, pool_st)

            def square_sum(norm, k, tok):
                pool.wait_ge(sq_rdy, KD * norm + k + 1)
                if k > 1:
                    st.sync()
                i = G.tensor_tensor(yT[:, 0, tok], yT[:, 0, tok], yT[:, k, tok], ALU.add)
                if k < KD - 1:
                    st.mark(i)
                else:
                    i.then_inc(sq_acc, 1)

            def diagonal(m):
                v = m[:].rearrange("p (i t) -> p i t", i=3)
                for i in (0, 2):
                    r = G.affine_select(out=v[:, i, :], in_=v[:, i, :], compare_op=ALU.is_gt, fill=0.0, base=0,
                                        pattern=[[1, P]], channel_multiplier=-1)
                return r

            for k in range(1, KD):
                square_sum(0, k, L1T)
            for h in range(HEADS):
                pool.wait_ge(A_rec, h + 1)
                G.tensor_tensor(sgate[:], qkvg[:, 3, :], egate[:], ALU.mult).then_inc(A_sg, 1)
                pool.wait_ge(A_sp, h + 1)
                diagonal(spz).then_inc(A_spm, 1)
                pool.wait_ge(A_e, h + 1)
                diagonal(aw).then_inc(A_w, 1)
            with pool.Fori(0, HEADS // 2) as c:
                pool.wait_ge(C_ev, c * 5 + 3)
                G.tensor_tensor(ct1[:], cqr[:], cosT[:], ALU.mult).then_inc(C_t1, 1)
                pool.wait_ge(C_rec, c + 1)
                G.tensor_tensor(csg[:], cg[:], csg[:], ALU.mult).then_inc(C_sg, 1)

            def residual(norm, tok, w, sq_tok):
                for c in (1, 2):
                    pool.wait_ge(y_ev, 4 * (norm - 1) + c + 1)
                    if c == 2:
                        pool.wait_ge(y_acc, 2 * (norm - 1) + 1)
                    G.tensor_tensor(yacc[:, :, 0:w], yacc[:, :, 0:w], ysq[:, :, 0:w], ALU.add).then_inc(y_acc, 1)
                for k in range(KD):
                    pool.wait_ge(y_t, KD * (norm - 1) + k + 1)
                    G.tensor_tensor(xT[:, k, tok], xT[:, k, tok], yT[:, k, tok], ALU.add).then_inc(x_new, 1)
                    if k >= 3:
                        square_sum(norm, k - 2, sq_tok)
                for k in (KD - 2, KD - 1):
                    square_sum(norm, k, sq_tok)

            residual(1, L1T, SEQ, KT2)
            G.memset(augR[:], 0.0)
            G.memset(augL[:], 0.0)
            G.memset(uT[:, :, 0:16], 0.0)
            st.mark(G.memset(ones8[:], 1.0))
            st.sync()
            G.memset(augL[0:8, :], 1.0)
            for h in range(HEADS):
                i = G.tensor_scalar(augR[32:40, h, :], ones8[32:40, :], cst[32:40, C_EYE8 + h:C_EYE8 + h + 1], None, ALU.mult)
            i.then_inc(E_pad, 1)

            for g, w in enumerate(POOL_W):
                pool.wait_ge(F_b, 4 * (2 * g + 2))
                src = uT[:, 2 * g:2 * g + 2, :]
                st.mark(G.tensor_tensor(wsum[:, 0], src[:, :, 16:16 + L2], src[:, :, 15:15 + L2], ALU.add))
                k, i = 2, 0
                while k < w:
                    st.sync()
                    c = 2 * k - 2
                    st.mark(G.tensor_tensor(wsum[:, 1 - i, :, c:L2], wsum[:, i, :, c:L2], wsum[:, i, :, c - k:L2 - k], ALU.add))
                    k, i = 2 * k, 1 - i
                st.sync()
                st.mark(G.tensor_scalar(pdiff[:, g], wsum[:, i, :, QT], 1.0 / w, None, ALU.mult))
                st.sync()
                if w > T0 + 1:
                    st.mark(G.tensor_scalar(pdiff[:, g, :, 0:1], wsum[:, i, :, T0:T0 + 1], 1.0 / (T0 + 1), None, ALU.mult))
                    st.sync()
                G.tensor_tensor(pdiff[:, g], pdiff[:, g], src[:, :, 16 + T0:16 + L2], ALU.subtract).then_inc(p_t, 1)
            with pool.Fori(0, 8) as c:
                pool.wait_ge(g_t, c * 2 + 2)
                G.tensor_tensor(gta[:], gta[:], gtp[:], ALU.add).then_inc(g_m, 1)
            residual(2, QT, NQ, QT)
            with pool.Fori(0, 22) as i:
                pool.wait_ge(i_ge, i + 1)
                G.tensor_tensor(actT[:, bass.ds(i * 2, 2), :], ge[:], cv[:, 2:4, :], ALU.mult).then_inc(i_act, 1)
            for t in range(2):
                pool.wait_ge(j_t, t + 1)
                G.tensor_tensor(o_tok[:, t, 0:1024], o_tok[:, t, 0:1024], r_tok[:, t, 0:1024], ALU.add).then_inc(j_op, 1)


INPUTS = ["x", "positions", "pre_norm_w", "w_in", "q_norm_w", "w_q_up", "kv_norm_w", "w_kv_up", "w_out", "post_norm_w",
          "meta_tokens_2", "mix_pre_g_2", "w_in_2", "b_in_2", "w_attn_o_2", "pool_w_2", "pool_scale_2", "w_pool_o_2",
          "w_out_2", "mix_post_g_2", "ffn_pre_g_2", "w_ffn_up_2", "ffn_conv_w_2", "ffn_conv_b_2", "w_ffn_down_2",
          "ffn_post_g_2"]


def kernel(**inputs):
    import numpy as _np
    import concourse.bacc as _bacc
    from concourse.bass_utils import run_bass_kernel_spmd as _run

    nc = _bacc.Bacc("TRN2", target_bir_lowering=False, num_devices=1)
    arrays, args = {}, {}
    for name in INPUTS:
        arr = _np.ascontiguousarray(inputs[name])
        arrays[f"in_{name}"] = arr
        args[name] = nc.dram_tensor(f"in_{name}", arr.shape, mybir.dt.from_np(arr.dtype), kind="ExternalInput").ap()
    arr = constants()
    arrays["in_consts"] = arr
    args["consts"] = nc.dram_tensor("in_consts", arr.shape, F32, kind="ExternalInput").ap()
    out = nc.dram_tensor("out_0", (1, SEQ, D), F32, kind="ExternalOutput").ap()
    build(nc, args, out)
    r = _run(nc, [arrays], core_ids=[0])
    return r.results[0]["out_0"]
```

```python
from contextlib import ExitStack

import numpy as np
import concourse.bass as bass
from concourse import mybir

F32 = mybir.dt.float32
F32R = mybir.dt.float32r
I32 = mybir.dt.int32
ALU = mybir.AluOpType
ACT = mybir.ActivationFunctionType
AX = mybir.AxisListType

P = 128
D = 2048
SEQ = 256
META = 16
L2 = SEQ + META
HALO = 2
T0 = META - HALO
NQ = L2 - T0
KD = D // P
EPS = 1e-6
HEADS = 8
QL = 512 // P
KVL = 256 // P
ROPE = 64
MLA_QK = 192
D_FF = 5632
KF = D_FF // P
QB = NQ // 3
KL = [T0 + QB * (i + 1) for i in range(3)]
POOL_W = (2, 4, 8, 16)
BIG = 2.0 ** 100
GROUP = 1024
RAW = 8
SPL = 4

C_ID, C_ONE, C_NTRI, C_NONE, C_ROT = 0, 128, 256, 384, 512
C_CAUSAL = 640
C_FREQ = C_CAUSAL + QB
C_EYE8 = C_FREQ + 1
C_ROWSEL = C_EYE8 + 8
C_COLMASK = C_ROWSEL + 128
NCONST = C_COLMASK + 64

V_PRE, V_QN, V_KVN, V_POST, V_MPRE, V_MPOST, V_FPRE, V_PSC = 0, 16, 20, 22, 38, 54, 70, 86
NV1 = 94
V_BQKV, V_BU, V_BGA, V_BGP = 94, 118, 126, 142
NV2 = 64
NV = NV1 + NV2


VEC1 = (("pre_norm_w", 16), ("q_norm_w", 4), ("kv_norm_w", 2), ("post_norm_w", 16), ("mix_pre_g_2", 16),
        ("mix_post_g_2", 16), ("ffn_pre_g_2", 16), ("pool_scale_2", 8))
MLA_BLOCKS = ((0, 0, P), (0, P, 2 * P), (1, 0, P), (1, P, 2 * P))
FG_BLOCKS = ((4, 0, 0), (4, KL[0], KL[0]), (5, 0, KL[0] + KL[1]))
INV_2PI = float(1 / (2 * np.pi))
MAGIC = 1.5 * 2 ** 23
PI_HI, PI_LO = 6.28125, float(2 * np.pi - 6.28125)


def constants():
    c = np.zeros((P, NCONST), np.float32)
    i = np.arange(P)
    c[:, C_ID:C_ID + P] = np.eye(P)
    c[:, C_ONE:C_ONE + P] = 1
    c[:, C_NTRI:C_NTRI + P] = -(i[:, None] >= i[None, :]).astype(np.float32)
    c[:, C_NONE:C_NONE + P] = -1
    for b in range(2):
        for j in range(32):
            c[64 * b + 32 + j, C_ROT + 64 * b + j] = -1
            c[64 * b + j, C_ROT + 64 * b + 32 + j] = 1
    q = np.arange(QB)
    c[:QB, C_CAUSAL:C_CAUSAL + QB] = np.where(q[None, :] > q[:, None], -BIG, 0)
    freq = (np.float32(10000.0) ** (-np.arange(0, ROPE, 2, dtype=np.float32) / np.float32(ROPE))).astype(np.float32)
    c[:, C_FREQ] = freq[i % 32]
    c[:8, C_EYE8:C_EYE8 + 8] = np.eye(8)
    c[32:40, C_EYE8:C_EYE8 + 8] = np.eye(8)
    c[0, C_ROWSEL:C_ROWSEL + 64] = 1
    c[0, C_COLMASK:C_COLMASK + 64] = -BIG
    return c


class Phase:

    def __init__(self, name, iters, sizes):
        self.name, self.iters, self.sizes, self.n = name, iters, sizes, len(sizes)


PHASES = [
    Phase("B1", 1, [(1024, 1)] * 8),
    Phase("B2", 1, [(768, 1)] * 8),
    Phase("A", HEADS, [(1024, 2)] * 8),
    Phase("C", HEADS // 2, [(1024, 1)] * 4 + [(768, 4)] * 2 + [(512, 1)] * 2),
    Phase("D", 4, [(1024, 1)] * 8),
    Phase("F0", 1, [(1024, 3)] * 8),
    Phase("E", 1, [(1024, 1)] * 2),
    Phase("F", HEADS - 1, [(1024, 3)] * 8),
    Phase("Ga", 1, [(1024, 1)] * 8),
    Phase("K", 1, [(512, 1)] * 4),
    Phase("Gb", 1, [(1024, 1)] * 4),
    Phase("G1", 1, [(1024, 1)] * 12),
    Phase("G", 3, [(1024, 1)] * 24),
    Phase("H", 4, [(1024, 1)] * 8),
    Phase("I0", 2, [(1024, 2)] * 8),
    Phase("I", 10, [(1024, 2)] * 16),
    Phase("J", 11, [(1024, 1)] * 8),
]


ROW_MAJOR = [(kk, half) for kk in range(4) for half in range(2)]
HALF_MAJOR = [(kk, half) for half in range(2) for kk in range(4)]


def plan():
    first, filled = 0, [0] * RAW
    for ph in PHASES:
        ph.first = first
        assert ph.iters == 1 or ph.n % RAW == 0
        per, ph.full = [0] * RAW, []
        for j, (_, dmas) in enumerate(ph.sizes):
            s = (first + j) % RAW
            per[s] += 16 * dmas
            ph.full.append([filled[s] + per[s], s])
        for f in ph.full:
            f.append(per[f[1]])
        filled = [a + b * ph.iters for a, b in zip(filled, per)]
        first += ph.iters * ph.n
    return {ph.name: ph for ph in PHASES}


class Steps:

    def __init__(self, eng, sem):
        self.eng, self.sem, self.base, self.n, self.it, self.stride = eng, sem, 0, 0, None, 0

    def mark(self, ins):
        self.n += 1
        ins.then_inc(self.sem, 1)

    def sync(self):
        if self.it is None:
            if self.base + self.n > 0:
                self.eng.wait_ge(self.sem, self.base + self.n)
        else:
            self.eng.wait_ge(self.sem, self.it * self.stride + (self.base + self.n))

    def loop(self, it, stride):
        self.base, self.n, self.it, self.stride = self.base + self.n, 0, it, stride

    def done(self, iters):
        assert self.n == self.stride, f"stride is {self.n}, not {self.stride}"
        self.base, self.n, self.it = self.base + iters * self.stride, 0, None


def build(nc, a, out):
    ph = plan()
    off = [(nc.sbuf_base + 63) // 64 * 64]
    end = nc.sbuf_usable_end

    def region(nbytes):
        o = off[0]
        off[0] += (nbytes + 31) // 32 * 32
        assert off[0] <= end, (off[0], end)
        return o

    def at(o, name, shape, dt=F32):
        return nc.alloc_sbuf_tensor_at(name, shape, dt, offset=o)

    raw = at(region(RAW * GROUP * 4), "raw", [P, RAW, GROUP])
    w_hi = at(region(SPL * GROUP * 4), "w_hi", [P, SPL, GROUP], F32R)
    w_lo = at(region(SPL * GROUP * 4), "w_lo", [P, SPL, GROUP], F32R)
    X_REG = region(KD * L2 * 4)
    xT = at(X_REG, "xT", [P, KD, L2])
    H_REG = region(2 * KD * L2 * 4)
    h_hi = at(H_REG, "h_hi", [P, KD, L2], F32R)
    h_lo = at(H_REG + KD * L2 * 4, "h_lo", [P, KD, L2], F32R)
    Y_REG = region(KD * L2 * 4)
    yT = at(Y_REG, "yT", [P, KD, L2])
    MB = KD * NQ * 4
    M_REG = region(2 * MB)
    mix_hi = at(M_REG, "mix_hi", [P, KD, NQ], F32R)
    mix_lo = at(M_REG + MB, "mix_lo", [P, KD, NQ], F32R)
    AB = HEADS * NQ * 4
    AP_REG = region(4 * AB)
    att_hi = at(AP_REG, "att_hi", [P, HEADS, NQ], F32R)
    att_lo = at(AP_REG + AB, "att_lo", [P, HEADS, NQ], F32R)
    POOL_REG = AP_REG + 2 * AB
    pool_hi = at(POOL_REG, "pool_hi", [P, HEADS, NQ], F32R)
    pool_lo = at(POOL_REG + AB, "pool_lo", [P, HEADS, NQ], F32R)
    cst = at(region(NCONST * 4), "cst", [P, NCONST])
    vec = at(region(NV * 4), "vec", [P, NV])
    cvw = at(region(4 * 88 * 4), "cvw", [P, 4, 88])
    rstd = at(region(L2 * 4), "rstd", [P, L2])
    root = at(region(L2 * 4), "root", [P, L2])
    stat = at(region(24 * 4), "stat", [P, 24])
    nmx, den, rden = stat[:, 0:4], stat[:, 4:8], stat[:, 8:12]
    b_f = at(region(32), "b_f", [8, 1])
    bqs = at(region(32), "bqs", [P, HEADS])

    x_in = at(M_REG, "x_in", [P, 2, D])
    meta_in = at(M_REG + 2 * D * 4, "meta_in", [META, D])
    vrow = at(M_REG + 3 * D * 4, "vrow", [P, 6, P])
    pos_i = at(M_REG + 3 * D * 4 + 6 * P * 4, "pos_i", [P, SEQ], I32)
    pos_f = at(M_REG + 3 * D * 4 + 6 * P * 4 + SEQ * 4, "pos_f", [P, SEQ])

    junk = at(X_REG, "junk", [P, 2, D])
    r_q = at(region(SEQ * 4), "r_q", [P, SEQ])
    r_kv = at(region(SEQ * 4), "r_kv", [P, SEQ])
    r_tok = at(Y_REG, "r_tok", [P, 2, D])
    gpost = at(H_REG, "gpost", [P, D])
    o_tok = at(H_REG + D * 4, "o_tok", [P, 2, D])

    def area(o, limit, *parts):
        r, o0 = [], o
        for name, shape, dt in parts:
            r.append(at(o, name, shape, dt))
            o += (int(np.prod(shape[1:])) * 4 + 31) // 32 * 32
        assert o - o0 <= limit, (parts[0][0], o - o0, limit)
        return r

    cosT, sinT, krot, qkvg, egate, sgate, mo, lnz, spz, aw, vtok, _ = area(
        POOL_REG, 2 * AB, ("cosT", [P, SEQ], F32), ("sinT", [P, SEQ], F32), ("krot", [P, SEQ], F32),
        ("qkvg", [P, 4, SEQ], F32), ("egate", [P, SEQ], F32), ("sgate", [P, SEQ], F32), ("mo", [P, SEQ], F32),
        ("lnz", [P, 384], F32), ("spz", [P, 384], F32), ("aw", [P, 384], F32), ("vtok", [P, 2, P], F32),
        ("pad", [P, 128], F32))
    SPZ = POOL_REG + 10 * SEQ * 4
    cp = at(SPZ, "cp", [P, 2, 384])
    cpt = at(SPZ + 3072, "cpt", [P, 2, 384])
    ysq, yacc = area(H_REG, 2 * KD * L2 * 4, ("ysq", [P, 4, NQ], F32), ("yacc", [P, 4, NQ], F32))
    lat, kr, tb = area(Y_REG, KD * L2 * 4, ("lat", [P, 6, SEQ], F32), ("kr", [P, SEQ], F32), ("tb", [P, 4, SEQ], F32))
    latsq, = area(M_REG, 2 * MB, ("latsq", [P, 6, SEQ], F32))
    cg, cqn, ckv, cqr, ct1, cqrr, csg, cmo, cvt = area(
        Y_REG, KD * L2 * 4, ("cg", [P, 2, SEQ], F32), ("cqn", [P, 2, SEQ], F32), ("ckv", [P, 2, 2, SEQ], F32),
        ("cqr", [P, SEQ], F32), ("ct1", [P, SEQ], F32), ("cqrr", [P, SEQ], F32), ("csg", [P, 2, SEQ], F32),
        ("cmo", [P, 2, SEQ], F32), ("cvt", [P, 4, P], F32))
    uT, augR, augL, fz, fq, fk, fv, ones8, tf = area(
        M_REG, 2 * MB, ("uT", [P, HEADS, 16 + L2], F32), ("augR", [40, HEADS, L2], F32), ("augL", [40, NQ], F32),
        ("fz", [8, 3, L2], F32), ("fq", [P, NQ], F32), ("fk", [P, L2], F32), ("fv", [P, L2], F32),
        ("ones8", [40, L2], F32), ("tf", [P, 4, L2], F32))
    d_hi, d_lo = area(M_REG + HEADS * (16 + L2) * 4, 8704 + 1056 + 3264 + 1056 + 3 * 1088,
                      ("d_hi", [P, HEADS, NQ], F32R), ("d_lo", [P, HEADS, NQ], F32R))
    fpt, fvt, fp = area(POOL_REG, 2 * AB, ("fpt", [P, 6, QB], F32), ("fvt", [P, 3, P], F32), ("fp", [QB, sum(KL)], F32))
    gsa, gsp, gta, gtp = area(Y_REG, KD * L2 * 4, *[(n, [P, 2, NQ], F32) for n in ("gsa", "gsp", "gta", "gtp")])
    wsum, = area(Y_REG, 4 * 2 * NQ * 4, ("wsum", [P, 2, 2, L2], F32))
    pdiff, = area(Y_REG + 4 * 2 * NQ * 4, KD * L2 * 4 - 4 * 2 * NQ * 4, ("pdiff", [P, 4, 2, NQ], F32))
    actT, ab, cv, ge, a_hi, a_lo = area(
        M_REG, 2 * MB + 4 * AB, ("actT", [P, KF, SEQ], F32), ("ab", [P, 4, NQ], F32), ("cv", [P, 4, SEQ], F32),
        ("ge", [P, 2, SEQ], F32), ("a_hi", [P, 4, SEQ], F32R), ("a_lo", [P, 4, SEQ], F32R))

    sq_ffn, = area(M_REG + KF * SEQ * 4 + 4 * (NQ + SEQ) * 4, 2 * SEQ * 4, ("sq_ffn", [P, L2], F32))
    sq_tile = (yT[:, 0, :], yT[:, 0, :], sq_ffn)

    pt = nc.alloc_psum_tensor("pt", [P, 8, 512], F32)
    mask_r = at(region((2 * QB + P + 64) * 4), "mask_r", [P, 2 * QB + P + 64], F32R)
    ident_r, causal_r = mask_r[0:QB, 0:QB], mask_r[0:QB, QB:2 * QB]
    rowsel_r, colmask_r = mask_r[0:1, 2 * QB:2 * QB + P], mask_r[0:1, 2 * QB + P:]
    ident, ones = cst[:, C_ID:C_ID + P], cst[:, C_ONE:C_ONE + P]
    ntri, nones, rot = cst[:, C_NTRI:C_NTRI + P], cst[:, C_NONE:C_NONE + P], cst[:, C_ROT:C_ROT + P]
    L1T, QT, KT2 = slice(META, L2), slice(T0, L2), slice(0, L2)

    def number(p, it, j):
        return p.first + it * p.n + j

    with ExitStack() as ctx:
        def sem(name):
            return ctx.enter_context(nc.semaphore(name))

        def sems(prefix, names):
            return [sem(prefix + n) for n in names.split()]

        raw_in = [sem(f"raw_in{i}") for i in range(RAW)]
        hi_done, lo_done, used = sems("w_", "hi_done lo_done used")
        act_st, dve_st, pool_st = sems("steps_", "act dve pool")
        sp_turn = sem("sp_turn")
        small_in, bias_in, pos_land, gpost_land, out_land = sems("in_", "small bias pos gpost out")
        ident_land, cst_land = sem("in_ident"), sem("in_cst")
        x_land = [sem(f"in_x{i}") for i in range(4)]
        vec_t, vec_ev, x_t, x_ev_d, x_ev_a = sems("start_", "vec_t vec_ev x_t x_ev_d x_ev_a")
        x_new, h_hi_s, h_rdy, sq_rdy, sq_acc, sq_sum, root_s = sems("norm_", "x_new h_hi h_rdy sq acc sum root")
        lat_ev, lat_sq, lat_hi_s, lat_rdy, lat_sum, lat_root, tab_r, tab_f, kr_c, kr_done = sems(
            "lat_", "ev sq hi rdy sum root tab_r tab_f kr_c kr_done")
        A_ev, A_eg, A_rec, A_sg, A_z, A_ln, A_sp, A_spm, A_ex, A_e, A_w, A_vt, A_pv, A_mo, A_mh = sems(
            "sb_", "ev eg rec sg z ln sp spm ex e w vt pv mo mh")
        mix_rdy = sem("mix_rdy")
        C_ev, C_eg, C_rec, C_sg, C_rot, C_t1, C_rope, C_s, C_vt, C_mx, C_p, C_pn, C_pt, C_pe, C_pv, C_mo, C_mh = sems(
            "mla_", "ev eg rec sg rot t1 rope s vt mx p pn pt pe pv mo mh")
        y_ev, y_acc, y_cp, y_t, y_tile, y_sq = sems("y_", "ev acc cp t tile sq")
        F_ev, F_b, F_s, F_vt, F_mx, F_p, F_pn, F_pt, F_pa, F_pd, F_pv, F_ah, F_ar = sems(
            "fg_", "ev b s vt mx p pn pt pa pd pv ah ar")
        E_x, E_e, E_aug, E_pad = sems("forget_", "x e aug pad")
        p_t, p_h, p_d, p_kh, p_r = sems("pool_", "t h d kh r")
        g_ev, g_sg, g_t, g_m, g_mh, g_mr = sems("mixer_", "ev sg t m mh mr")
        i_ev, i_cb, i_cv, i_ge, i_act, i_rt, i_re, i_rd = sems("up_", "ev cb cv ge act rt re rd")
        j_hi, j_a, j_sq, j_b, j_rt, j_r, j_t, j_od, j_op, j_fin = sems("down_", "hi a sq b root r t od op fin")

        block = ctx.enter_context(nc.Block())

        @block.sync
        def _(sp):
            w_in1 = a["w_in"][0].rearrange("(k p) n -> p k n", p=P)
            w_in2 = a["w_in_2"][0].rearrange("(k p) n -> p k n", p=P)
            w_up = a["w_ffn_up_2"][0].rearrange("(k p) (f n) -> p k f n", p=P, f=2)

            def load(p, it, j, *pieces):
                g = number(p, it, j)
                if p.first + j >= RAW:
                    sp.wait_ge(lo_done, g - RAW + 1)
                    sp.sem_inc(sp_turn, 1)
                s = (p.first + j) % RAW
                assert len(pieces) == p.sizes[j][1]
                for dst, src in pieces:
                    sp.dma_start(dst(raw[:, s, :]), src).then_inc(raw_in[s], 16)

            def kn(k, n=None):
                return lambda r: (r if n is None else r[:, 0:k * n]).rearrange("p (k n) -> p k n", k=k)

            def row(kk, f, parts=None):
                return lambda r: r.rearrange("p (k f n) -> p k f n", k=2, f=f)[:, kk, 0:parts or f, :]

            xv = a["x"][0].rearrange("(t p) n -> p t n", p=P)
            for i in range(4):
                sp.dma_start(x_in[:, :, i * 512:i * 512 + 512], xv[:, :, i * 512:i * 512 + 512]).then_inc(x_land[i], 16)
            for j in range(8):
                load(ph["B1"], 0, j, (kn(2), w_in1[:, 2 * j:2 * j + 2, 4096:4608]))
            for j in range(8):
                load(ph["B2"], 0, j, (kn(2, 384), w_in1[:, 2 * j:2 * j + 2, 4608:4992]))
            heads1 = w_in1[:, :, 0:4096].rearrange("p k (f n) -> p k f n", f=4)
            with sp.Fori(0, HEADS) as h:
                for j in range(8):
                    load(ph["A"], h, j, *[(row(kk, 4), heads1[:, 2 * j + kk, :, bass.ds(h * P, P)]) for kk in range(2)])
            wq = a["w_q_up"][0].rearrange("(k p) n -> p k n", p=P)
            wkv = a["w_kv_up"][0].rearrange("(k p) n -> p k n", p=P)
            with sp.Fori(0, HEADS // 2) as c:
                for j in range(4):
                    load(ph["C"], c, j, (kn(4), w_in1[:, 4 * j:4 * j + 4, bass.ds(c * 256 + 4928, 256)]))
                for j in range(2):
                    load(ph["C"], c, 4 + j, *[
                        (lambda r, kk=kk, o=o, n=n: r[:, kk * 384 + o:kk * 384 + o + 2 * n].rearrange("p (h n) -> p h n", h=2),
                         wq[:, 2 * j + kk, bass.ds(c * 384, 384)].rearrange("p (h n) -> p h n", h=2)[:, :, (0, P)[o > 0]:(P, MLA_QK)[o > 0]])
                        for kk in range(2) for o, n in ((0, P), (2 * P, ROPE))])
                for j in range(2):
                    load(ph["C"], c, 6 + j, (kn(1, 512), wkv[:, j:j + 1, bass.ds(c * 512, 512)]))
            wo1 = a["w_out"][0].rearrange("(k p) n -> p k n", p=P)
            with sp.Fori(0, 4) as c:
                for j in range(8):
                    load(ph["D"], c, j, (kn(2), wo1[:, 2 * j:2 * j + 2, bass.ds(c * 512, 512)]))
            heads2 = w_in2[:, :, 0:3072].rearrange("p k (f n) -> p k f n", f=3)

            def qkvu(p, it, h):
                for j in range(8):
                    load(p, it, j,
                         *[(row(kk, 4, 3), heads2[:, 2 * j + kk, :, bass.ds(h * P, P)]) for kk in range(2)],
                         (lambda r: r.rearrange("p (k f n) -> p k f n", k=2, f=4)[:, :, 3, :],
                          w_in2[:, 2 * j:2 * j + 2, bass.ds(h * P + 3080, P)]))

            qkvu(ph["F0"], 0, 0)
            for j in range(2):
                load(ph["E"], 0, j, (kn(8), w_in2[:, 8 * j:8 * j + 8, 3072:3200]))
            with sp.Fori(0, HEADS - 1) as it:
                qkvu(ph["F"], it, it + 1)
            wao = a["w_attn_o_2"][0].rearrange("(k p) n -> p k n", p=P)
            wpo = a["w_pool_o_2"][0].rearrange("(k p) n -> p k n", p=P)

            def gates(p, it, j0, c):
                for j in range(8):
                    load(p, it, j0 + j, (kn(4), w_in2[:, 4 * (j % 4):4 * (j % 4) + 4,
                                                      bass.ds(c * 256 + (4104 if j < 4 else 6152), 256)]))

            def ups(p, it, j0, c):
                for j in range(4):
                    src = wao if j < 2 else wpo
                    load(p, it, j0 + j, (kn(4), src[:, 4 * (j % 2):4 * (j % 2) + 4, bass.ds(c * 256, 256)]))

            gates(ph["Ga"], 0, 0, 0)
            for g in range(4):
                load(ph["K"], 0, g, (kn(2, 256), a["pool_w_2"][0, g].rearrange("(k p) n -> p k n", p=P)))
            ups(ph["Gb"], 0, 0, 0)
            gates(ph["G1"], 0, 0, 1)
            ups(ph["G1"], 0, 8, 1)
            with sp.Fori(0, 3) as b:
                for e in range(2):
                    gates(ph["G"], b, 12 * e, b * 2 + (2 + e))
                    ups(ph["G"], b, 12 * e + 8, b * 2 + (2 + e))
            wo2 = a["w_out_2"][0].rearrange("(k p) n -> p k n", p=P)
            with sp.Fori(0, 4) as c:
                for j in range(8):
                    load(ph["H"], c, j, (kn(2), wo2[:, 2 * j:2 * j + 2, bass.ds(c * 512, 512)]))

            def ffn_up(p, it, j0, i):
                for j in range(8):
                    load(p, it, j0 + j, *[(row(kk, 2), w_up[:, 2 * j + kk, :, bass.ds(i * 256, 256)]) for kk in range(2)])

            with sp.Fori(0, 2) as it:
                ffn_up(ph["I0"], it, 0, it)
            with sp.Fori(0, 10) as b:
                for e in range(2):
                    ffn_up(ph["I"], b, 8 * e, b * 2 + (2 + e))
            wd = a["w_ffn_down_2"][0]

            def down(it, order):
                for j, (kk, half) in enumerate(order):
                    load(ph["J"], it, j, (lambda r: r, wd[bass.ds(it * 512 + kk * P, P), half * 1024:half * 1024 + 1024]))

            with sp.Fori(0, 10) as it:
                down(it, ROW_MAJOR)
            down(10, HALF_MAJOR)
            sp.wait_ge(used, ph["J"].first)
            sp.dma_start(gpost[:], a["ffn_post_g_2"][0].partition_broadcast(P)).then_inc(gpost_land, 16)
            outv = out[0].rearrange("(t p) n -> p t n", p=P)
            for t, c0, c1, rdy, n in ((0, 0, 1024, j_od, 1), (0, 1024, 2048, j_od, 2), (1, 512, 1024, j_od, 3),
                                      (1, 0, 512, j_op, 1), (1, 1024, 2048, j_od, 4)):
                sp.wait_ge(rdy, n)
                sp.dma_start(outv[:, t, c0:c1], o_tok[:, t, c0:c1]).then_inc(out_land, 16)
            sp.wait_ge(out_land, 80)

        @block.tensor
        def _(pe):
            def ma(out_, l, r, start, stop=False):
                return nc.tensor.matmul(out_, l, r, start=start, stop=stop, skip_group_check=True)

            tr = nc.tensor.transpose

            def group(p, it, j, k0, nk, tiles, acts, k_all, bank_free=None, tile_done=None, before_k=None):
                pe.wait_ge(lo_done, number(p, it, j) + 1)
                s = (p.first + j) % SPL
                width = p.sizes[j][0] // nk

                def products(kk, tile):
                    dst, cols, tok, opens = tile
                    k = k0 + kk
                    wh, wl = (cols(w[:, s, kk * width:kk * width + width]) for w in (w_hi, w_lo))
                    ma(dst, wh, acts[0][:, k, tok], opens and k == 0)
                    ma(dst, wh, acts[1][:, k, tok], False)
                    return ma(dst, wl, acts[0][:, k, tok], False, k == k_all - 1)

                if bank_free or tile_done:
                    for n, tile in enumerate(tiles):
                        if bank_free:
                            bank_free(n)
                        for kk in range(nk):
                            last = products(kk, tile)
                        if tile_done and n < 3:
                            last.then_inc(y_tile, 1)
                            tile_done(n)
                    last.then_inc(used, 1)
                    if tile_done:
                        tile_done(3)
                else:
                    for kk in range(nk):
                        if before_k:
                            before_k(k0 + kk)
                        for tile in tiles:
                            last = products(kk, tile)
                    last.then_inc(used, 1)

            def cut(c):
                return lambda w: w[:, c:c + P]

            def ramp(p, norm, tiles, tok, width, after=None, sums_after=7):
                for j in range(8):
                    group(p, 0, j, 2 * j, 2, tiles, H, KD, before_k=lambda k: pe.wait_ge(h_rdy, KD * norm + k + 1))
                    if j == sums_after:
                        if norm == 0:
                            pe.wait_ge(cst_land, 16)
                        if norm == 0:
                            pe.wait_ge(vec_ev, 4)
                        pe.wait_ge(sq_acc, norm + 1)
                        ma(pt[:, 7, 0:width], ones, sq_tile[norm][:, tok], True, True).then_inc(sq_sum, 1)
                    if after:
                        after(j)

            H, MIX, ATT, POOL = (h_hi, h_lo), (mix_hi, mix_lo), (att_hi, att_lo), (pool_hi, pool_lo)
            full = slice(0, SEQ)

            pe.wait_ge(ident_land, 16)
            for b in range(8):
                if b == 6:
                    pe.wait_ge(small_in, 16)
                    pe.wait_ge(x_ev_d, 1)
                    tr(pt[:, 0, 0:KD], vrow[0:KD, 0, :], cst[0:KD, C_ID:C_ID + KD]).then_inc(vec_t, 1)
                if b % 2 == 0:
                    pe.wait_ge(x_land[b // 2], 16)
                for i in range(4):
                    k, t = 2 * b + i // 2, i % 2
                    last = tr(pt[:, b, i * P:i * P + P], x_in[:, t, k * P:k * P + P], ident)
                last.then_inc(x_t, 1)

            def vectors_turn(j):
                if j == 5:
                    pe.wait_ge(bias_in, 16 * (len(VEC1) - 1 + 10))
                    pe.wait_ge(x_ev_d, 4)
                    pe.wait_ge(x_ev_a, 4)
                    tr(pt[:, 6, 0:NV1], vrow[0:NV1, 0, :], cst[0:NV1, C_ID:C_ID + NV1])
                    tr(pt[:, 6, NV1:NV], vrow[0:NV2, 1, :], cst[0:NV2, C_ID:C_ID + NV2])
                    for k in range(KD):
                        tr(pt[:, 6, 256 + k * META:256 + (k + 1) * META], meta_in[:, k * P:k * P + P],
                           cst[0:META, C_ID:C_ID + META])
                    for i in range(4):
                        last = tr(pt[:, 7, 88 * i:88 * i + 88], vrow[0:88, 2 + i, :], cst[0:88, C_ID:C_ID + 88])
                    last.then_inc(vec_t, 1)

            pe.wait_ge(vec_ev, 1)
            pe.wait_ge(x_ev_d, 2)
            pe.wait_ge(x_ev_a, 2)
            ramp(ph["B1"], 0, [(pt[:, n, 0:SEQ], cut(n * P), L1T, True) for n in range(4)], L1T, SEQ, vectors_turn)
            pe.wait_ge(vec_ev, 3)
            for j in range(8):
                group(ph["B2"], 0, j, 2 * j, 2, [(pt[:, 4 + n, 0:SEQ], cut(n * P), L1T, True) for n in range(3)], H, KD)

            def sb_values(h):
                pe.wait_ge(A_w, h + 1)
                pe.wait_ge(A_vt, h + 1)
                ma(pt[:, 6, 0:256], vtok[:, 0, :], aw[:, 0:256], True)
                ma(pt[:, 6, 128:256], vtok[:, 1, :], aw[:, 256:384], False, True).then_inc(A_pv, 1)

            def sb_scores(h):
                pe.wait_ge(A_ev, h * 2 + 2)
                for t in range(2):
                    tr(pt[:, 5, t * P:t * P + P], qkvg[:, 2, t * P:t * P + P], ident)
                ma(pt[:, 4, 0:256], qkvg[:, 1, 0:P], qkvg[:, 0, 0:256], True)
                ma(pt[:, 4, 256:384], qkvg[:, 1, P:2 * P], qkvg[:, 0, P:2 * P], False, True).then_inc(A_z, 1)

            def sb_later(h):
                pe.wait_ge(A_spm, h + 1)
                ma(pt[:, 4, 0:256], ntri, spz[:, 0:256], False)
                ma(pt[:, 4, 128:256], nones, spz[:, 256:384], False)
                ma(pt[:, 4, 256:384], ntri, spz[:, 256:384], False, True).then_inc(A_ex, 1)

            def sb_unit(h, post, values):
                def bank_free(n):
                    if post and n == 0:
                        pe.wait_ge(A_ev, h * 2 - 1)
                    elif post and n == 1:
                        pe.wait_ge(A_ev, h * 2)
                    elif n == 0:
                        pe.wait_ge(lat_ev, 1)

                if values:
                    sb_values(h - 2)
                for j in range(8):
                    group(ph["A"], h, j, 2 * j, 2, [(pt[:, n, 0:SEQ], cut(n * P), L1T, True) for n in range(4)], H, KD,
                          bank_free if j == 0 else None)
                    if post and j == 1:
                        sb_scores(h - 1)
                    if post and j == 4:
                        sb_later(h - 1)
                    if not post and j == 3:
                        pe.wait_ge(lat_sq, 2)
                        pe.wait_ge(lat_ev, 3)
                        pe.wait_ge(root_s, 1)
                        for i in range(QL):
                            ma(pt[:, 7, 0:256], ones, latsq[:, i, :], i == 0)
                        for i in range(KVL):
                            ma(pt[:, 7, 256:512], ones, latsq[:, QL + i, :], False, i == KVL - 1)
                        ma(pt[:, 6, 256:512], rot, kr[:], True, True).then_inc(lat_sum, 1)

            sb_unit(0, False, False)
            pe.wait_ge(kr_done, 1)
            sb_unit(1, True, False)
            with pe.Fori(0, HEADS - 2) as n:
                sb_unit(n + 2, True, True)

            def mla_rope(c):
                pe.wait_ge(C_ev, c * 5 + 5)
                ma(pt[:, 7, 256:512], rot, cqr[:], True, True).then_inc(C_rot, 1)

            def mla_scores(c):
                pe.wait_ge(C_ev, c * 5 + 5)
                pe.wait_ge(C_rope, c + 1)
                if isinstance(c, int) and c == 0:
                    pe.wait_ge(A_mo, HEADS)
                else:
                    pe.wait_ge(C_mo, c)
                for x in range(2):
                    for t in range(2):
                        tr(pt[:, 6, (2 * x + t) * P:(2 * x + t + 1) * P], ckv[:, x, 1, t * P:t * P + P], ident)
                for x in range(2):
                    r = slice(64 * x, 64 * x + 64)
                    for t, o0 in ((0, 0), (1, P)):
                        n = P * (t + 1)
                        s_ = pt[:, 4 + x, o0:o0 + n]
                        ma(s_, cqn[:, x, t * P:t * P + P], ckv[:, x, 0, 0:n], t == 0)
                        ma(s_, cqrr[r, t * P:t * P + P], krot[r, 0:n], False)
                        last = ma(s_[:, n - 64:n], rowsel_r, colmask_r, False, True)
                last.then_inc(C_s, 1)

            def mla_turn(c):
                pe.wait_ge(C_pn, c + 1)
                for x in range(2):
                    for i in range(3):
                        last = tr(pt[:, 4 + x, i * P:i * P + P], cp[:, x, i * P:i * P + P], ident)
                last.then_inc(C_pt, 1)

            def mla_values(c):
                pe.wait_ge(C_pe, c + 1)
                pe.wait_ge(C_vt, c + 1)
                for x in range(2):
                    ma(pt[:, 6, 256 * x:256 * x + 256], cvt[:, 2 * x, :], cpt[:, x, 0:256], x == 0)
                    last = ma(pt[:, 6, 256 * x + 128:256 * x + 256], cvt[:, 2 * x + 1, :], cpt[:, x, 256:384], False, True)
                last.then_inc(C_pv, 1)

            def mla_gemm(c, j):
                p = ph["C"]
                first = isinstance(c, int) and c == 0
                if j < 4:
                    if j == 0:
                        pe.wait_ge(A_ev, 2 * HEADS) if first else pe.wait_ge(C_ev, c * 5 - 4)
                    group(p, c, j, 4 * j, 4, [(pt[:, 0, 0:256], cut(0), L1T, True), (pt[:, 0, 256:512], cut(P), L1T, False)], H, KD)
                elif j < 6:
                    if j == 4:
                        if first:
                            pe.wait_ge(lat_rdy, 6)
                        else:
                            pe.wait_ge(C_ev, c * 5 - 2)
                    group(p, c, j, 2 * (j - 4), 2,
                          [(pt[:, 1, 0:256], cut(0), full, True), (pt[:, 1, 256:512], cut(P), full, False),
                           (pt[:, 2, 0:256], cut(2 * P), full, True)],
                          ATT, QL)
                else:
                    if j == 6:
                        if first:
                            pe.wait_ge(lat_root, 1)
                        else:
                            pe.wait_ge(C_rope, c)
                    group(p, c, j, j - 6, 1,
                          [(pt[:, 3, 0:256], cut(0), full, True), (pt[:, 3, 256:512], cut(P), full, False),
                           (pt[:, 7, 0:256], cut(2 * P), full, True), (pt[:, 7, 256:512], cut(3 * P), full, False)],
                          (att_hi[:, QL:QL + KVL, :], att_lo[:, QL:QL + KVL, :]), KVL)

            def mla_unit(c):
                for j in range(8):
                    mla_gemm(c, j)
                    if j == 1:
                        mla_rope(c - 1)
                    if j == 2:
                        mla_scores(c - 1)
                    if j == 5:
                        mla_turn(c - 1)

            sb_values(HEADS - 2)
            for j in range(8):
                mla_gemm(0, j)
                if j == 1:
                    sb_scores(HEADS - 1)
                if j == 4:
                    sb_later(HEADS - 1)
            sb_values(HEADS - 1)
            mla_unit(1)
            with pe.Fori(0, 2) as n:
                mla_values(n)
                mla_unit(n + 2)

            def out_chunk(p, c, j, tok, bank_free=None):
                norm = 1 if p is ph["D"] else 2
                last_group = c == 3 and j == 7
                if last_group:
                    y_squares(norm, tok, yacc, True, (0,))
                b = 4 * (c % 2)
                w = tok.stop - tok.start
                group(p, c, j, 2 * j, 2, [(pt[:, b + n, 0:w], cut(n * P), tok, True) for n in range(4)], MIX, KD,
                      bank_free, (lambda n: y_squares(norm, tok, ysq, False, {0: (), 3: (2, 3)}.get(n, (n - 1,))))
                      if last_group else None)

            def y_squares(norm, tok, src, opens, tiles=range(4)):
                w = tok.stop - tok.start
                if opens:
                    pe.wait_ge(y_ev, 3 * norm)
                    pe.wait_ge(y_acc, 4 * norm)
                for i in tiles:
                    if not opens:
                        pe.wait_ge(y_sq, 4 * (norm - 1) + i + 1)
                    last = ma(pt[:, 0, 0:w], ones, src[:, i, 0:w], opens and i == 0, not opens and i == 3)
                    if not opens and i == 3:
                        last.then_inc(sq_sum, 1)

            mla_values(2)
            for j in range(8):
                if j == 6:
                    mla_values(3)
                    pe.wait_ge(mix_rdy, 11)
                if j == 7:
                    pe.wait_ge(mix_rdy, 12)
                out_chunk(ph["D"], 0, j, full, (lambda n: pe.wait_ge(C_ev, 16 + n)) if j == 0 else None)
                if j == 1:
                    mla_rope(3)
                if j == 2:
                    mla_scores(3)
                if j == 4:
                    mla_turn(3)
            for c in range(1, 4):
                if c >= 2:
                    pe.wait_ge(y_ev, c - 1)
                for j in range(8):
                    out_chunk(ph["D"], c, j, full)

            FT = [(pt[:, 0, 0:NQ], cut(0), QT, True)] + [(pt[:, n, 0:L2], cut(n * P), KT2, True) for n in (1, 2, 3)]
            PTS = [(0, 0, KL[0]), (KL[0], 0, P), (KL[0] + P, 0, KL[1] - P),
                   (KL[0] + KL[1], 1, P), (KL[0] + KL[1] + P, 1, P), (KL[0] + KL[1] + 2 * P, 1, KL[2] - 2 * P)]

            def fg_scores(h):
                pe.wait_ge(F_b, h * 4 + 4)
                tr(pt[:, 6, 0:P], fv[:, 0:P], ident)
                tr(pt[:, 6, P:2 * P], fv[:, P:2 * P], ident)
                tr(pt[0:L2 - 2 * P, 6, 2 * P:3 * P], fv[:, 2 * P:L2], ident)
                for i, (b, o0) in enumerate(((4, 0), (4, KL[0]), (5, 0))):
                    s_ = pt[0:QB, b, o0:o0 + KL[i]]
                    qs = slice(QB * i, QB * i + QB)
                    ma(s_, fq[:, qs], fk[:, 0:KL[i]], i != 1)
                    ma(s_, augL[:, qs], augR[:, h, 0:KL[i]], False)
                    last = ma(s_[:, KL[i] - QB:KL[i]], ident_r, causal_r, False, True)
                last.then_inc(F_s, 1)

            def fg_turn(h):
                pe.wait_ge(F_pn, h + 1)
                for i, (c0, b, n) in enumerate(PTS):
                    last = tr(pt[0:n, 4 + b, (i % 3) * QB:(i % 3) * QB + QB], fp[:, c0:c0 + n], cst[0:QB, C_ID:C_ID + QB])
                last.then_inc(F_pt, 1)

            def fg_values(h):
                pe.wait_ge(F_pa, h + 1)
                pe.wait_ge(F_pd, h + 1)
                pe.wait_ge(F_vt, h + 1)
                for i, v, blk in ((0, 0, 0), (1, 0, 1), (2, 1, 1), (3, 0, 2), (4, 1, 2), (5, 2, 2)):
                    n = PTS[i][2]
                    last = ma(pt[:, 7, blk * QB:blk * QB + QB], fvt[0:n, v, :], fpt[0:n, i, :], i == 0, i in (0, 2, 5))
                last.then_inc(F_pv, 1)

            ramp(ph["F0"], 1, FT, KT2, L2)
            for j in range(2):
                group(ph["E"], 0, j, 8 * j, 8, [(pt[:, 4, 0:L2], cut(0), KT2, True)], H, KD)

            def fg_unit(h, it, values):
                if values:
                    fg_values(h - 2)
                for j in range(8):
                    group(ph["F"], it, j, 2 * j, 2, FT, H, KD,
                          (lambda n: pe.wait_ge(F_ev, h * 4 + (n - 3))) if j == 0 else None)
                    if j == (2 if values else 3):
                        if not values:
                            pe.wait_ge(E_aug, 1)
                        fg_scores(h - 1)
                    if j == (5 if values else 6):
                        fg_turn(h - 1)

            fg_unit(1, 0, False)
            with pe.Fori(0, HEADS - 2) as n:
                fg_unit(n + 2, n + 1, True)

            def gate_group(p, it, j0, j):
                b = 0 if j < 4 else 2
                group(p, it, j0 + j, 4 * (j % 4), 4, [(pt[:, b + n, 0:NQ], cut(n * P), QT, True) for n in range(2)], H, KD)

            def up_group(p, it, j0, j):
                b, acts = (4, ATT) if j < 2 else (6, POOL)
                group(p, it, j0 + j, 4 * (j % 2), 4, [(pt[:, b + n, 0:NQ], cut(n * P), slice(0, NQ), True) for n in range(2)],
                      acts, HEADS)

            fg_values(HEADS - 2)
            pe.wait_ge(F_ev, HEADS * 4)
            for j in range(8):
                gate_group(ph["Ga"], 0, 0, j)
                if j == 2:
                    fg_scores(HEADS - 1)
                if j == 5:
                    fg_turn(HEADS - 1)
            fg_values(HEADS - 1)
            for g in range(4):
                if g == 1:
                    pe.wait_ge(F_ar, HEADS)
                if g >= 2:
                    pe.wait_ge(p_r, g - 1)
                pe.wait_ge(p_d, g + 1)
                b = 4 + 2 * (g % 2)
                group(ph["K"], 0, g, 0, 2, [(pt[:, b + n, 0:NQ], cut(n * P), slice(0, NQ), True) for n in range(2)],
                      (d_hi[:, 2 * g:2 * g + 2, :], d_lo[:, 2 * g:2 * g + 2, :]), 2)
            for j in range(4):
                if j % 2 == 0:
                    pe.wait_ge(p_r, 3 + j // 2)
                up_group(ph["Gb"], 0, 0, j)

            def pair(p, it, j0, c):
                for j in range(8):
                    if j % 4 == 0:
                        pe.wait_ge(g_ev, c * 2 - 1 + j // 4)
                    gate_group(p, it, j0, j)
                for j in range(4):
                    if j % 2 == 0:
                        pe.wait_ge(g_t, c * 2 - 1 + j // 2)
                    up_group(p, it, j0 + 8, j)

            pair(ph["G1"], 0, 0, 1)
            with pe.Fori(0, 3) as n:
                for e in range(2):
                    pair(ph["G"], n, 12 * e, n * 2 + (2 + e))

            MT = slice(0, NQ)
            for c in range(4):
                if c == 0:
                    pe.wait_ge(g_ev, 16)
                if c == 1:
                    pe.wait_ge(g_t, 16)
                if c >= 2:
                    pe.wait_ge(y_ev, 3 + c - 1)
                for j in range(8):
                    if c == 0 and j >= 6:
                        pe.wait_ge(g_mr, j + 1)
                    out_chunk(ph["H"], c, j, MT)

            def up_tiles(e):
                return [(pt[:, 4 * e + n, 0:NQ], cut(n * P), QT, True) for n in range(4)]

            def residual_turn(j):
                if j >= 3:
                    pe.wait_ge((i_rd, i_re)[j % 2], (j - 3) // 2 + 1)
                for i in range(4):
                    k, t = 2 * j + i // 2, i % 2
                    last = tr(pt[:, 4 + j % 3, (2 * t + i // 2) * P:(2 * t + i // 2 + 1) * P],
                              xT[:, k, META + t * P:META + t * P + P], ident)
                last.then_inc(i_rt, 1)

            def turns(j):
                for i in {6: range(3), 7: range(3, 8)}.get(j, ()):
                    residual_turn(i)

            ramp(ph["I0"], 2, up_tiles(0), QT, NQ, turns, 6)
            pe.wait_ge(i_re, 4)
            pe.wait_ge(i_rd, 4)
            pe.wait_ge(root_s, 5)
            for j in range(8):
                group(ph["I0"], 1, j, 2 * j, 2, up_tiles(1), H, KD)
            with pe.Fori(0, 10) as n:
                for e in range(2):
                    pe.wait_ge(i_ev, n * 2 + (1 + e))
                    for j in range(8):
                        group(ph["I"], n, 8 * e + j, 2 * j, 2, up_tiles(e), H, KD)

            def down(it, order, opens, closes_first):
                for j, (kk, half) in enumerate(order):
                    pe.wait_ge(lo_done, number(ph["J"], it, j) + 1)
                    if half == 0:
                        pe.wait_ge(j_a, it * 4 + (kk + 1))
                    s = (ph["J"].first + j) % SPL
                    for t in range(2):
                        if opens and j == 0:
                            pe.wait_ge(i_ev, 21 + t)
                        for c in range(2):
                            bank = pt[:, 4 * t + 2 * half + c, :]
                            ts, cs = slice(t * P, t * P + P), slice(c * 512, c * 512 + 512)
                            ma(bank, a_hi[:, kk, ts], w_hi[:, s, cs], opens and kk == 0)
                            ma(bank, a_hi[:, kk, ts], w_lo[:, s, cs], False)
                            last = ma(bank, a_lo[:, kk, ts], w_hi[:, s, cs], False, closes_first and kk == 3)
                    last.then_inc(used, 1)

            down(0, ROW_MAJOR, True, False)
            with pe.Fori(0, 9) as n:
                down(n + 1, ROW_MAJOR, False, False)
            down(10, HALF_MAJOR[0:4], False, True)
            for t, cs_ in ((0, (0, 1)), (1, (0,)), (1, (1,))):
                for kk in range(4):
                    if t == 0:
                        pe.wait_ge(lo_done, number(ph["J"], 10, 4 + kk) + 1)
                    s = (ph["J"].first + 4 + kk) % SPL
                    for c in cs_:
                        bank = pt[:, 4 * t + 2 + c, :]
                        ts, cs = slice(t * P, t * P + P), slice(c * 512, c * 512 + 512)
                        ma(bank, a_hi[:, kk, ts], w_hi[:, s, cs], False)
                        ma(bank, a_hi[:, kk, ts], w_lo[:, s, cs], False)
                        last = ma(bank, a_lo[:, kk, ts], w_hi[:, s, cs], False, kk == 3)
                last.then_inc(j_fin, 1)


        @block.scalar
        def _(act):
            A = nc.scalar.activation
            st = Steps(act, act_st)

            def hi(p, it, j):
                base, s, step = p.full[j]
                g = number(p, it, j)
                act.wait_ge(raw_in[s], base if p.iters == 1 else it * step + base)
                if p.first + j >= SPL:
                    act.wait_ge(used, g - SPL + 1)
                n = p.sizes[j][0]
                A(w_hi[:, (p.first + j) % SPL, 0:n], raw[:, s, 0:n], ACT.Copy).then_inc(hi_done, 1)

            act.dma_start(cst[:, 0:P], a["consts"][:, 0:P]).then_inc(ident_land, 16)
            act.dma_start(vrow[0:KD, 0, :], a[VEC1[0][0]][0].rearrange("(r c) -> r c", c=P)).then_inc(small_in, 16)

            def high(norm, k, tok, g):
                if norm == 0:
                    act.wait_ge(x_ev_d, k // 4 + 1) if (k // 2) % 2 == 0 else act.wait_ge(x_ev_a, k // 4 + 1)
                else:
                    act.wait_ge(x_new, KD * (norm - 1) + k + 1)
                A(h_hi[:, k, tok], xT[:, k, tok], ACT.Copy, scale=vec[:, g + k:g + k + 1]).then_inc(h_hi_s, 1)

            def ramp(p, norm, tok, g, split):
                for j in range(8):
                    if j >= split:
                        hi(p, 0, j)
                    for k in (2 * j, 2 * j + 1):
                        high(norm, k, tok, g)
                    for k in (2 * j, 2 * j + 1):
                        A(yT[:, k, tok], xT[:, k, tok], ACT.Square).then_inc(sq_rdy, 1)

            def sqrt_mean(dst, src, n):
                return A(dst, src, ACT.Sqrt, scale=1.0 / n, bias=EPS_AP)

            EPS_AP = stat[:, 20:21]
            for b in (1, 3, 5, 7):
                if b == 7:
                    hi(ph["B1"], 0, 0)
                act.wait_ge(x_t, b + 1)
                A(xT[:, 2 * b:2 * b + 2, META:L2], pt[:, b, :].rearrange("p (k t) -> p k t", k=2), ACT.Copy).then_inc(x_ev_a, 1)
            act.dma_start(cst[:, P:NCONST], a["consts"][:, P:NCONST]).then_inc(cst_land, 16)
            act.wait_ge(vec_ev, 1)
            ramp(ph["B1"], 0, L1T, V_PRE, 1)
            act.wait_ge(cst_land, 16)
            for dst, c0 in ((ident_r, C_ID), (causal_r, C_CAUSAL), (rowsel_r, C_ROWSEL), (colmask_r, C_COLMASK)):
                A(dst, cst[0:dst.shape[0], c0:c0 + dst.shape[1]], ACT.Copy)
            for j in range(8):
                hi(ph["B2"], 0, j)
                if j == 2:
                    act.wait_ge(sq_sum, 1)
                    sqrt_mean(root[:, L1T], pt[:, 7, 0:SEQ], D).then_inc(root_s, 1)
                if j == 3:
                    act.wait_ge(lat_ev, 1)
                    A(latsq[:, 0:QL, :], lat[:, 0:QL, :], ACT.Square).then_inc(lat_sq, 1)
                if j == 7:
                    act.wait_ge(tab_r, 1)
                    A(sinT[:], tb[:, 1, :], ACT.Sin).then_inc(tab_f, 1)
                    A(cosT[:], tb[:, 3, :], ACT.Sin).then_inc(tab_f, 1)
            for j in range(8):
                hi(ph["A"], 0, j)
                if j == 3:
                    act.wait_ge(lat_ev, 2)
                    A(latsq[:, QL:, :], lat[:, QL:, :], ACT.Square).then_inc(lat_sq, 1)
                    for i in range(QL + KVL):
                        A(att_hi[:, i, 0:SEQ], lat[:, i, :], ACT.Copy, scale=vec[:, V_QN + i:V_QN + i + 1]).then_inc(lat_hi_s, 1)
                if j == 6:
                    act.wait_ge(lat_sum, 1)
                    sqrt_mean(tb[:, 0, :], pt[:, 7, 0:SEQ], QL * P)
                    sqrt_mean(tb[:, 1, :], pt[:, 7, SEQ:2 * SEQ], KVL * P).then_inc(lat_root, 1)

            def sb_mix(h):
                act.wait_ge(A_mo, h + 1)
                A(mix_hi[:, bass.ds(h, 1), 0:SEQ], mo[:].unsqueeze(1), ACT.Copy).then_inc(A_mh, 1)

            def sb_gate(h):
                act.wait_ge(A_ev, h * 2 + 2)
                A(egate[:], qkvg[:, 3, :], ACT.Exp, scale=-1.0).then_inc(A_eg, 1)

            def sb_softplus(h):
                act.wait_ge(A_z, h + 1)
                st.mark(A(lnz[:], pt[:, 4, 0:384], ACT.Abs))
                st.sync()
                st.mark(A(lnz[:], lnz[:], ACT.Exp, scale=-1.0))
                st.sync()
                A(lnz[:], lnz[:], ACT.Ln, bias=ONE_AP).then_inc(A_ln, 1)
                A(vtok[:], pt[:, 5, 0:256].rearrange("p (t d) -> p t d", t=2), ACT.Copy).then_inc(A_vt, 1)

            def sb_exp(h):
                act.wait_ge(A_ex, h + 1)
                A(aw[:], pt[:, 4, 0:384], ACT.Exp).then_inc(A_e, 1)

            ONE_AP = cst[:, C_ONE:C_ONE + 1]

            def sb_unit(h, mix):
                for j in range(8):
                    hi(ph["A"], h, j)
                    if j == 2:
                        if mix:
                            sb_mix(h - 2)
                        sb_gate(h - 1)
                    if j == 4:
                        sb_softplus(h - 1)
                    if j == 7:
                        sb_exp(h - 1)

            sb_unit(1, False)
            with act.Fori(0, HEADS - 2) as n:
                st.loop(n, 2)
                sb_unit(n + 2, True)
            st.done(HEADS - 2)

            def mla_mix(c):
                act.wait_ge(C_mo, c + 1)
                A(mix_hi[:, bass.ds(c * 2 + HEADS, 2), 0:SEQ], cmo[:], ACT.Copy).then_inc(C_mh, 1)

            def mla_gate(c):
                act.wait_ge(C_ev, c * 5 + 1)
                A(csg[:], cg[:], ACT.Exp, scale=-1.0).then_inc(C_eg, 1)

            def mla_exp(c):
                act.wait_ge(C_s, c + 1)
                A(cvt[:], pt[:, 6, :].rearrange("p (i d) -> p i d", i=4), ACT.Copy).then_inc(C_vt, 1)
                for i, (x, o0, n) in enumerate(MLA_BLOCKS):
                    if i % 2 == 0:
                        act.wait_ge(C_mx, c * 4 + (i + 2))
                    A(cp[:, x, o0:o0 + n], pt[:, 4 + x, o0:o0 + n], ACT.Exp, bias=nmx[:, i:i + 1],
                      accum_out=den[:, i:i + 1]).then_inc(C_p, 1)

            def mla_turned(c):
                act.wait_ge(C_pt, c + 1)
                A(cpt[:], pt[:, 4:6, 0:384], ACT.Copy).then_inc(C_pe, 1)

            for j in range(8):
                hi(ph["C"], 0, j)
                if j == 2:
                    sb_mix(HEADS - 2)
                    sb_gate(HEADS - 1)
                if j == 4:
                    sb_softplus(HEADS - 1)
                if j == 7:
                    sb_exp(HEADS - 1)

            def mla_unit(c, mix):
                for j in range(8):
                    hi(ph["C"], c, j)
                    if j == 2:
                        if mix:
                            mla_mix(c - 2)
                        else:
                            sb_mix(HEADS - 1)
                        mla_gate(c - 1)
                    if j == 5:
                        mla_exp(c - 1)
                    if j == 7:
                        mla_turned(c - 1)

            mla_unit(1, False)
            with act.Fori(0, 2) as n:
                mla_unit(n + 2, True)

            def y_chunk(p, norm, c, tok):
                w = tok.stop - tok.start
                b = 4 * (c % 2)
                if c < 3:
                    act.wait_ge(used, number(p, c, 7) + 1)
                if c >= 2:
                    act.wait_ge(y_acc, 4 * (norm - 1) + c - 1)
                if c < 3:
                    A((ysq if c else yacc)[:, :, 0:w], pt[:, b:b + 4, 0:w], ACT.Square)
                    A(yT[:, 4 * c:4 * c + 4, tok], pt[:, b:b + 4, 0:w], ACT.Copy).then_inc(y_ev, 1)
                else:
                    for n in range(4):
                        if n < 3:
                            act.wait_ge(y_tile, 3 * (norm - 1) + n + 1)
                        else:
                            act.wait_ge(used, number(p, c, 7) + 1)
                        A(ysq[:, n, 0:w], pt[:, b + n, 0:w], ACT.Square).then_inc(y_sq, 1)

            def y_root(norm, p, tok):
                w = tok.stop - tok.start
                act.wait_ge(sq_sum, 2 * norm)
                sqrt_mean(root[:, tok], pt[:, 0, 0:w], D).then_inc(root_s, 1)
                A(yT[:, 12:16, tok], pt[:, 4:8, 0:w], ACT.Copy).then_inc(y_cp, 1)
                hi(p, 0, SPL - 1)

            for j in range(8):
                hi(ph["D"], 0, j)
                if j == 2:
                    mla_mix(2)
                    mla_gate(3)
                if j == 4:
                    mla_exp(3)
                if j == 7:
                    mla_turned(3)
                    mla_mix(3)
            for c in range(1, 4):
                for j in range(8):
                    hi(ph["D"], c, j)
                    if j == 2:
                        y_chunk(ph["D"], 1, c - 1, L1T)
            A(stat[:, 21:22], stat[:, 20:21], ACT.Sqrt)
            for j in range(SPL - 1):
                hi(ph["F0"], 0, j)
            y_chunk(ph["D"], 1, 3, L1T)
            y_root(1, ph["F0"], L1T)

            ramp(ph["F0"], 1, KT2, V_MPRE, SPL)
            hi(ph["E"], 0, 0)
            hi(ph["E"], 0, 1)

            def fg_att(h):
                act.wait_ge(F_pv, h + 1)
                A(att_hi[:, bass.ds(h, 1), :], pt[:, 7:8, 0:NQ], ACT.Copy).then_inc(F_ah, 1)

            def fg_bias(h):
                for i, dst in enumerate((fq[:], fk[:], fv[:], None)):
                    act.wait_ge(F_ev, h * 4 + (i + 1))
                    n = NQ if i == 0 else L2
                    b = bqs[:, bass.ds(h, 1)] if i == 0 else vec[:, bass.ds(h + (V_BQKV + 8 * i), 1)]
                    if i == 3:
                        A(uT[:, bass.ds(h, 1), 16:16 + L2], tf[:, 3:4, :], ACT.Identity, bias=b).then_inc(F_b, 1)
                    else:
                        A(dst, tf[:, i, 0:n], ACT.Identity, bias=b, scale=P ** -0.5 if i == 0 else 1.0).then_inc(F_b, 1)

            def fg_exp(h):
                act.wait_ge(F_s, h + 1)
                A(fvt[:, 0:2, :], pt[:, 6, 0:256].rearrange("p (t d) -> p t d", t=2), ACT.Copy)
                A(fvt[0:L2 - 2 * P, 2, :], pt[0:L2 - 2 * P, 6, 256:384], ACT.Copy).then_inc(F_vt, 1)
                for i, (b, o0, c0) in enumerate(FG_BLOCKS):
                    if i != 1:
                        act.wait_ge(F_mx, h * 3 + (2, 0, 3)[i])
                    A(fp[:, c0:c0 + KL[i]], pt[0:QB, b, o0:o0 + KL[i]], ACT.Exp, bias=nmx[0:QB, i:i + 1],
                      accum_out=den[0:QB, i:i + 1]).then_inc(F_p, 1)

            def fg_turned(h):
                act.wait_ge(F_pt, h + 1)
                A(fpt[:, 3:5, :], pt[:, 5, 0:2 * QB].rearrange("p (i q) -> p i q", i=2), ACT.Copy)
                A(fpt[0:KL[2] - 2 * P, 5, :], pt[0:KL[2] - 2 * P, 5, 2 * QB:3 * QB], ACT.Copy).then_inc(F_pa, 1)

            def fg_post(h, j, att):
                if j == 2 and att:
                    fg_att(h - 1)
                    fg_bias(h)
                if j == 5:
                    fg_exp(h)
                if j == 7:
                    fg_turned(h)

            act.wait_ge(sq_sum, 3)
            sqrt_mean(root[:], pt[:, 7, 0:L2], D).then_inc(root_s, 1)
            for j in range(8):
                hi(ph["F"], 0, j)
                if j == 0:
                    fg_bias(0)
                if j == 3:
                    act.wait_ge(E_x, 1)
                    st.mark(A(fz[:, 1, :], fz[:, 0, :], ACT.Abs))
                    st.sync()
                    st.mark(A(fz[:, 1, :], fz[:, 1, :], ACT.Exp, scale=-1.0))
                    st.sync()
                    A(fz[:, 1, :], fz[:, 1, :], ACT.Ln, bias=cst[0:8, C_ONE:C_ONE + 1]).then_inc(E_e, 1)
                fg_post(0, j, False)
            with act.Fori(0, HEADS - 2) as n:
                for j in range(8):
                    hi(ph["F"], n + 1, j)
                    fg_post(n + 1, j, True)

            def sigmoid(c, which):
                act.wait_ge(g_ev, c * 2 + (which + 1))
                for n in range(2):
                    i = A((gsa, gsp)[which][:, n, :], (gta, gtp)[which][:, n, :], ACT.Sigmoid,
                          bias=vec[:, bass.ds(c * 2 + ((V_BGA, V_BGP)[which] + n), 1)])
                i.then_inc(g_sg, 1)

            def mixed(c):
                act.wait_ge(g_m, c + 1)
                A(mix_hi[:, bass.ds(c * 2, 2), :], gta[:], ACT.Copy).then_inc(g_mh, 1)

            def pool_hi_part(g):
                act.wait_ge(F_s, HEADS)
                act.wait_ge(p_t, g + 1)
                A(d_hi[:, 2 * g:2 * g + 2, :], pdiff[:, g], ACT.Copy).then_inc(p_h, 1)

            for j in range(8):
                hi(ph["Ga"], 0, j)
                fg_post(HEADS - 1, j, True)
                if j >= 5:
                    pool_hi_part(j - 5)
            pool_hi_part(3)
            sigmoid(0, 0)
            for g in range(4):
                hi(ph["K"], 0, g)
            fg_att(HEADS - 1)
            for g in range(4):
                act.wait_ge(used, number(ph["K"], 0, g) + 1)
                for n in range(2):
                    i = A(pool_hi[:, 2 * g + n, :], pt[:, 4 + 2 * (g % 2) + n, 0:NQ], ACT.Copy,
                          scale=vec[:, V_PSC + 2 * g + n:V_PSC + 2 * g + n + 1])
                i.then_inc(p_kh, 1)
                if g:
                    hi(ph["Gb"], 0, g - 1)
            hi(ph["Gb"], 0, 3)
            sigmoid(0, 1)

            def pair(p, it, j0, c):
                for j in range(12):
                    hi(p, it, j0 + j)
                    if j == 3:
                        mixed(c - 1)
                    if j == 7:
                        sigmoid(c, 0)
                    if j == 11:
                        sigmoid(c, 1)

            pair(ph["G1"], 0, 0, 1)
            with act.Fori(0, 3) as n:
                for e in range(2):
                    pair(ph["G"], n, 12 * e, n * 2 + (2 + e))
            for c in range(4):
                for j in range(8):
                    hi(ph["H"], c, j)
                    if j == 3 and c == 0:
                        mixed(7)
                    if j == 2 and c:
                        y_chunk(ph["H"], 2, c - 1, QT)
            A(stat[:, 21:22], stat[:, 20:21], ACT.Sqrt)
            for j in range(SPL - 1):
                hi(ph["I0"], 0, j)
            y_chunk(ph["H"], 2, 3, QT)
            y_root(2, ph["I0"], QT)

            ramp(ph["I0"], 2, QT, V_FPRE, SPL)
            hi(ph["I0"], 1, 0)
            hi(ph["I0"], 1, 1)
            act.wait_ge(sq_sum, 5)
            sqrt_mean(root[:, QT], pt[:, 7, 0:NQ], D).then_inc(root_s, 1)
            for j in range(0, 8, 2):
                act.wait_ge(i_rt, j + 1)
                A(r_tok[:, :, 256 * j:256 * j + 256], pt[:, 4 + j % 3, :].rearrange("p (t c) -> p t c", t=2),
                  ACT.Copy).then_inc(i_re, 1)
                if j in (2, 6):
                    hi(ph["I0"], 1, 2 + j // 4)

            def conv_tap2(i):
                act.wait_ge(i_ev, i + 1)
                if not (isinstance(i, int) and i == 0):
                    act.wait_ge(i_act, i)
                for n in range(4):
                    t = i * 2 + ((n // 2) * KF + n % 2)
                    ins = A(cv[:, n, :], ab[:, n, HALO:NQ], ACT.Identity, bias=cvw[:, 3, bass.ds(t, 1)],
                            scale=cvw[:, 2, bass.ds(t, 1)])
                ins.then_inc(i_cb, 1)

            def gelu(i):
                act.wait_ge(i_cv, i + 1)
                A(ge[:], cv[:, 0:2, :], ACT.Gelu_apprx_tanh).then_inc(i_ge, 1)

            for j in range(8):
                if j >= 4:
                    hi(ph["I0"], 1, j)
                if j == 4:
                    conv_tap2(0)
                if j == 6:
                    gelu(0)
            with act.Fori(0, 10) as n:
                for e in range(2):
                    for j in range(8):
                        hi(ph["I"], n, 8 * e + j)
                        if j == 2:
                            conv_tap2(n * 2 + (1 + e))
                        if j == 5:
                            gelu(n * 2 + (1 + e))

            def a_hi_part(it, kk):
                A(a_hi[:, kk, :], actT[:, bass.ds(it * 4 + kk, 1), :].rearrange("p o t -> p (o t)"), ACT.Copy).then_inc(j_hi, 1)

            def down(it, post):
                for j in range(8):
                    if j % 2 == 0:
                        a_hi_part(it, j // 2)
                    hi(ph["J"], it, j)
                    if post and j == 2:
                        conv_tap2(21)
                    if post and j == 5:
                        gelu(21)

            act.wait_ge(i_act, 20)
            down(0, True)
            with act.Fori(0, 9) as n:
                down(n + 1, False)
            act.wait_ge(i_act, 22)
            for j in range(8):
                hi(ph["J"], 10, j)
                if j < 4:
                    a_hi_part(10, j)

            def out_square(t, c, n, col):
                A(junk[:, t, c * 512:(c + n) * 512].rearrange("p (c n) -> p c n", c=n), pt[:, 4 * t + c:4 * t + c + n, :], ACT.Square,
                  accum_out=stat[:, col:col + 1]).then_inc(j_sq, 1)

            def out_root(t, col):
                A(stat[:, 16 + t:17 + t], stat[:, col:col + 1], ACT.Sqrt, scale=1.0 / D, bias=stat[:, 18 + t:19 + t]).then_inc(j_rt, 1)

            act.wait_ge(used, ph["J"].first + 84)
            out_square(0, 0, 2, 12)
            out_square(1, 0, 2, 14)
            st.mark(A(stat[:, 16:17], stat[:, 20:21], ACT.Sqrt))
            act.wait_ge(j_fin, 1)
            out_square(0, 2, 2, 13)
            st.sync()
            act.wait_ge(j_sq, 3)
            act.wait_ge(j_b, 1)
            out_root(0, 13)
            act.wait_ge(j_fin, 2)
            out_square(1, 2, 1, 15)
            act.wait_ge(j_fin, 3)
            out_square(1, 3, 1, 11)
            act.wait_ge(j_sq, 5)
            act.wait_ge(j_b, 3)
            out_root(1, 11)
            act.wait_ge(j_r, 2)
            A(o_tok[:, 1, 0:512], o_tok[:, 1, 0:512], ACT.Copy, scale=stat[:, 23:24]).then_inc(j_t, 1)

        @block.vector
        def _(dve):
            V = nc.vector
            st = Steps(dve, dve_st)

            def lo(p, it, j):
                s, t, n = (p.first + j) % RAW, (p.first + j) % SPL, p.sizes[j][0]
                dve.wait_ge(hi_done, number(p, it, j) + 1)
                V.tensor_tensor(w_lo[:, t, 0:n], raw[:, s, 0:n], w_hi[:, t, 0:n].bitcast(F32), ALU.subtract).then_inc(lo_done, 1)

            def stt(out_, in0, sc, in1, op0, op1):
                return V.scalar_tensor_tensor(out=out_, in0=in0, scalar=sc, in1=in1, op0=op0, op1=op1)

            def tt(out_, x, y, op):
                return V.tensor_tensor(out_, x, y, op)

            def bc(ap, n):
                return ap.unsqueeze(1).to_broadcast([P, n, ap.shape[-1]])

            def prep_lo(k, tok, g, norm):
                dve.wait_ge(h_hi_s, KD * norm + k + 1)
                stt(h_lo[:, k, tok], xT[:, k, tok], vec[:, g + k:g + k + 1], h_hi[:, k, tok].bitcast(F32),
                    ALU.mult, ALU.subtract).then_inc(h_rdy, 1)

            V.memset(stat[:, 20:21], EPS)
            for b in (0, 2, 4, 6):
                if b == 6:
                    dve.wait_ge(vec_t, 1)
                    V.tensor_copy(vec[:, 0:KD], pt[:, 0, 0:KD]).then_inc(vec_ev, 1)
                dve.wait_ge(x_t, b + 1)
                V.tensor_copy(xT[:, 2 * b:2 * b + 2, META:L2], pt[:, b, :].rearrange("p (k t) -> p k t", k=2)).then_inc(x_ev_d, 1)
            dve.wait_ge(vec_ev, 1)
            for j in range(8):
                lo(ph["B1"], 0, j)
                prep_lo(2 * j, L1T, V_PRE, 0)
                prep_lo(2 * j + 1, L1T, V_PRE, 0)
                if j == 7:
                    dve.wait_ge(vec_t, 2)
                    V.tensor_copy(vec[:, KD:NV], pt[:, 6, KD:NV]).then_inc(vec_ev, 1)
                    V.tensor_copy(xT[:, :, 0:META], pt[:, 6, 256:512].rearrange("p (k t) -> p k t", k=KD)).then_inc(vec_ev, 1)
                    V.tensor_copy(cvw[:].rearrange("p i n -> p (i n)"), pt[:, 7, 0:352]).then_inc(vec_ev, 1)
                    dve.wait_ge(vec_ev, 2)
                    V.tensor_scalar(bqs[:], vec[:, V_BQKV:V_BQKV + HEADS], P ** -0.5, None, ALU.mult).then_inc(vec_ev, 1)
            for j in range(8):
                lo(ph["B2"], 0, j)
                if j == 2:
                    dve.wait_ge(root_s, 1)
                    st.mark(V.reciprocal(rstd[:, L1T], root[:, L1T]))
                    st.sync()
                    tt(lat[:, 0:QL, :], pt[:, 0:QL, 0:SEQ], bc(rstd[:, L1T], QL), ALU.mult).then_inc(lat_ev, 1)
                if j in (3, 5):
                    if j == 3:
                        dve.wait_ge(pos_land, 16)
                        st.mark(V.tensor_copy(pos_f[:], pos_i[:]))
                        st.sync()
                        st.mark(V.tensor_scalar(tb[:, 0, :], pos_f[:], cst[:, C_FREQ:C_FREQ + 1], None, ALU.mult))
                        st.sync()
                    r, turn = {3: (1, 0.0), 5: (3, 0.25)}[j]
                    st.mark(V.tensor_scalar(tb[:, 2, :], tb[:, 0, :], INV_2PI, turn, ALU.mult, ALU.add))
                    st.sync()
                    st.mark(V.tensor_scalar(tb[:, 2, :], tb[:, 2, :], MAGIC, MAGIC, ALU.add, ALU.subtract))
                    st.sync()
                    st.mark(stt(tb[:, r, :], tb[:, 2, :], -PI_HI, tb[:, 0, :], ALU.mult, ALU.add))
                    st.sync()
                    st.mark(stt(tb[:, r, :], tb[:, 2, :], -PI_LO, tb[:, r, :], ALU.mult, ALU.add))
                    st.sync()
                    if turn:
                        st.mark(V.tensor_scalar(tb[:, r, :], tb[:, r, :], float(np.pi / 2), None, ALU.add))
                        st.sync()
                    i = V.tensor_scalar(tb[:, r, :], tb[:, r, :], 3.1415925, -3.1415925, ALU.min, ALU.max)
                    if turn:
                        i.then_inc(tab_r, 1)
                    else:
                        st.mark(i)
                        st.sync()
            for j in range(8):
                lo(ph["A"], 0, j)
                if j == 2:
                    dve.wait_ge(used, ph["A"].first)
                    tt(lat[:, QL:, :], pt[:, 4:6, 0:SEQ], bc(rstd[:, L1T], KVL), ALU.mult).then_inc(lat_ev, 1)
                    dve.wait_ge(tab_f, 2)
                    tt(kr[0:64, :], pt[0:64, 6, 0:SEQ], rstd[0:64, L1T], ALU.mult)
                    tt(kr[64:128, :], pt[0:64, 6, 0:SEQ], rstd[0:64, L1T], ALU.mult).then_inc(lat_ev, 1)
                if j == 3:
                    for i in range(QL + KVL):
                        dve.wait_ge(lat_hi_s, i + 1)
                        stt(att_lo[:, i, 0:SEQ], lat[:, i, :], vec[:, V_QN + i:V_QN + i + 1],
                            att_hi[:, i, 0:SEQ].bitcast(F32), ALU.mult, ALU.subtract).then_inc(lat_rdy, 1)
                if j == 6:
                    dve.wait_ge(lat_sum, 1)
                    tt(tb[:, 2, :], kr[:], cosT[:], ALU.mult)
                    tt(tb[:, 3, :], pt[:, 6, 256:512], sinT[:], ALU.mult).then_inc(kr_done, 1)
                    dve.wait_ge(kr_done, 1)
                    tt(krot[:], tb[:, 2, :], tb[:, 3, :], ALU.add).then_inc(kr_c, 1)
                    dve.wait_ge(lat_root, 1)
                    st.mark(V.reciprocal(r_q[:], tb[:, 0, :]))
                    st.mark(V.reciprocal(r_kv[:], tb[:, 1, :]))
                    st.sync()
                    st.mark(V.tensor_scalar(r_q[:], r_q[:], MLA_QK ** -0.5, None, ALU.mult))
                    st.sync()

            def sb_result(h):
                dve.wait_ge(A_pv, h + 1)
                dve.wait_ge(A_sg, h + 1)
                tt(mo[:], pt[:, 6, 0:256], sgate[:], ALU.mult).then_inc(A_mo, 1)

            def sb_mix(h):
                dve.wait_ge(A_mh, h + 1)
                tt(mix_lo[:, bass.ds(h, 1), 0:SEQ], mo[:].unsqueeze(1), mix_hi[:, bass.ds(h, 1), 0:SEQ].bitcast(F32),
                   ALU.subtract).then_inc(mix_rdy, 1)

            def sb_in(h):
                dve.wait_ge(used, number(ph["A"], h, 7) + 1)
                if not (isinstance(h, int) and h == 0):
                    dve.wait_ge(A_sg, h)
                stt(qkvg[:, 0, :], pt[:, 0, 0:SEQ], P ** -0.5, rstd[:, L1T], ALU.mult, ALU.mult).then_inc(A_ev, 1)
                tt(qkvg[:, 1:4, :], pt[:, 1:4, 0:SEQ], bc(rstd[:, L1T], 3), ALU.mult).then_inc(A_ev, 1)

            def sb_post(h, j, mix):
                if j == 2:
                    sb_in(h)
                    if mix:
                        sb_result(h - 1)
                        sb_mix(h - 1)
                if j == 3:
                    dve.wait_ge(A_eg, h + 1)
                    st.mark(V.tensor_scalar(egate[:], egate[:], 1.0, None, ALU.add))
                    st.sync()
                    V.reciprocal(egate[:], egate[:]).then_inc(A_rec, 1)
                if j == 4:
                    dve.wait_ge(A_ln, h + 1)
                    stt(spz[:], pt[:, 4, 0:384], 0.0, lnz[:], ALU.max, ALU.add).then_inc(A_sp, 1)

            for j in range(8):
                lo(ph["A"], 1, j)
                sb_post(0, j, False)
            with dve.Fori(0, HEADS - 2) as n:
                st.loop(n, 1)
                for j in range(8):
                    lo(ph["A"], n + 2, j)
                    sb_post(n + 1, j, True)
            st.done(HEADS - 2)
            for j in range(8):
                lo(ph["C"], 0, j)
                sb_post(HEADS - 1, j, True)

            def mla_result(c):
                dve.wait_ge(C_pv, c + 1)
                dve.wait_ge(C_sg, c + 1)
                tt(cmo[:], pt[:, 6, :].rearrange("p (x t) -> p x t", x=2), csg[:], ALU.mult).then_inc(C_mo, 1)

            def mla_mix(c):
                dve.wait_ge(C_mh, c + 1)
                tt(mix_lo[:, bass.ds(c * 2 + HEADS, 2), 0:SEQ], cmo[:], mix_hi[:, bass.ds(c * 2 + HEADS, 2), 0:SEQ].bitcast(F32),
                   ALU.subtract).then_inc(mix_rdy, 1)

            def mla_in(c):
                dve.wait_ge(used, number(ph["C"], c, 7) + 1)
                if not (isinstance(c, int) and c == 0):
                    dve.wait_ge(C_sg, c)

                def two(b):
                    return pt[:, b, :].rearrange("p (x t) -> p x t", x=2)
                tt(cg[:], two(0), bc(rstd[:, L1T], 2), ALU.mult).then_inc(C_ev, 1)
                tt(cqn[:], two(1), bc(r_q[:], 2), ALU.mult).then_inc(C_ev, 1)
                tt(cqr[:], pt[:, 2, 0:SEQ], r_q[:], ALU.mult).then_inc(C_ev, 1)
                tt(ckv[:, 0, :, :], two(3), bc(r_kv[:], 2), ALU.mult).then_inc(C_ev, 1)
                tt(ckv[:, 1, :, :], two(7), bc(r_kv[:], 2), ALU.mult).then_inc(C_ev, 1)

            def mla_post(c, j, first, early=0):
                if j == 1:
                    mla_in(c)
                    if first:
                        sb_result(HEADS - 1)
                        sb_mix(HEADS - 1)
                    else:
                        mla_result(c - 1)
                        mla_mix(c - 1)
                if j == 2:
                    dve.wait_ge(C_rot, c + 1)
                    st.mark(tt(cqrr[:], pt[:, 7, 256:512], sinT[:], ALU.mult))
                    dve.wait_ge(C_t1, c + 1)
                    st.sync()
                    tt(cqrr[:], cqrr[:], ct1[:], ALU.add).then_inc(C_rope, 1)
                if j == 3:
                    dve.wait_ge(C_eg, c + 1)
                    st.mark(V.tensor_scalar(csg[:], csg[:], 1.0, None, ALU.add))
                    st.sync()
                    V.reciprocal(csg[:], csg[:]).then_inc(C_rec, 1)
                if j == 5 - early:
                    dve.wait_ge(C_s, c + 1)
                    for i, (x, o0, n) in enumerate(MLA_BLOCKS):
                        V.tensor_reduce(nmx[:, i:i + 1], pt[:, 4 + x, o0:o0 + n], AX.X, ALU.max, negate=True).then_inc(C_mx, 1)
                if j == 6 - early:
                    dve.wait_ge(C_p, c * 4 + 4)
                    st.mark(V.reciprocal(rden, den))
                    st.sync()
                    for i, (x, o0, n) in enumerate(MLA_BLOCKS):
                        ins = V.tensor_scalar(cp[:, x, o0:o0 + n], cp[:, x, o0:o0 + n], rden[:, i:i + 1], None, ALU.mult)
                    ins.then_inc(C_pn, 1)

            for j in range(8):
                lo(ph["C"], 1, j)
                mla_post(0, j, True)
            with dve.Fori(0, 2) as n:
                st.loop(n, 3)
                for j in range(8):
                    lo(ph["C"], n + 2, j)
                    mla_post(n + 1, j, False)
            st.done(2)
            for j in range(8):
                lo(ph["D"], 0, j)
                mla_post(3, j, False, 1)
            mla_result(3)
            mla_mix(3)
            for c in range(1, 4):
                for j in range(8):
                    lo(ph["D"], c, j)

            def residual(norm, p, tok, g, gn):
                for j in range(SPL - 1):
                    lo(p, 0, j)
                dve.wait_ge(root_s, 2 * norm)
                st.mark(V.reciprocal(rstd[:, tok], root[:, tok]))
                st.sync()

                def scaled(k):
                    stt(yT[:, k, tok], yT[:, k, tok], vec[:, g + k:g + k + 1], rstd[:, tok], ALU.mult, ALU.mult).then_inc(y_t, 1)

                scaled(0)
                scaled(1)
                for k in range(KD):
                    if k == 2:
                        lo(p, 0, SPL - 1)
                    if k % 2 == 0 and k // 2 >= SPL:
                        lo(p, 0, k // 2)
                    if k == 10:
                        dve.wait_ge(y_cp, norm)
                    if k + 2 < KD:
                        scaled(k + 2)
                    prep_lo(k, KT2 if norm == 1 else tok, gn, norm)

            residual(1, ph["F0"], L1T, V_POST, V_MPRE)
            lo(ph["E"], 0, 0)
            lo(ph["E"], 0, 1)

            def fg_in(h):
                if not (isinstance(h, int) and h == 0):
                    dve.wait_ge(F_b, h * 4)
                tt(tf[:, 0, 0:NQ], pt[:, 0, 0:NQ], rstd[:, QT], ALU.mult).then_inc(F_ev, 1)
                for i in (1, 2, 3):
                    tt(tf[:, i, :], pt[:, i, 0:L2], rstd[:], ALU.mult).then_inc(F_ev, 1)

            def fg_post(h, j):
                if j == 2 and not (isinstance(h, int) and h == 0):
                    fg_in(h)
                    dve.wait_ge(F_ah, h)
                    tt(att_lo[:, bass.ds(h - 1, 1), :], pt[:, 7:8, 0:NQ], att_hi[:, bass.ds(h - 1, 1), :].bitcast(F32),
                       ALU.subtract).then_inc(F_ar, 1)
                if j == 5:
                    dve.wait_ge(F_s, h + 1)
                    for i, (b, o0, c0) in enumerate(FG_BLOCKS):
                        V.tensor_reduce(nmx[0:QB, i:i + 1], pt[0:QB, b, o0:o0 + KL[i]], AX.X, ALU.max, negate=True).then_inc(F_mx, 1)
                if j == 6:
                    dve.wait_ge(F_p, h * 3 + 3)
                    st.mark(V.reciprocal(rden[0:QB, 0:3], den[0:QB, 0:3]))
                    st.sync()
                    for i, (b, o0, c0) in enumerate(FG_BLOCKS):
                        ins = V.tensor_scalar(fp[:, c0:c0 + KL[i]], fp[:, c0:c0 + KL[i]], rden[0:QB, i:i + 1], None, ALU.mult)
                    ins.then_inc(F_pn, 1)
                if j == 7:
                    dve.wait_ge(F_pt, h + 1)
                    V.tensor_copy(fpt[0:KL[0], 0, :], pt[0:KL[0], 4, 0:QB])
                    V.tensor_copy(fpt[:, 1, :], pt[:, 4, QB:2 * QB])
                    V.tensor_copy(fpt[0:KL[1] - P, 2, :], pt[0:KL[1] - P, 4, 2 * QB:3 * QB]).then_inc(F_pd, 1)

            dve.wait_ge(root_s, 3)
            st.mark(V.reciprocal(rstd[:], root[:]))
            dve.wait_ge(used, ph["E"].first)
            st.sync()
            fg_in(0)
            for j in range(8):
                lo(ph["F"], 0, j)
                if j == 2:
                    dve.wait_ge(used, ph["F"].first)
                    st.mark(tt(fz[:, 0, :], pt[0:8, 4, 0:L2], rstd[0:8, :], ALU.mult))
                    st.sync()
                    V.tensor_scalar(fz[:, 0, :], fz[:, 0, :], b_f[:, 0:1], -1.0, ALU.add, ALU.mult).then_inc(E_x, 1)
                if j == 3:
                    dve.wait_ge(E_e, 1)
                    st.mark(stt(fz[:, 2, :], fz[:, 0, :], 0.0, fz[:, 1, :], ALU.max, ALU.add))
                    dve.wait_ge(E_pad, 1)
                    st.sync()
                    st.mark(V.tensor_tensor_scan(fz[:, 1, :], ones8[0:8, :], fz[:, 2, :], 0.0, ALU.mult, ALU.add))
                    st.sync()
                    V.tensor_scalar(augL[32:40, :], fz[:, 1, QT], -1.0, None, ALU.mult)
                    for h in range(HEADS):
                        ins = V.tensor_scalar(augR[0:8, h, :], fz[:, 1, :], cst[0:8, C_EYE8 + h:C_EYE8 + h + 1], None, ALU.mult)
                    ins.then_inc(E_aug, 1)
                fg_post(0, j)
            with dve.Fori(0, HEADS - 2) as n:
                st.loop(n, 1)
                for j in range(8):
                    lo(ph["F"], n + 1, j)
                    if j == 2:
                        dve.wait_ge(used, number(ph["F"], n, 7) + 1)
                    fg_post(n + 1, j)
            st.done(HEADS - 2)

            def pool_diff(g):
                dve.wait_ge(F_s, HEADS)
                dve.wait_ge(p_h, g + 1)
                tt(d_lo[:, 2 * g:2 * g + 2, :], pdiff[:, g], d_hi[:, 2 * g:2 * g + 2, :].bitcast(F32), ALU.subtract).then_inc(p_d, 1)

            def gate_in(p, it, j, which):
                dve.wait_ge(used, number(p, it, j) + 1)
                tt((gta, gtp)[which][:], pt[:, 2 * which:2 * which + 2, 0:NQ], bc(rstd[:, QT], 2), ALU.mult).then_inc(g_ev, 1)

            def up_in(c, last_group):
                dve.wait_ge(used, last_group + 1)
                for i, (t_, s_) in enumerate(((gta, gsa), (gtp, gsp))):
                    dve.wait_ge(g_sg, c * 2 + (i + 1))
                    tt(t_[:], pt[:, 4 + 2 * i:6 + 2 * i, 0:NQ], s_[:], ALU.mult).then_inc(g_t, 1)

            def mixed(c):
                dve.wait_ge(g_mh, c + 1)
                tt(mix_lo[:, bass.ds(c * 2, 2), :], gta[:], mix_hi[:, bass.ds(c * 2, 2), :].bitcast(F32), ALU.subtract).then_inc(g_mr, 1)

            for j in range(8):
                lo(ph["Ga"], 0, j)
                if j == 2:
                    dve.wait_ge(used, number(ph["F"], HEADS - 2, 7) + 1)
                fg_post(HEADS - 1, j)
                if j >= 5:
                    pool_diff(j - 5)
            pool_diff(3)
            gate_in(ph["Ga"], 0, 3, 0)
            for g in range(4):
                lo(ph["K"], 0, g)
            dve.wait_ge(F_ah, HEADS)
            tt(att_lo[:, HEADS - 1, :], pt[:, 7, 0:NQ], att_hi[:, HEADS - 1, :].bitcast(F32), ALU.subtract).then_inc(F_ar, 1)
            for g in range(4):
                dve.wait_ge(p_kh, g + 1)
                for n in range(2):
                    i = stt(pool_lo[:, 2 * g + n, :], pt[:, 4 + 2 * (g % 2) + n, 0:NQ],
                            vec[:, V_PSC + 2 * g + n:V_PSC + 2 * g + n + 1], pool_hi[:, 2 * g + n, :].bitcast(F32),
                            ALU.mult, ALU.subtract)
                i.then_inc(p_r, 1)
                if g:
                    lo(ph["Gb"], 0, g - 1)
            lo(ph["Gb"], 0, 3)
            gate_in(ph["Ga"], 0, 7, 1)

            def pair(p, it, j0, c, before):
                for j in range(12):
                    lo(p, it, j0 + j)
                    if j == 2:
                        up_in(c - 1, before)
                    if j == 3:
                        mixed(c - 1)
                    if j == 6:
                        dve.wait_ge(g_mr, c)
                        gate_in(p, it, j0 + 3, 0)
                    if j == 10:
                        gate_in(p, it, j0 + 7, 1)

            pair(ph["G1"], 0, 0, 1, number(ph["Gb"], 0, 3))
            with dve.Fori(0, 3) as n:
                for e in range(2):
                    pair(ph["G"], n, 12 * e, n * 2 + (2 + e), number(ph["G"], n, 12 * e - 1))
            for c in range(4):
                for j in range(8):
                    lo(ph["H"], c, j)
                    if c == 0 and j == 2:
                        up_in(7, ph["H"].first - 1)
                    if c == 0 and j == 3:
                        mixed(7)
            residual(2, ph["I0"], QT, V_MPOST, V_FPRE)

            def up_out(i, last_group, e):
                dve.wait_ge(used, last_group + 1)
                if not (isinstance(i, int) and i == 0):
                    dve.wait_ge(i_cv, i)
                tt(ab[:], pt[:, 4 * e:4 * e + 4, 0:NQ], bc(rstd[:, QT], 4), ALU.mult).then_inc(i_ev, 1)

            def conv(i):
                dve.wait_ge(i_cb, i + 1)
                for tap in (1, 0):
                    for n in range(4):
                        t = i * 2 + ((n // 2) * KF + n % 2)
                        ins = stt(cv[:, n, :], ab[:, n, tap:tap + SEQ], cvw[:, tap, bass.ds(t, 1)], cv[:, n, :], ALU.mult, ALU.add)
                    if tap:
                        st.mark(ins)
                        st.sync()
                ins.then_inc(i_cv, 1)

            lo(ph["I0"], 1, 0)
            lo(ph["I0"], 1, 1)
            for j in range(1, 8, 2):
                dve.wait_ge(i_rt, j + 1)
                V.tensor_copy(r_tok[:, :, 256 * j:256 * j + 256],
                              pt[:, 4 + j % 3, :].rearrange("p (t c) -> p t c", t=2)).then_inc(i_rd, 1)
                if j == 1:
                    dve.wait_ge(root_s, 5)
                    st.mark(V.reciprocal(rstd[:, QT], root[:, QT]))
                    lo(ph["I0"], 1, 2)
            lo(ph["I0"], 1, 3)
            st.sync()
            up_out(0, number(ph["I0"], 0, 7), 0)
            for j in range(4, 8):
                lo(ph["I0"], 1, j)
                if j == 4:
                    conv(0)
            with dve.Fori(0, 10) as n:
                st.loop(n, 2)
                for e in range(2):
                    for j in range(8):
                        lo(ph["I"], n, 8 * e + j)
                        if j == 2:
                            up_out(n * 2 + (1 + e), number(ph["I"], n, 8 * e - 1), 1 - e)
                        if j == 3:
                            conv(n * 2 + (1 + e))
            st.done(10)

            def a_lo_part(it, kk):
                dve.wait_ge(j_hi, it * 4 + (kk + 1))
                tt(a_lo[:, kk, :], actT[:, bass.ds(it * 4 + kk, 1), :].rearrange("p o t -> p (o t)"),
                   a_hi[:, kk, :].bitcast(F32), ALU.subtract).then_inc(j_a, 1)

            def down(it, post):
                for j in range(8):
                    if j % 2 == 0:
                        a_lo_part(it, j // 2)
                    lo(ph["J"], it, j)
                    if post and j == 2:
                        up_out(21, ph["J"].first - 1, 1)
                    if post and j == 3:
                        conv(21)

            down(0, True)
            with dve.Fori(0, 9) as n:
                down(n + 1, False)
            for j in range(8):
                lo(ph["J"], 10, j)
                if j < 4:
                    a_lo_part(10, j)

            def weighted(t, c, n):
                cs = slice(c * 512, (c + n) * 512)
                st.mark(tt(o_tok[:, t, cs], pt[:, 4 * t + c:4 * t + c + n, :].rearrange("p b n -> p (b n)"), gpost[:, cs], ALU.mult))

            def mean(t, col):
                dst = stat[:, 18 + t:19 + t]
                stt(dst, stat[:, col:col + 1], 1.0 / D, stat[:, 20:21] if col % 2 == 0 else dst, ALU.mult, ALU.add).then_inc(j_b, 1)

            def inverse(t):
                dve.wait_ge(j_rt, t + 1)
                V.reciprocal(stat[:, 22 + t:23 + t], stat[:, 16 + t:17 + t]).then_inc(j_r, 1)
                dve.wait_ge(j_r, t + 1)

            def finish(t, c0, c1, done):
                stt(o_tok[:, t, c0:c1], o_tok[:, t, c0:c1], stat[:, 22 + t:23 + t], r_tok[:, t, c0:c1], ALU.mult, ALU.add).then_inc(done, 1)

            dve.wait_ge(gpost_land, 16)
            for t in range(2):
                dve.wait_ge(j_sq, t + 1)
                mean(t, 12 + 2 * t)
                weighted(t, 0, 2)
            dve.wait_ge(j_sq, 3)
            weighted(0, 2, 2)
            st.sync()
            inverse(0)
            finish(0, 0, 1024, j_od)
            finish(0, 1024, 2048, j_od)
            dve.wait_ge(j_sq, 4)
            dve.wait_ge(j_b, 2)
            mean(1, 15)
            weighted(1, 2, 1)
            dve.wait_ge(j_sq, 5)
            weighted(1, 3, 1)
            st.sync()
            inverse(1)
            finish(1, 512, 1024, j_od)
            finish(1, 1024, 2048, j_od)

        @block.gpsimd
        def _(pool):
            G = nc.gpsimd

            st = Steps(pool, pool_st)

            def rows(dst, src):
                pool.dma_start(dst, src.rearrange("(r c) -> r c", c=P)).then_inc(bias_in, 16)

            pool.dma_start(pos_i[:], a["positions"][0].partition_broadcast(P)).then_inc(pos_land, 16)
            r = VEC1[0][1]
            for name, n in VEC1[1:]:
                rows(vrow[r:r + n, 0, :], a[name][0])
                r += n
            bi = a["b_in_2"][0]
            r = 0
            for first, n in ((0, 24), (3080, 8), (4104, 16), (6152, 16)):
                rows(vrow[r:r + n, 1, :], bi[first:first + n * P])
                r += n
            for i in range(3):
                rows(vrow[0:88, 2 + i, :], a["ffn_conv_w_2"][0, i])
            rows(vrow[0:88, 5, :], a["ffn_conv_b_2"][0])
            pool.dma_start(b_f[:], bi[3072:3080].rearrange("(r c) -> r c", c=1)).then_inc(bias_in, 16)
            pool.dma_start(meta_in[:], a["meta_tokens_2"]).then_inc(bias_in, 16)

            def square_sum(norm, k, tok):
                pool.wait_ge(sq_rdy, KD * norm + k + 1)
                if k > 1:
                    st.sync()
                acc = sq_tile[norm][:, tok]
                i = G.tensor_tensor(acc, yT[:, 0, tok] if k == 1 else acc, yT[:, k, tok], ALU.add)
                if k < KD - 1:
                    st.mark(i)
                else:
                    i.then_inc(sq_acc, 1)

            def diagonal(m):
                v = m[:].rearrange("p (i t) -> p i t", i=3)
                for i in (0, 2):
                    r = G.affine_select(out=v[:, i, :], in_=v[:, i, :], compare_op=ALU.is_gt, fill=0.0, base=0,
                                        pattern=[[1, P]], channel_multiplier=-1)
                return r

            for k in range(1, KD):
                square_sum(0, k, L1T)
            for h in range(HEADS):
                pool.wait_ge(A_rec, h + 1)
                G.tensor_tensor(sgate[:], qkvg[:, 3, :], egate[:], ALU.mult).then_inc(A_sg, 1)
                pool.wait_ge(A_sp, h + 1)
                diagonal(spz).then_inc(A_spm, 1)
                pool.wait_ge(A_e, h + 1)
                diagonal(aw).then_inc(A_w, 1)
            with pool.Fori(0, HEADS // 2) as c:
                pool.wait_ge(C_ev, c * 5 + 3)
                G.tensor_tensor(ct1[:], cqr[:], cosT[:], ALU.mult).then_inc(C_t1, 1)
                pool.wait_ge(C_rec, c + 1)
                G.tensor_tensor(csg[:], cg[:], csg[:], ALU.mult).then_inc(C_sg, 1)

            def residual(norm, tok, w, sq_tok):
                for c in (1, 2):
                    pool.wait_ge(y_ev, 3 * (norm - 1) + c + 1)
                    if c == 2:
                        pool.wait_ge(y_acc, 4 * (norm - 1) + 1)
                    G.tensor_tensor(yacc[:, :, 0:w], yacc[:, :, 0:w], ysq[:, :, 0:w], ALU.add).then_inc(y_acc, 1)
                for n in (2, 1):
                    pool.wait_ge(y_acc, 4 * (norm - 1) + 4 - n)
                    G.tensor_tensor(yacc[:, 0:n, 0:w], yacc[:, 0:n, 0:w], yacc[:, n:2 * n, 0:w], ALU.add).then_inc(y_acc, 1)
                for k in range(KD):
                    pool.wait_ge(y_t, KD * (norm - 1) + k + 1)
                    G.tensor_tensor(xT[:, k, tok], xT[:, k, tok], yT[:, k, tok], ALU.add).then_inc(x_new, 1)
                    if k >= 3:
                        square_sum(norm, k - 2, sq_tok)
                for k in (KD - 2, KD - 1):
                    square_sum(norm, k, sq_tok)

            residual(1, L1T, SEQ, KT2)
            G.memset(augR[:], 0.0)
            G.memset(augL[:], 0.0)
            G.memset(uT[:, :, 0:16], 0.0)
            st.mark(G.memset(ones8[:], 1.0))
            st.sync()
            G.memset(augL[0:8, :], 1.0)
            for h in range(HEADS):
                i = G.tensor_scalar(augR[32:40, h, :], ones8[32:40, :], cst[32:40, C_EYE8 + h:C_EYE8 + h + 1], None, ALU.mult)
            i.then_inc(E_pad, 1)

            for g, w in enumerate(POOL_W):
                pool.wait_ge(F_b, 4 * (2 * g + 2))
                src = uT[:, 2 * g:2 * g + 2, :]
                st.mark(G.tensor_tensor(wsum[:, 0], src[:, :, 16:16 + L2], src[:, :, 15:15 + L2], ALU.add))
                k, i = 2, 0
                while k < w:
                    st.sync()
                    c = 2 * k - 2
                    st.mark(G.tensor_tensor(wsum[:, 1 - i, :, c:L2], wsum[:, i, :, c:L2], wsum[:, i, :, c - k:L2 - k], ALU.add))
                    k, i = 2 * k, 1 - i
                st.sync()
                st.mark(G.tensor_scalar(pdiff[:, g], wsum[:, i, :, QT], 1.0 / w, None, ALU.mult))
                st.sync()
                if w > T0 + 1:
                    st.mark(G.tensor_scalar(pdiff[:, g, :, 0:1], wsum[:, i, :, T0:T0 + 1], 1.0 / (T0 + 1), None, ALU.mult))
                    st.sync()
                G.tensor_tensor(pdiff[:, g], pdiff[:, g], src[:, :, 16 + T0:16 + L2], ALU.subtract).then_inc(p_t, 1)
            with pool.Fori(0, 8) as c:
                pool.wait_ge(g_t, c * 2 + 2)
                G.tensor_tensor(gta[:], gta[:], gtp[:], ALU.add).then_inc(g_m, 1)
            residual(2, QT, NQ, QT)
            with pool.Fori(0, 22) as i:
                pool.wait_ge(i_ge, i + 1)
                G.tensor_tensor(actT[:, bass.ds(i * 2, 2), :], ge[:], cv[:, 2:4, :], ALU.mult).then_inc(i_act, 1)
            pool.wait_ge(j_t, 1)
            G.tensor_tensor(o_tok[:, 1, 0:512], o_tok[:, 1, 0:512], r_tok[:, 1, 0:512], ALU.add).then_inc(j_op, 1)


INPUTS = ["x", "positions", "pre_norm_w", "w_in", "q_norm_w", "w_q_up", "kv_norm_w", "w_kv_up", "w_out", "post_norm_w",
          "meta_tokens_2", "mix_pre_g_2", "w_in_2", "b_in_2", "w_attn_o_2", "pool_w_2", "pool_scale_2", "w_pool_o_2",
          "w_out_2", "mix_post_g_2", "ffn_pre_g_2", "w_ffn_up_2", "ffn_conv_w_2", "ffn_conv_b_2", "w_ffn_down_2",
          "ffn_post_g_2"]


def kernel(**inputs):
    import numpy as _np
    import concourse.bacc as _bacc
    from concourse.bass_utils import run_bass_kernel_spmd as _run

    nc = _bacc.Bacc("TRN2", target_bir_lowering=False, num_devices=1)
    arrays, args = {}, {}
    for name in INPUTS:
        arr = _np.ascontiguousarray(inputs[name])
        arrays[f"in_{name}"] = arr
        args[name] = nc.dram_tensor(f"in_{name}", arr.shape, mybir.dt.from_np(arr.dtype), kind="ExternalInput").ap()
    arr = constants()
    arrays["in_consts"] = arr
    args["consts"] = nc.dram_tensor("in_consts", arr.shape, F32, kind="ExternalInput").ap()
    out = nc.dram_tensor("out_0", (1, SEQ, D), F32, kind="ExternalOutput").ap()
    build(nc, args, out)
    r = _run(nc, [arrays], core_ids=[0])
    return r.results[0]["out_0"]
```
